# Optimizing a Trainium2 kernel written in Bass

```python
import math
import jax, jax.numpy as jnp
from jax import lax
import numpy as np

D_MODEL = 1024
BATCH = 1
SEQ = 512
DEPTH = 1

HEAD_DIM = 64
BRANCH_WIDTH = 8 * HEAD_DIM
RWKV_HEADS = BRANCH_WIDTH // HEAD_DIM
RWKV_WIDTH = BRANCH_WIDTH
RWKV_W_LORA = 64
RWKV_A_LORA = 64
RWKV_G_LORA = 128
RWKV_LN_EPS = 64e-5
NSA_HEADS = BRANCH_WIDTH // HEAD_DIM
NSA_KV_GROUPS = 2
NSA_WIDTH = BRANCH_WIDTH
NSA_KV_WIDTH = NSA_KV_GROUPS * HEAD_DIM
CMP_STRIDE = 16
CMP_LEN = 2 * CMP_STRIDE
CMP_HIDDEN = 256
SEL_BLOCK = 64
SEL_TOPK = 16
SEL_OVERLAP_W = (1.0, 2.0, 2.0, 2.0, 1.0)
SEL_FORCE_SCORE = 1e4
NSA_WINDOW = 512
Q_BLOCK = 128
SWA_HEADS = BRANCH_WIDTH // HEAD_DIM
SWA_KV_HEADS = 2
SWA_WIDTH = BRANCH_WIDTH
SWA_KV_WIDTH = SWA_KV_HEADS * HEAD_DIM
SWA_WINDOW = 128
REL_BUCKETS = 32
REL_MAX_DIST = 1024
FFN_HIDDEN = ((8 * D_MODEL + 3 * 256 - 1) // (3 * 256)) * 256
N_BRANCHES = 3
NORM_EPS = 1e-6
NEG_INF = -1e30
RWKV_COLS = 3 * RWKV_WIDTH + RWKV_W_LORA + RWKV_A_LORA + RWKV_G_LORA
NSA_COLS = NSA_WIDTH + 6 * NSA_KV_WIDTH + 3 * NSA_HEADS
SWA_COLS = SWA_WIDTH + 2 * SWA_KV_WIDTH
GATE_COLS = N_BRANCHES * D_MODEL
IN_COLS = RWKV_COLS + NSA_COLS + SWA_COLS + GATE_COLS

kernel_name = "hybrid_rwkv7_nsa_swa_gated_trunk"

def _split(x, sizes):
    idx = [int(v) for v in np.cumsum(sizes)[:-1]]
    return jnp.split(x, idx, axis=-1)

def rms_norm(x, g):
    xf = x.astype(jnp.float32)
    y = xf * lax.rsqrt(jnp.mean(xf * xf, axis=-1, keepdims=True) + NORM_EPS)
    return (y * g.astype(jnp.float32)).astype(x.dtype)

def t5_bucket(dist):
    n = jnp.maximum(dist, 0)
    max_exact = REL_BUCKETS // 2
    nf = jnp.maximum(n, 1).astype(jnp.float32)
    large = max_exact + (jnp.log(nf / max_exact) / math.log(REL_MAX_DIST / max_exact)
                         * (REL_BUCKETS - max_exact)).astype(jnp.int32)
    large = jnp.minimum(large, REL_BUCKETS - 1)
    return jnp.where(n < max_exact, n, large)

def rel_bias_2d(table, dist, groups):
    b = table[t5_bucket(dist)].astype(jnp.float32)
    return b.reshape(dist.shape + (groups, -1)).transpose(2, 3, 0, 1)

def masked_softmax(s, mask, sink=None):
    s = jnp.where(mask, s, NEG_INF)
    m = jnp.max(s, axis=-1, keepdims=True)
    if sink is not None:
        m = jnp.maximum(m, sink)
    p = jnp.where(mask, jnp.exp(s - m), 0.0)
    den = jnp.sum(p, axis=-1, keepdims=True)
    if sink is not None:
        den = den + jnp.exp(sink - m)
    return p / jnp.where(den > 0, den, 1.0)

def rwkv7_time_mix(p, mu, w0, w2, a0, a2, g2, k_k, k_a, r_k, ln_w, ln_b):
    B, T, _ = p.shape
    H, N = RWKV_HEADS, HEAD_DIM
    f32 = jnp.float32
    prev = jnp.pad(p, ((0, 0), (1, 0), (0, 0)))[:, :-1]
    p = p + (prev - p) * mu
    r, k, v, zw, za, zg = _split(p, (RWKV_WIDTH,) * 3 + (RWKV_W_LORA, RWKV_A_LORA, RWKV_G_LORA))
    w = -jax.nn.softplus(-(w0 + jnp.tanh(zw) @ w2).astype(f32)) - 0.5
    decay = jnp.exp(-jnp.exp(w))
    a = jax.nn.sigmoid((a0 + za @ a2).astype(f32))
    g = jax.nn.sigmoid(zg) @ g2
    kk = (k * k_k).astype(f32).reshape(B, T, H, N)
    kk = kk / jnp.maximum(jnp.sqrt(jnp.sum(kk * kk, axis=-1, keepdims=True)), 1e-12)
    k = k.astype(f32) * (1.0 + (a - 1.0) * k_a.astype(f32))

    def heads(z):
        return z.astype(f32).reshape(B, T, H, N)
    r_h, w_h, k_h, v_h, a_h = heads(r), heads(decay), heads(k), heads(v), heads(a)
    xs = tuple(jnp.swapaxes(z, 0, 1) for z in (r_h, w_h, k_h, v_h, -kk, kk * a_h))

    def step(S, inp):
        r_t, w_t, k_t, v_t, a_t, b_t = inp
        sa = jnp.einsum('bhij,bhj->bhi', S, a_t)
        S = S * w_t[:, :, None, :] + sa[..., None] * b_t[:, :, None, :] + v_t[..., None] * k_t[:, :, None, :]
        y = jnp.einsum('bhij,bhj->bhi', S, r_t)
        return S, y

    S0 = jnp.zeros((B, H, N, N), f32)
    _, y = lax.scan(step, S0, xs)
    y = jnp.swapaxes(y, 0, 1)
    mean = jnp.mean(y, axis=-1, keepdims=True)
    var = jnp.mean(jnp.square(y - mean), axis=-1, keepdims=True)
    y = ((y - mean) * lax.rsqrt(var + RWKV_LN_EPS)).reshape(B, T, RWKV_WIDTH)
    y = y * ln_w.astype(f32) + ln_b.astype(f32)
    bonus = jnp.sum(r_h * k_h * r_k.astype(f32), axis=-1, keepdims=True) * v_h
    y = y + bonus.reshape(B, T, RWKV_WIDTH)
    return (y * g.astype(f32)).astype(p.dtype)

def nsa_mix(p, pe_k, pe_v, ck_w1, ck_w2, cv_w1, cv_w2, rel_tbl):
    B, T, _ = p.shape
    G, R, N = NSA_KV_GROUPS, NSA_HEADS // NSA_KV_GROUPS, HEAD_DIM
    f32 = jnp.float32
    q, kc, vc, ks, vs, kw, vw, gl = _split(p, (NSA_WIDTH,) + (NSA_KV_WIDTH,) * 6 + (3 * NSA_HEADS,))
    nq = T // Q_BLOCK
    n_cmp = T // CMP_STRIDE - 1
    n_sel = T // SEL_BLOCK
    topk = min(SEL_TOPK, n_sel)
    sel_per_cmp = SEL_BLOCK // CMP_STRIDE

    def compress(z, pe, w1, w2):
        c = z.reshape(B, T // CMP_STRIDE, CMP_STRIDE, G, N)
        blk = jnp.concatenate([c[:, :-1], c[:, 1:]], axis=2) + pe[None, None, :, None, :]
        blk = blk.transpose(0, 3, 1, 2, 4).reshape(B, G, n_cmp, CMP_LEN * N)
        return jax.nn.gelu(blk @ w1) @ w2

    k_cmp = compress(kc, pe_k, ck_w1, ck_w2)
    v_cmp = compress(vc, pe_v, cv_w1, cv_w2)
    cmp_end = jnp.arange(n_cmp) * CMP_STRIDE + (CMP_LEN - 1)

    k_sel = ks.reshape(B, n_sel, SEL_BLOCK, G, N).transpose(0, 3, 1, 2, 4)
    v_sel = vs.reshape(B, n_sel, SEL_BLOCK, G, N).transpose(0, 3, 1, 2, 4)
    pad = ((0, 0), (NSA_WINDOW, 0), (0, 0), (0, 0))
    k_win = jnp.pad(kw.reshape(B, T, G, N), pad)
    v_win = jnp.pad(vw.reshape(B, T, G, N), pad)

    q_blk = (q * HEAD_DIM ** -0.5).reshape(B, nq, Q_BLOCK, G, R, N).transpose(1, 0, 3, 4, 2, 5)
    gates = jax.nn.sigmoid(gl.astype(f32)).reshape(B, nq, Q_BLOCK, 3, G, R).transpose(1, 0, 3, 4, 5, 2)
    tbl_g = rel_tbl.reshape(REL_BUCKETS, G, R).transpose(1, 0, 2).astype(f32)
    b_idx = jnp.arange(B)[:, None, None, None]
    g_idx = jnp.arange(G)[None, :, None, None]
    sel_ids = jnp.arange(n_sel)

    def one_block(args):
        qb, gb, blk = args
        t = blk * Q_BLOCK + jnp.arange(Q_BLOCK)
        dist_c = t[:, None] - cmp_end[None, :]
        s_c = jnp.einsum('bgrqd,bgcd->bgrqc', qb, k_cmp).astype(f32) + rel_bias_2d(rel_tbl, dist_c, G)
        p_c = masked_softmax(s_c, dist_c >= 0)
        o_c = jnp.einsum('bgrqc,bgcd->bgrqd', p_c.astype(v_cmp.dtype), v_cmp)
        imp = jnp.pad(jnp.sum(p_c, axis=2), ((0, 0), (0, 0), (0, 0), (1, sel_per_cmp)))
        imp = sum(wt * lax.slice_in_dim(imp, o, o + sel_per_cmp * (n_sel - 1) + 1, stride=sel_per_cmp, axis=3)
                  for o, wt in enumerate(SEL_OVERLAP_W))
        cur = (t // SEL_BLOCK)[:, None]
        sid = sel_ids[None, :]
        forced = (sid == 0) | (sid == cur) | (sid == cur - 1)
        score = jnp.where(forced, SEL_FORCE_SCORE, jnp.where(sid <= cur, imp, -1.0))
        _, sel = lax.top_k(score, topk)
        k_g = k_sel[b_idx, g_idx, sel].reshape(B, G, Q_BLOCK, topk * SEL_BLOCK, N)
        v_g = v_sel[b_idx, g_idx, sel].reshape(B, G, Q_BLOCK, topk * SEL_BLOCK, N)
        pos = (sel[..., None] * SEL_BLOCK + jnp.arange(SEL_BLOCK)).reshape(B, G, Q_BLOCK, topk * SEL_BLOCK)
        dist_s = t[None, None, :, None] - pos
        bias_s = jnp.moveaxis(tbl_g[g_idx, t5_bucket(dist_s)], -1, 2)
        s_s = jnp.einsum('bgrqd,bgqmd->bgrqm', qb, k_g).astype(f32) + bias_s
        p_s = masked_softmax(s_s, (dist_s >= 0)[:, :, None])
        o_s = jnp.einsum('bgrqm,bgqmd->bgrqd', p_s.astype(v_g.dtype), v_g)
        start = blk * Q_BLOCK
        k_w = lax.dynamic_slice_in_dim(k_win, start, Q_BLOCK + NSA_WINDOW, axis=1)
        v_w = lax.dynamic_slice_in_dim(v_win, start, Q_BLOCK + NSA_WINDOW, axis=1)
        spos = start - NSA_WINDOW + jnp.arange(Q_BLOCK + NSA_WINDOW)
        dist_w = t[:, None] - spos[None, :]
        mask_w = (dist_w >= 0) & (dist_w < NSA_WINDOW) & (spos[None, :] >= 0)
        s_w = jnp.einsum('bgrqd,bsgd->bgrqs', qb, k_w).astype(f32) + rel_bias_2d(rel_tbl, dist_w, G)
        p_w = masked_softmax(s_w, mask_w)
        o_w = jnp.einsum('bgrqs,bsgd->bgrqd', p_w.astype(v_w.dtype), v_w)
        gb = gb[..., None]
        out = gb[:, 0] * o_c + gb[:, 1] * o_s + gb[:, 2] * o_w
        return out.astype(qb.dtype)

    o = lax.map(one_block, (q_blk, gates, jnp.arange(nq)))
    return o.transpose(1, 0, 4, 2, 3, 5).reshape(B, T, NSA_WIDTH)

def swa_sink_mix(p, sinks, rel_tbl):
    B, T, _ = p.shape
    G, R, N, W = SWA_KV_HEADS, SWA_HEADS // SWA_KV_HEADS, HEAD_DIM, SWA_WINDOW
    f32 = jnp.float32
    q, k, v = _split(p, (SWA_WIDTH, SWA_KV_WIDTH, SWA_KV_WIDTH))
    nb = T // W
    q = (q * HEAD_DIM ** -0.5).reshape(B, nb, W, G, R, N)
    k = k.reshape(B, nb, W, G, N)
    v = v.reshape(B, nb, W, G, N)
    shift = ((0, 0), (1, 0), (0, 0), (0, 0), (0, 0))
    kb = jnp.concatenate([jnp.pad(k, shift)[:, :-1], k], axis=2)
    vb = jnp.concatenate([jnp.pad(v, shift)[:, :-1], v], axis=2)
    i = jnp.arange(W)
    j = jnp.arange(2 * W)
    dist = W + i[:, None] - j[None, :]
    valid_key = (jnp.arange(nb)[:, None] > 0) | (j[None, :] >= W)
    mask = ((dist >= 0) & (dist < W))[None] & valid_key[:, None, :]
    s = jnp.einsum('bnqgrd,bnkgd->bngrqk', q, kb).astype(f32) + rel_bias_2d(rel_tbl, dist, G)[None, None]
    sink = sinks.astype(f32).reshape(G, R)[None, None, :, :, None, None]
    pr = masked_softmax(s, mask[None, :, None, None], sink)
    o = jnp.einsum('bngrqk,bnkgd->bnqgrd', pr.astype(vb.dtype), vb)
    return o.reshape(B, T, SWA_WIDTH)

def setup_inputs(seed: int = 0) -> dict:
    key = jax.random.key(seed)
    ks = jax.random.split(key, 32)
    f32 = jnp.float32
    L, D = DEPTH, D_MODEL

    def nrm(k, shape, scale):
        return jax.random.normal(k, shape, f32) * scale

    def gain(k, shape):
        return 1.0 + nrm(k, shape, 0.1)

    return {
        "x": nrm(ks[0], (BATCH, SEQ, D), 1.0),
        "norm_pre_mix": gain(ks[1], (L, D)),
        "norm_post_mix": gain(ks[2], (L, D)),
        "norm_pre_ffn": gain(ks[3], (L, D)),
        "norm_post_ffn": gain(ks[4], (L, D)),
        "w_in": nrm(ks[5], (L, D, IN_COLS), D ** -0.5),
        "rwkv_mu": jax.random.uniform(ks[6], (L, RWKV_COLS), f32),
        "rwkv_w0": jax.random.uniform(ks[7], (L, RWKV_WIDTH), f32, -6.0, 0.0),
        "rwkv_w2": nrm(ks[8], (L, RWKV_W_LORA, RWKV_WIDTH), 0.5 * RWKV_W_LORA ** -0.5),
        "rwkv_a0": nrm(ks[9], (L, RWKV_WIDTH), 0.5),
        "rwkv_a2": nrm(ks[10], (L, RWKV_A_LORA, RWKV_WIDTH), RWKV_A_LORA ** -0.5),
        "rwkv_g2": nrm(ks[11], (L, RWKV_G_LORA, RWKV_WIDTH), RWKV_G_LORA ** -0.5),
        "rwkv_k_k": 0.85 + nrm(ks[12], (L, RWKV_WIDTH), 0.1),
        "rwkv_k_a": 1.0 + nrm(ks[13], (L, RWKV_WIDTH), 0.1),
        "rwkv_r_k": nrm(ks[14], (L, RWKV_HEADS, HEAD_DIM), 0.1),
        "rwkv_ln_w": gain(ks[15], (L, RWKV_WIDTH)),
        "rwkv_ln_b": nrm(ks[16], (L, RWKV_WIDTH), 0.02),
        "nsa_pe_k": nrm(ks[17], (L, CMP_LEN, HEAD_DIM), 0.1),
        "nsa_pe_v": nrm(ks[18], (L, CMP_LEN, HEAD_DIM), 0.1),
        "nsa_ck_w1": nrm(ks[19], (L, CMP_LEN * HEAD_DIM, CMP_HIDDEN), (CMP_LEN * HEAD_DIM) ** -0.5),
        "nsa_ck_w2": nrm(ks[20], (L, CMP_HIDDEN, HEAD_DIM), CMP_HIDDEN ** -0.5),
        "nsa_cv_w1": nrm(ks[21], (L, CMP_LEN * HEAD_DIM, CMP_HIDDEN), (CMP_LEN * HEAD_DIM) ** -0.5),
        "nsa_cv_w2": nrm(ks[22], (L, CMP_HIDDEN, HEAD_DIM), CMP_HIDDEN ** -0.5),
        "swa_sinks": nrm(ks[23], (L, SWA_HEADS), 1.0),
        "rel_bias": nrm(ks[24], (REL_BUCKETS, NSA_HEADS + SWA_HEADS), 0.5),
        "w_branch": nrm(ks[25], (L, N_BRANCHES, BRANCH_WIDTH, D), BRANCH_WIDTH ** -0.5),
        "w_out": nrm(ks[26], (L, D, D), D ** -0.5),
        "ffn_w_gate": nrm(ks[27], (L, D, FFN_HIDDEN), D ** -0.5),
        "ffn_w_up": nrm(ks[28], (L, D, FFN_HIDDEN), D ** -0.5),
        "ffn_w_down": nrm(ks[29], (L, FFN_HIDDEN, D), FFN_HIDDEN ** -0.5),
    }

def reference(x, norm_pre_mix, norm_post_mix, norm_pre_ffn, norm_post_ffn, w_in, rwkv_mu, rwkv_w0, rwkv_w2,
              rwkv_a0, rwkv_a2, rwkv_g2, rwkv_k_k, rwkv_k_a, rwkv_r_k, rwkv_ln_w, rwkv_ln_b, nsa_pe_k, nsa_pe_v,
              nsa_ck_w1, nsa_ck_w2, nsa_cv_w1, nsa_cv_w2, swa_sinks, rel_bias, w_branch, w_out,
              ffn_w_gate, ffn_w_up, ffn_w_down):
    B, T, D = x.shape
    rel_nsa = rel_bias[:, :NSA_HEADS]
    rel_swa = rel_bias[:, NSA_HEADS:]
    for l in range(DEPTH):
        h = rms_norm(x, norm_pre_mix[l])
        proj = h @ w_in[l]
        p_rwkv, p_nsa, p_swa, p_gate = _split(proj, (RWKV_COLS, NSA_COLS, SWA_COLS, GATE_COLS))
        o_rwkv = rwkv7_time_mix(p_rwkv, rwkv_mu[l], rwkv_w0[l], rwkv_w2[l], rwkv_a0[l], rwkv_a2[l],
                                rwkv_g2[l], rwkv_k_k[l], rwkv_k_a[l], rwkv_r_k[l], rwkv_ln_w[l], rwkv_ln_b[l])
        o_nsa = nsa_mix(p_nsa, nsa_pe_k[l], nsa_pe_v[l], nsa_ck_w1[l], nsa_ck_w2[l], nsa_cv_w1[l],
                        nsa_cv_w2[l], rel_nsa)
        o_swa = swa_sink_mix(p_swa, swa_sinks[l], rel_swa)
        gates = jax.nn.sigmoid(p_gate.astype(jnp.float32)).reshape(B, T, N_BRANCHES, D).astype(x.dtype)
        merged = (gates[:, :, 0] * (o_rwkv @ w_branch[l, 0])
                  + gates[:, :, 1] * (o_nsa @ w_branch[l, 1])
                  + gates[:, :, 2] * (o_swa @ w_branch[l, 2]))
        x = x + rms_norm(merged @ w_out[l], norm_post_mix[l])
        h = rms_norm(x, norm_pre_ffn[l])
        f = (jax.nn.silu(h @ ffn_w_gate[l]) * (h @ ffn_w_up[l])) @ ffn_w_down[l]
        x = x + rms_norm(f, norm_post_ffn[l])
    return x


_drawn_inputs = setup_inputs


def setup_inputs(seed=0):
    import zlib

    import numpy as np

    out = dict(_drawn_inputs(seed))
    spreads = {}
    factors = {'rwkv_w2': 3.267, 'rwkv_ln_b': 4.282, 'nsa_pe_k': 8.0, 'swa_sinks': 3.431}
    for name, (base, spread) in spreads.items():
        noise = np.random.default_rng([zlib.crc32(name.encode()), seed]).standard_normal(out[name].shape)
        drawn = base * np.exp(spread * noise) if base else spread * noise
        out[name] = __import__('jax').numpy.asarray(drawn.astype(out[name].dtype))
    for name, factor in factors.items():
        out[name] = (out[name] * factor).astype(out[name].dtype)
    return out
```

```python
import numpy as np
import concourse.bass as bass
from concourse import mybir

F32 = mybir.dt.float32
F32R = mybir.dt.float32r
ALU = mybir.AluOpType
ACT = mybir.ActivationFunctionType
AX = mybir.AxisListType

T, D, P = 512, 1024, 128
HD, NH = 64, 8
BW = NH * HD
KC = D // P
RW_COLS, NSA_COLS, SWA_COLS = 3 * BW + 256, BW + 6 * 128 + 3 * NH, BW + 256
NSA0, SWA0 = RW_COLS, RW_COLS + NSA_COLS
GATE0 = SWA0 + SWA_COLS
FFN = 2816
NF = FFN // P
NCMP = T // 16 - 1
WIN = 128
C = 64
CH = 256
NEG = -1e30
EPS, LN_EPS = 1e-6, 64e-5
BUCKET0 = list(range(16)) + [16, 21, 27, 35, 46, 59, 77, 99, 128, 166, 216, 280, 363, 470]

PAR = {}
_row = 0
for _name, _n in (("g_pre_mix", 8), ("g_post_mix", 8), ("g_pre_ffn", 8), ("g_post_ffn", 8), ("mu", 14), ("w0", 4),
                  ("a0", 4), ("k_k", 4), ("k_a", 4), ("r_k", 4), ("ln_w", 4), ("ln_b", 4)):
    PAR[_name] = _row
    _row += _n
NPAR1 = _row
NPAR2 = 64
PAR["pe"] = NPAR1

CON = {}
_col = 0
for _name, _n in (("ident", 128), ("bones", 128), ("ones", 128), ("maskG", 128), ("maskA", 128), ("m1", 128),
                  ("m2", 128), ("m4", 128), ("m8", 128), ("m16", 128), ("m32", 128), ("ic", 64), ("reset", 512)):
    CON[_name] = _col
    _col += _n
NCON, NCONP = _col, 384


def constants():
    con = np.zeros((P, NCON), np.float32)
    s, t = np.arange(P)[:, None], np.arange(P)[None, :]
    put = lambda name, x: con.__setitem__((slice(None), slice(CON[name], CON[name] + x.shape[1])), x)
    put("ident", s == t)
    put("bones", (s // C) == (t // C))
    put("ones", np.ones((P, P)))
    put("maskG", np.where(t < C, (s % C) < (t % C), (s % C) <= (t % C)))
    put("maskA", ((s // C) == (t // C)) & (s < t))
    for m in (1, 2, 4, 8, 16, 32):
        put(f"m{m}", (s // (2 * m) == t // (2 * m)) & (s % (2 * m) < m) & (t % (2 * m) >= m))
    put("ic", (s % C) == np.arange(C)[None, :])
    put("reset", np.broadcast_to(np.arange(T) % C != 0, (P, T)))
    hot = np.zeros((33, 1024), np.float32)
    for x in range(640):
        d = x - 127
        hot[32 if d < 0 else int(np.searchsorted(BUCKET0, d, side="right")) - 1, x] = 1
    for x in range(384):
        d = x - 127
        hot[32 if d < 0 or d >= WIN else int(np.searchsorted(BUCKET0, d, side="right")) - 1, 640 + x] = 1
    return con, hot


JOBS = []
for _n in range(14):
    JOBS.append(("rwkv", _n, 0, 8))
NS0 = len(JOBS)
for _n in range(11):
    JOBS.append(("nsa", _n, 0, 8))
SW0 = len(JOBS)
for _n in range(6):
    JOBS.append(("swa", _n, 0, 8))
GS = 3
NGA = 8
_gates = [("gate", _i, 0, 8) for _i in list(range(3 * GS, 3 * KC)) + list(range(3 * GS))]
JOBS += _gates[:NGA]
CMP0 = len(JOBS)
for _kv in range(2):
    for _half in range(2):
        for _part in range(2):
            JOBS.append(("cmp", 2 * _kv + _half, _part, 8))
GB0 = len(JOBS)
JOBS += _gates[NGA:]
GC0 = len(JOBS) - 3 * GS
MERGE0 = len(JOBS)
for _d in range(KC):
    for _b in range(3):
        JOBS.append(("branch", 3 * _d + _b, 0, 4))
OUT0 = len(JOBS)
for _n in range(KC):
    JOBS.append(("out", _n, 0, 8))
FF0 = len(JOBS)
for _f in range(NF):
    JOBS.append(("ffg", _f, 0, 8))
    JOBS.append(("ffu", _f, 0, 8))
DN0 = len(JOBS)
DPARTS = [6, 6, 5, 5]
for _d in range(KC):
    for _q in range(4):
        JOBS.append(("down", _d, _q, DPARTS[_q]))
NJ = len(JOBS)
NRAW, NSPL = 4, 2
POOL_HI = [n for n in range(NS0, MERGE0) if not CMP0 <= n < GB0]
SPILLED = list(range(SW0, CMP0)) + list(range(GB0, GC0))
NSTAGE = 2
LOADS = [2 if (j[0] in ("nsa", "swa") and j[1] < 4) else 1 for j in JOBS]


def group_of(n):
    return n if n < CMP0 else CMP0 + (n - CMP0) // 2 if n < GB0 else n - (GB0 - CMP0) // 2


def loaded_value(n):
    return 16 * sum(LOADS[m] for m in range(n % NRAW, n + 1, NRAW))


def ends_group(n):
    return not (CMP0 <= n < GB0 and (n - CMP0) % 2 == 0)


FILL = []
PT_UP = len(FILL); FILL += [10, 8, 8]
PT_CP = []
for _cp in range(4):
    PT_CP.append(len(FILL)); FILL += [5, 2] + [2, 2] * 4 + [2, 2] + [1, 8]
_left = 8 * (CMP0 - NS0) - sum(FILL)
assert _left >= 0, _left
PT_GN = len(FILL); FILL += [3, _left - 3, 16, 16, 16, 16]
PT_NSA = len(FILL); FILL += [3] * 34
_rest = 8 * (MERGE0 - NS0) - sum(FILL)
PT_SWA = len(FILL); FILL += [_rest // 18] * 18
FILL[-1] += _rest - 18 * (_rest // 18)
DONE = []
_k = 0
for _f in FILL:
    _k += _f
    DONE.append(NS0 + _k // 8)
assert DONE[-1] == MERGE0


def build(nc, x, w_in, w_branch, w_out, w_gate, w_up, w_down, w2, a2, g2, ck1, ck2, cv1, cv2, sinks, rel_bias,
          par1, par2, con, hot, out):
    base = 16512

    class Region:
        def __init__(self, at):
            self.at = at

        def take(self, name, shape, dt=F32):
            n = (4 * int(np.prod(shape[1:])) + 31) // 32 * 32
            t = nc.alloc_sbuf_tensor_at(name, list(shape), dt, offset=self.at)
            self.at += n
            return t

    per = Region(base)
    CONP = per.take("CONP", [P, NCONP])
    PARC = per.take("PARC", [P, NPAR1 + NPAR2])
    MISC = per.take("MISC", [P, 96])
    RINV = per.take("RINV", [P, T])
    SQ = per.take("SQ", [P, 2, T])
    SSUM = per.take("SSUM", [P, T])
    WRAW = per.take("WRAW", [P, NRAW, 8, P])
    WHI = per.take("WHI", [P, NSPL, 8, P], F32R)
    WLO = per.take("WLO", [P, NSPL, 8, P], F32R)
    HHI = per.take("HHI", [P, KC, T], F32R)
    HLO = per.take("HLO", [P, KC, T], F32R)
    Z = per.at
    KB = 1024

    def at(name, kb, shape, dt=F32):
        return Region(Z + int(kb * KB)).take(name, shape, dt)

    RW = at("RW", 0, [P, 14, T])
    CUM = at("CUM", 28, [P, 4, T])
    AA = at("AA", 36, [P, 4, T])
    KK = at("KK", 44, [P, 4, T])
    AR = at("AR", 52, [P, 4, 2, P])
    BK = at("BK", 56, [P, 4, 2, P])
    BKT = at("BKT", 60, [P, 2, 4, P])
    SV = at("SV", 64, [P, 2, BW])
    G = at("G", 68, [P, 2, NH, P])
    ABD = at("ABD", 76, [P, NH, P])
    E1 = at("E1", 76, [P, 4, P])
    E2 = at("E2", 78, [P, 4, P])
    AM = at("AM", 80, [P, NH, P])
    XC = at("XC", 84, [P, NH, C])
    XTC = at("XTC", 86, [P, NH, C])
    UC = at("UC", 88, [P, NH, C])
    UBD = at("UBD", 90, [P, NH, P])
    XTBD = at("XTBD", 94, [P, NH, P])
    T1 = at("T1", 98, [P, NH, C])
    ST = at("ST", 100, [P, 2, 4, C])
    MASK = at("MASK", 102, [P, NCON - NCONP])
    WA = at("WA", 108.5, [P, BW])
    PSH = at("PSH", 52, [P, 2, T + 1])
    DSH = at("DSH", 57, [P, T])
    TMP = at("TMP", 60, [P, 4, T])
    XTOK0 = at("XTOK0", 76, [P, 4, D])
    PRAW = at("PRAW", 52, [P, 2, P])
    NQ = at("NQ", 110.5, [P, 10, T])
    GL = at("GL", 130.5, [P, T])
    O = at("O", 0, [P, 3, 4, T])
    VT = at("VT", 24, [P, 3, 4, P])
    SWQ = at("SWQ", 30, [P, 6, T])
    TBS = at("TBS", 42, [P, NH, 256])
    EB = at("EB", 50, [P, 2, 2, T])
    PTB = at("PTB", 58, [P, 2, 2, T])
    OTK = at("OTK", 66, [P, 2, BW])
    OTS = at("OTS", 70, [P, 2, BW])
    TB = at("TB", 74, [P, NH, T])
    GATES = at("GATES", 90, [P, 15, T])
    XHI = at("XHI", 90, [P, 2, 16, 2 * NCMP], F32R)
    XLO = at("XLO", 98, [P, 2, 16, 2 * NCMP], F32R)
    XF = at("XF", 52, [P, 16, 2 * NCMP])
    small = Region(Z + int(118.5 * KB))
    HG = small.take("HG", [P, 4, 2 * NCMP])
    HT = small.take("HT", [P, 2, 2 * NCMP])
    KCT = small.take("KCT", [P, NCMP])
    VCT = small.take("VCT", [32, 2, C])
    GLT = small.take("GLT", [P, 4, 3 * NH])
    CW2 = small.take("CW2", [P, 2, 2, C])
    ECB = small.take("ECB", [P, 2, 32])
    PTC = at("PTC", 108.5, [32, 2, P])
    assert small.at <= Z + int(122.5 * KB)
    OHI = at("OHI", 24, [P, 3, 4, T], F32R)
    OLO = at("OLO", 48, [P, 3, 4, T], F32R)
    MHI = at("MHI", 0, [P, KC, T], F32R)
    MLO = at("MLO", 72, [P, KC, T], F32R)
    MT = at("MT", 122, [P, 2, T])
    DSH2 = at("DSH2", 126, [P, 2, T])
    XTOK = at("XTOK", 24, [P, 4, D])
    OT = at("OT", 40, [P, KC, T])
    X1 = at("X1", 116, [P, KC, T])
    DHI = at("DHI", 0, [P, NF, T], F32R)
    DLO = at("DLO", 44, [P, NF, T], F32R)
    FT = at("FT", 88, [P, 6, T])
    OF = at("OF", 100, [P, KC, T])
    OTOK = Region(Z - 32 * KB).take("OTOK", [P, 4, D])
    HOT = at("HOT", 24, [33, 1024])
    TBL = at("TBL", 28, [33, 16])
    VR = at("VR", 29, [8, 1024])
    SNK = MISC[:, 0:8]
    EPSC = MISC[:, 8:10]
    PCS = MISC[:, 10:18]
    STAT = MISC[:, 18:42].rearrange("p (a b) -> p a b", b=12)
    STAT2 = STAT[:, :, 6:9]
    STATS = MISC[:, 42:66].rearrange("p (a b) -> p a b", b=12)

    assert Z + 132.9 * KB <= 229344, (Z + 132.9 * KB)

    ident, bones, ones = CONP[:, 0:128], CONP[:, 128:256], CONP[:, 256:384]

    def mask(name, n=128):
        c = CON[name] - NCONP
        return MASK[:, c:c + n]

    def par(name, i):
        return PARC[:, PAR[name] + i:PAR[name] + i + 1]

    bias_rows = nc.dram_tensor("bias_rows", (8, 1024), F32, kind="Internal").ap()

    spilled = nc.dram_tensor("spilled", (len(SPILLED), P, T), F32, kind="Internal").ap()

    def stage(n):
        e = SPILLED.index(n)
        return SQ[:, e % NSTAGE, :] if n < CMP0 else GATES[:, n - GB0, :]

    psum = [nc.alloc_psum_tensor(f"ps{n}", [P, T], F32) for n in range(8)]
    DB, R = psum[0:2], psum[2:8]
    DB4 = [DB[0], DB[1], R[0], R[1]]

    sem = lambda name: nc.alloc_semaphore(name)
    con_in, x_in, par_in, wsmall_in, hot_in = sem("con_in"), sem("x_in"), sem("par_in"), sem("wsmall_in"), sem("hot_in")
    tb_in, tbs_in, g2_in, cw2_in, rows_out = sem("tb_in"), sem("tbs_in"), sem("g2_in"), sem("cw2_in"), sem("rows_out")
    w_loaded = [sem(f"w_loaded{s}") for s in range(NRAW)]
    spill_out = [sem(f"spill_out{e}") for e in range(NSTAGE + 2)]
    swq_in, gates_in = sem("swq_in"), [sem(f"gates_in{s}") for s in range(2)]
    w_hi, w_lo, dense_done, dense_evac = sem("w_hi"), sem("w_lo"), sem("dense_done"), sem("dense_evac")
    prow_T, prow_ok, rel_mm, rel_ok, rel_tbl = sem("prow_T"), sem("prow_ok"), sem("rel_mm"), sem("rel_ok"), sem("rel_tbl")
    rel_in, sc_used = sem("rel_in"), sem("sc_used")
    xT_done, xsq_ok, xlo_ok, xsum_ok = sem("xT_done"), sem("xsq_ok"), sem("xlo_ok"), sem("xsum_ok")
    ss_done, std_ok = sem("ss_done"), sem("std_ok")
    mixed_ok, tanh_ok, eps_ok = sem("mixed_ok"), sem("tanh_ok"), sem("eps_ok")
    zmm_done, sig_ok = sem("zmm_done"), sem("sig_ok")
    kk_raw, kk_sq, kk_ss, kk_std = sem("kk_raw"), sem("kk_sq"), sem("kk_ss"), sem("kk_std")
    cum_ok = sem("cum_ok")
    exp_ok, arbk_ok, ag_mm, bkend_ok, vt_T, vt_ok, bkt_T, bkt_ok = (sem(s) for s in (
        "exp_ok", "arbk_ok", "ag_mm", "bkend_ok", "vt_T", "vt_ok", "bkt_T", "bkt_ok"))
    ag_ok, x2t_ok, x2_mm, x2_ok, am_ok = (sem(s) for s in ("ag_ok", "x2t_ok", "x2_mm", "x2_ok", "am_ok"))
    u_mm, uc_ok, ubd_ok, xa_mm, xt_ok, xtbd_ok = (sem(s) for s in ("u_mm", "uc_ok", "ubd_ok", "xa_mm", "xt_ok", "xtbd_ok"))
    svz_ok, t1_mm, t1_dve, t1_act, sa_mm, sa_dve, sa_act = (sem(s) for s in (
        "svz_ok", "t1_mm", "t1_dve", "t1_act", "sa_mm", "sa_dve", "sa_act"))
    ys_mm, y_ok, st_ok = sem("ys_mm"), sem("y_ok"), sem("st_ok")
    gn_mean, gn_c, gn_sq, gn_var, gn_std, gn_bp, gn_bmm, gn_b, gn_n, gn_aff, gn_g, gn_ok = (sem(s) for s in (
        "gn_mean", "gn_c", "gn_sq", "gn_var", "gn_std", "gn_bp", "gn_bmm", "gn_b", "gn_n", "gn_aff", "gn_g", "gn_ok"))
    vtok_T, vtok_ok, gl_ok, gl_T, glt_ok = (sem(s) for s in ("vtok_T", "vtok_ok", "gl_ok", "gl_T", "glt_ok"))
    xsplit_ok, hg_u, hg_t, kv_mm, kv_ok = (sem(s) for s in ("xsplit_ok", "hg_u", "hg_t", "kv_mm", "kv_ok"))
    qk_mm, s_used, p_exp, p_T, pts_ok, ptw_ok, pv_mm, o_ok, o_T, oT_ok = (sem(s) for s in (
        "qk_mm", "s_used", "p_exp", "p_T", "pts_ok", "ptw_ok", "pv_mm", "o_ok", "o_T", "oT_ok"))
    sq_mm, ssw_used, sp_exp, sp_T, spt_ok, spv_mm, so_ok, so_T, soT_ok = (sem(s) for s in (
        "sq_mm", "ssw_used", "sp_exp", "sp_T", "spt_ok", "spv_mm", "so_ok", "so_T", "soT_ok"))
    ohi_ok, olo_ok, gsig_ok, mt_ok, mhi_ok, mlo_ok = (sem(s) for s in (
        "ohi_ok", "olo_ok", "gsig_ok", "mt_ok", "mhi_ok", "mlo_ok"))
    xtok_in, x1T, x1T_ok, out_sq, out_sum, post_ss, post_std, post_rinv = (sem(s) for s in (
        "xtok_in", "x1T", "x1T_ok", "out_sq", "out_sum", "post_ss", "post_std", "post_rinv"))
    x1_ok, h2hi_ok, h2lo_ok, x1_sq, x1_sum, pre_ss, pre_std, pre_rinv = (sem(s) for s in (
        "x1_ok", "h2hi_ok", "h2lo_ok", "x1_sq", "x1_sum", "pre_ss", "pre_std", "pre_rinv"))
    ff_gate, ff_sig, ff_x, ff_hid, ff_hi, ff_lo = (sem(s) for s in (
        "ff_gate", "ff_sig", "ff_x", "ff_hid", "ff_hi", "ff_lo"))
    dn_evac, dn_sq, dn_sum, fin_ss, fin_std, fin_ok, fin_T, fin_act, fin_dve, out_stored = (sem(s) for s in (
        "dn_evac", "dn_sq", "dn_sum", "fin_ss", "fin_std", "fin_ok", "fin_T", "fin_act", "fin_dve", "out_stored"))

    def chunked(w, c0, n=P):
        return w.rearrange("(k p) n -> p k n", p=P)[:, :, c0:c0 + n]

    def job_sources(n):
        kind, i, part, _ = JOBS[n]
        full = slice(0, P)
        if kind in ("nsa", "swa") and i < 4:
            c = (NSA0 if kind == "nsa" else SWA0) + HD * i
            return [(slice(0, HD), chunked(w_in, c, HD)), (slice(HD, P), chunked(w_in, c + 4 * HD, HD))]
        if kind == "rwkv":
            return [(full, chunked(w_in, P * i))]
        if kind == "nsa":
            return [(full, chunked(w_in, NSA0 + P * i))]
        if kind == "swa":
            return [(full, chunked(w_in, SWA0 + P * i))]
        if kind == "gate":
            return [(full, chunked(w_in, GATE0 + (i % 3) * D + P * (i // 3)))]
        if kind == "cmp":
            return [(full, chunked((ck1, cv1)[i // 2][part * D:(part + 1) * D, :], P * (i % 2)))]
        if kind == "branch":
            return [(full, chunked(w_branch[i % 3], P * (i // 3)))]
        if kind == "out":
            return [(full, chunked(w_out, P * i))]
        raise ValueError(kind)

    def spill_sem(n):
        return spill_out[SPILLED.index(n) % NSTAGE if n < CMP0 else NSTAGE + n % 2]

    def spilled_before(eng, n):
        jobs = [m for m in SPILLED if m < n]
        for s in spill_out:
            mine = [m for m in jobs if spill_sem(m) is s]
            if mine:
                eng.wait_ge(s, 16 * len(mine))

    class Chain:
        def __init__(self, eng, name):
            self.eng, self.sem, self.n = eng, nc.alloc_semaphore(name), 0

        def do(self, ins):
            self.n += 1
            ins.then_inc(self.sem, 1)

        def link(self, ins):
            self.do(ins)
            self.eng.wait_ge(self.sem, self.n)

        def settle(self):
            self.eng.wait_ge(self.sem, self.n)

    block = nc.Block()
    with block:
        @block.sync
        def _(sp):
            sp.dma_start(XTOK0[:, :, :], x.rearrange("(t p) d -> p t d", p=P)).then_inc(x_in, 16)
            for n in range(FF0):
                if n - 5 in SPILLED:
                    sp.wait_ge(dense_evac, group_of(n - 5) + 1)
                    sp.dma_start(spilled[SPILLED.index(n - 5)], stage(n - 5)).then_inc(spill_sem(n - 5), 16)
                if n == GB0 + 4:
                    sp.wait_ge(gn_ok, 4)
                    spilled_before(sp, CMP0)
                    sp.dma_start(SWQ[:, :, :], spilled[0:6].rearrange("b p t -> p b t")).then_inc(swq_in, 16)
                for d in range(GS, KC):
                    if n == MERGE0 + max(1, 3 * (d - 2)):
                        sp.wait_ge(pv_mm, 32)
                        sp.wait_ge(s_used, 32)
                        if d >= 5:
                            sp.wait_ge(mt_ok, d - 4)
                        spilled_before(sp, GC0)
                        at0, e0 = 3 * d % 15, 6 + 3 * (d - GS)
                        sp.dma_start(GATES[:, at0:at0 + 3, :], spilled[e0:e0 + 3].rearrange("b p t -> p b t"))\
                            .then_inc(gates_in[(d - GS) % 2], 16)
                if n >= NRAW:
                    sp.wait_ge(w_lo, n - NRAW + 1)
                for cols, src in job_sources(n):
                    sp.dma_start(WRAW[:, n % NRAW, 0:JOBS[n][3], cols], src).then_inc(w_loaded[n % NRAW], 16)
                if n == OUT0 + 3:
                    sp.wait_ge(dense_done, OUT0)
                    sp.dma_start(XTOK[:, :, :], x.rearrange("(t p) d -> p t d", p=P)).then_inc(xtok_in, 16)
            wg, wu = (w.rearrange("(k p) n -> p k n", p=P) for w in (w_gate, w_up))
            with sp.Fori(0, NF // 2) as i:
                for u in range(4):
                    n = FF0 + u
                    sp.wait_ge(w_lo, i * 4 + (n - NRAW + 1))
                    sp.dma_start(WRAW[:, n % NRAW, :, :],
                                 (wg, wu)[u % 2][:, :, bass.ds(i * (2 * P) + P * (u // 2), P)])\
                        .then_inc(w_loaded[n % NRAW], 16)
            wd = w_down.rearrange("(k p) n -> p k n", p=P)
            with sp.Fori(0, KC) as i:
                k0 = 0
                for q in range(4):
                    n = DN0 + q
                    sp.wait_ge(w_lo, i * 4 + (n - NRAW + 1))
                    sp.dma_start(WRAW[:, n % NRAW, 0:DPARTS[q], :],
                                 wd[:, k0:k0 + DPARTS[q], bass.ds(i * P, P)]).then_inc(w_loaded[n % NRAW], 16)
                    k0 += DPARTS[q]
            for t in range(4):
                sp.wait_ge(fin_act, t + 1)
                sp.wait_ge(fin_dve, t + 1)
                sp.dma_start(out.rearrange("(t p) d -> p t d", p=P)[:, t, :], OTOK[:, t, :]).then_inc(out_stored, 16)
            sp.wait_ge(out_stored, 64)

        @block.gpsimd
        def _(pool):
            pool.memset(TBL[:, :], NEG).then_inc(rel_tbl, 1)
            pool.wait_ge(rel_tbl, 1)
            pool.dma_start(TBL[0:32, :], rel_bias).then_inc(rel_in, 16)

            def lo_part(n, chunks):
                return pool.tensor_tensor(WLO[:, n % NSPL, 0:chunks, :], WRAW[:, n % NRAW, 0:chunks, :],
                                          WHI[:, n % NSPL, 0:chunks, :].bitcast(F32), ALU.subtract)

            for n in range(FF0):
                if n in POOL_HI:
                    pool.wait_ge(w_loaded[n % NRAW], loaded_value(n))
                    pool.wait_ge(dense_done, n - NSPL + 1)
                    pool.tensor_copy(WHI[:, n % NSPL, 0:JOBS[n][3], :],
                                     WRAW[:, n % NRAW, 0:JOBS[n][3], :]).then_inc(w_hi, 1)
                pool.wait_ge(w_hi, n + 1)
                lo_part(n, JOBS[n][3]).then_inc(w_lo, 1)
            with pool.Fori(0, NF // 2) as i:
                for u in range(4):
                    pool.wait_ge(w_hi, i * 4 + (FF0 + u + 1))
                    lo_part(FF0 + u, 8).then_inc(w_lo, 1)
            with pool.Fori(0, KC) as i:
                for q in range(4):
                    pool.wait_ge(w_hi, i * 4 + (DN0 + q + 1))
                    lo_part(DN0 + q, DPARTS[q]).then_inc(w_lo, 1)

        @block.scalar
        def _(act):
            act.dma_start(CONP[:, :], con[:, 0:NCONP]).then_inc(con_in, 16)
            act.dma_start(PRAW[0:NPAR1, 0, :], par1).then_inc(par_in, 16)
            act.dma_start(PRAW[0:NPAR2, 1, :], par2).then_inc(par_in, 16)
            act.dma_start(MASK[:, :], con[:, NCONP:NCON]).then_inc(con_in, 16)
            act.dma_start(WA[0:64, :], w2).then_inc(wsmall_in, 16)
            act.dma_start(WA[64:128, :], a2).then_inc(wsmall_in, 16)
            act.dma_start(HOT[:, :], hot).then_inc(hot_in, 16)
            act.dma_start(SNK, bass.AP(sinks.tensor, 0, [[0, P], [1, NH]])).then_inc(hot_in, 16)

            def hi_part(n, chunks=None):
                act.wait_ge(w_loaded[n % NRAW], loaded_value(n))
                if n >= NSPL:
                    act.wait_ge(dense_done, n - NSPL + 1)
                if n in (CMP0, MERGE0):
                    act.wait_ge(w_hi, n)
                act.activation(WHI[:, n % NSPL, 0:JOBS[n][3], :], WRAW[:, n % NRAW, 0:JOBS[n][3], :],
                               ACT.Copy).then_inc(w_hi, 1)

            act.wait_ge(rel_ok, 1)
            act.dma_start(bias_rows, VR[:, :]).then_inc(rows_out, 16)
            act.wait_ge(prow_ok, 2)
            for k in range(KC):
                act.wait_ge(xT_done, k + 1)
                act.activation(HHI[:, k, :], R[k % 4][:, :], ACT.Identity, scale=par("g_pre_mix", k))
                if k >= 2:
                    act.wait_ge(xsum_ok, k - 1)
                act.activation(SQ[:, k % 2, :], R[k % 4][:, :], ACT.Square).then_inc(xsq_ok, 1)
                if k == 3:
                    hi_part(0)
            hi_part(1)
            act.wait_ge(ss_done, 1)
            act.wait_ge(eps_ok, 1)
            act.activation(SQ[:, 0, :], R[4][:, :], ACT.Sqrt, scale=1.0 / D, bias=EPSC[:, 0:1]).then_inc(std_ok, 1)
            for n in range(2, NS0):
                hi_part(n)
            act.wait_ge(mixed_ok, 13)
            act.activation(RW[0:64, 12, :], RW[0:64, 12, :], ACT.Tanh).then_inc(tanh_ok, 1)
            act.wait_ge(mixed_ok, 14)
            act.activation(RW[:, 13, :], RW[:, 13, :], ACT.Sigmoid).then_inc(tanh_ok, 1)
            act.wait_ge(rows_out, 16)
            for m in range(4):
                act.wait_ge(zmm_done, m + 1)
                act.activation(CUM[:, m, :], R[(2 * m) % 6][:, :], ACT.Sigmoid, bias=par("w0", m)).then_inc(sig_ok, 1)
                act.activation(AA[:, m, :], R[(2 * m + 1) % 6][:, :], ACT.Sigmoid, bias=par("a0", m)).then_inc(sig_ok, 1)
            act.wait_ge(zmm_done, 4)
            act.dma_start(WA[:, :], g2).then_inc(g2_in, 16)
            for m in range(4):
                act.wait_ge(kk_raw, m + 1)
                if m >= 2:
                    act.wait_ge(kk_ss, m - 1)
                act.activation(SQ[:, m % 2, :], KK[:, m, :], ACT.Square).then_inc(kk_sq, 1)
            for m in range(4):
                act.wait_ge(kk_ss, m + 1)
                act.activation(TMP[:, m, :], R[m][:, :], ACT.Sqrt).then_inc(kk_std, 1)

            for cp in range(4):
                s = slice(cp * P, (cp + 1) * P)
                if cp == 0:
                    act.wait_ge(cum_ok, 4)
                    act.wait_ge(st_ok, 1)
                else:
                    act.wait_ge(x2t_ok, cp)
                    act.wait_ge(am_ok, 5 * cp)
                act.activation(E1[:, :, :], CUM[:, :, s], ACT.Exp).then_inc(exp_ok, 1)
                act.activation(E2[:, :, :], CUM[:, :, s], ACT.Exp, scale=-1.0).then_inc(exp_ok, 1)
                act.wait_ge(vt_T, cp + 1)
                if cp:
                    act.wait_ge(ys_mm, 2 * cp)
                for c in range(2):
                    act.activation(SV[64:128, c, :], R[c][64:128, :], ACT.Copy).then_inc(vt_ok, 1)
                act.wait_ge(bkt_T, cp + 1)
                for c in range(2):
                    act.activation(BKT[:, c, :, :], R[4 + c][:, :].rearrange("p (m n) -> p m n", m=4),
                                   ACT.Copy).then_inc(bkt_ok, 1)
                for lv in range(5):
                    g = 5 * cp + lv
                    act.wait_ge(uc_ok, g + 1)
                    for h in range(2):
                        act.activation(UBD[64 * h:64 * h + 64, :, 64 * h:64 * h + 64], UC[64 * h:64 * h + 64, :, :],
                                       ACT.Copy).then_inc(ubd_ok, 1)
                    if lv < 3:
                        act.wait_ge(xt_ok, g + 1)
                        act.wait_ge(xa_mm, g + 1)
                        for h in range(2):
                            act.activation(XTBD[64 * h:64 * h + 64, :, 64 * h:64 * h + 64],
                                           XTC[64 * h:64 * h + 64, :, :], ACT.Copy).then_inc(xtbd_ok, 1)
                for c in range(2):
                    g = 2 * cp + c
                    p = slice(64 * c, 64 * c + 64)
                    act.wait_ge(t1_mm, g + 1)
                    act.activation(T1[p, 4:8, :], R[1][p, 0:256].rearrange("p (a b) -> p a b", a=4),
                                   ACT.Copy).then_inc(t1_act, 1)
                    act.wait_ge(sa_mm, g + 1)
                    act.activation(SV[0:64, c, 256:512], R[5][0:64, 0:256], ACT.Copy).then_inc(sa_act, 1)
                    act.wait_ge(ys_mm, g + 1)
                    t0 = cp * P + c * C
                    for q in range(2):
                        act.activation(KK[64 * q:64 * q + 64, :, t0:t0 + C],
                                       R[3 + q][64 * q:64 * q + 64, 0:256].rearrange("p (a b) -> p a b", a=4),
                                       ACT.Copy).then_inc(y_ok, 1)
            act.wait_ge(ys_mm, 8)
            act.wait_ge(st_ok, 9)
            rows = bias_rows.tensor
            act.dma_start(TB[:, :, :], bass.AP(rows, 0, [[1, P], [1024, NH], [1, T]])).then_inc(tb_in, 16)
            hi_part(CMP0)
            hi_part(CMP0 + 1)
            for m in range(4):
                act.wait_ge(gn_c, m + 1)
                act.activation(KK[:, m, :], TMP[:, m, :], ACT.Square).then_inc(gn_sq, 1)
            act.wait_ge(xsplit_ok, 2)
            for kv, w in enumerate((ck2, cv2)):
                act.dma_start(CW2[:, kv, :, :], w.rearrange("(h p) d -> p h d", p=P)).then_inc(cw2_in, 16)
            hi_part(CMP0 + 2)
            hi_part(CMP0 + 3)
            for m in range(4):
                act.wait_ge(gn_var, m + 1)
                act.activation(KK[:, m, :], R[m][:, :], ACT.Sqrt, scale=1.0 / HD, bias=EPSC[:, 1:2]).then_inc(gn_std, 1)
            for i in range(4):
                act.wait_ge(hg_u, i + 1)
                act.activation(HT[:, i % 2, :], HT[:, i % 2, :], ACT.Tanh, scale=0.7978845608028654).then_inc(hg_t, 1)
                if i < 2:
                    hi_part(CMP0 + 2 * i + 4)
                    hi_part(CMP0 + 2 * i + 5)
                if i == 0:
                    for m in range(4):
                        act.wait_ge(gn_n, m + 1)
                        act.activation(TMP[:, m, :], TMP[:, m, :], ACT.Identity, scale=par("ln_w", m),
                                       bias=par("ln_b", m)).then_inc(gn_aff, 1)
            act.wait_ge(gn_ok, 4)
            act.dma_start(TBS[:, :, :], bass.AP(rows, 640, [[1, P], [1024, NH], [1, 256]])).then_inc(tbs_in, 16)
            act.wait_ge(dense_evac, group_of(NS0 + 10) + 1)
            act.activation(GL[:, :], GL[:, :], ACT.Sigmoid).then_inc(gl_ok, 1)
            act.wait_ge(vtok_T, 1)
            for b in range(2):
                act.activation(VT[:, b, :, :], R[2 + b][:, :].rearrange("p (a b) -> p a b", a=4),
                               ACT.Copy).then_inc(vtok_ok, 1)

            def nsa_exp(u):
                i, h = divmod(u, NH)
                w = P * (i + 1)
                act.wait_ge(s_used, u + 1)
                act.activation(ECB[:, u % 2, 0:8 * i + 7], ECB[:, u % 2, 0:8 * i + 7], ACT.Exp,
                               bias=STAT[:, u % 2, 0:1], accum_out=STAT[:, u % 2, 3:4])
                for b in range(2):
                    last = act.activation(EB[:, u % 2, b, 0:w], EB[:, u % 2, b, 0:w], ACT.Exp,
                                          bias=STAT[:, u % 2, 1 + b:2 + b], accum_out=STAT[:, u % 2, 4 + b:5 + b])
                last.then_inc(p_exp, 1)

            def nsa_ptw(u):
                w = P * (u // NH + 1)
                act.wait_ge(p_T, u + 1)
                if u >= 2:
                    act.wait_ge(pv_mm, u - 1)
                act.activation(PTB[:, u % 2, 1, 0:w], R[4][:, 0:w], ACT.Copy).then_inc(ptw_ok, 1)

            def nsa_oT(i):
                act.wait_ge(o_T, i + 1)
                act.activation(O[:, 1, :, i * P:(i + 1) * P], R[3][:, :].rearrange("p (a b) -> p a b", a=4),
                               ACT.Copy).then_inc(oT_ok, 1)

            for u in range(34):
                if u < 32:
                    nsa_exp(u)
                if 1 <= u < 33:
                    nsa_ptw(u - 1)
                if u >= 3 and (u - 3) % NH == NH - 1:
                    nsa_oT((u - 3) // NH)
            nsa_oT(3)
            act.wait_ge(vtok_T, 2)
            act.activation(VT[:, 2, :, :], R[2][:, :].rearrange("p (a b) -> p a b", a=4), ACT.Copy).then_inc(vtok_ok, 1)

            def swa_exp(v):
                blk = v // 4
                w = WIN if blk == 0 else 2 * WIN
                act.wait_ge(ssw_used, v + 1)
                act.activation(STATS[:, v % 2, 4:6], STATS[:, v % 2, 4:6], ACT.Exp)
                for g in range(2):
                    last = act.activation(EB[:, v % 2, g, 0:w], EB[:, v % 2, g, 0:w], ACT.Exp,
                                          bias=STATS[:, v % 2, g:g + 1], accum_out=STATS[:, v % 2, 2 + g:3 + g])
                last.then_inc(sp_exp, 1)

            def swa_oT(blk):
                act.wait_ge(so_T, blk + 1)
                act.activation(O[:, 2, :, blk * P:(blk + 1) * P], R[2][:, :].rearrange("p (a b) -> p a b", a=4),
                               ACT.Copy).then_inc(soT_ok, 1)

            for v in range(18):
                if v < 16:
                    swa_exp(v)
                if v >= 3 and (v - 3) % 4 == 3:
                    swa_oT((v - 3) // 4)
            swa_oT(3)

            hi_part(MERGE0)
            for b in range(3):
                for m in range(4):
                    if b == 0 and m == 0:
                        act.wait_ge(gn_ok, 4)
                        act.wait_ge(oT_ok, 4)
                        act.wait_ge(so_T, 4)
                        act.wait_ge(soT_ok, 4)
                        act.wait_ge(vtok_ok, 3)
                    act.activation(OHI[:, b, m, :], O[:, b, m, :], ACT.Copy).then_inc(ohi_ok, 1)
                if b == 0:
                    hi_part(MERGE0 + 1)
            act.wait_ge(dense_evac, group_of(MERGE0 - 1) + 1)
            n = MERGE0 + 2
            for d in range(KC):
                if d >= GS:
                    act.wait_ge(gates_in[(d - GS) % 2], 16 * ((d - GS) // 2 + 1))
                for b in range(3):
                    i = 3 * d % 15 + b
                    act.activation(GATES[:, i, :], GATES[:, i, :], ACT.Sigmoid).then_inc(gsig_ok, 1)
                    hi_part(n)
                    n += 1
                act.wait_ge(mt_ok, d + 1)
                act.activation(MHI[:, d, :], MT[:, d % 2, :], ACT.Copy).then_inc(mhi_ok, 1)
            for d in range(KC):
                if n < FF0:
                    hi_part(n)
                    n += 1
                act.wait_ge(dense_evac, group_of(OUT0 + d) + 1)
                if d >= 2:
                    act.wait_ge(out_sum, d - 1)
                act.activation(SQ[:, d % 2, :], OT[:, d, :], ACT.Square).then_inc(out_sq, 1)
            assert n == FF0
            act.wait_ge(post_ss, 1)
            act.activation(SQ[:, 0, :], R[4][:, :], ACT.Sqrt, scale=1.0 / D, bias=EPSC[:, 0:1]).then_inc(post_std, 1)
            for k in range(KC):
                if k == 0:
                    act.wait_ge(post_rinv, 1)
                act.wait_ge(x1_ok, k + 1)
                act.activation(HHI[:, k, :], X1[:, k, :], ACT.Identity, scale=par("g_pre_ffn", k)).then_inc(h2hi_ok, 1)
                if k >= 2:
                    act.wait_ge(x1_sum, k - 1)
                act.activation(SQ[:, k % 2, :], X1[:, k, :], ACT.Square).then_inc(x1_sq, 1)
                if k == 0:
                    for m in range(2):
                        act.wait_ge(w_loaded[(FF0 + m) % NRAW], loaded_value(FF0 + m))
                        act.wait_ge(dense_done, FF0 + m - NSPL + 1)
                        act.activation(WHI[:, (FF0 + m) % NSPL, :, :], WRAW[:, (FF0 + m) % NRAW, :, :],
                                       ACT.Copy).then_inc(w_hi, 1)
            act.wait_ge(pre_ss, 1)
            act.activation(SQ[:, 0, :], R[4][:, :], ACT.Sqrt, scale=1.0 / D, bias=EPSC[:, 0:1]).then_inc(pre_std, 1)

            def hi_loop(n, i, chunks):
                act.wait_ge(w_loaded[n % NRAW], i * 16 + loaded_value(n))
                act.wait_ge(dense_done, i * 4 + (n - NSPL + 1))
                act.activation(WHI[:, n % NSPL, 0:chunks, :], WRAW[:, n % NRAW, 0:chunks, :],
                               ACT.Copy).then_inc(w_hi, 1)

            def ffn_act(f, i):
                act.wait_ge(ff_gate, i * 2 + (f + 1))
                act.activation(FT[:, 3 * (f % 2) + 1, :], FT[:, 3 * (f % 2), :], ACT.Sigmoid).then_inc(ff_sig, 1)
                act.wait_ge(ff_hid, i * 2 + (f + 1))
                act.activation(DHI[:, bass.ds(i * 2 + f, 1), :],
                               FT[:, 3 * (f % 2) + 2, :], ACT.Copy).then_inc(ff_hi, 1)

            with act.Fori(0, NF // 2 - 1) as i:
                hi_loop(FF0 + 2, i, 8)
                hi_loop(FF0 + 3, i, 8)
                ffn_act(0, i)
                hi_loop(FF0 + 4, i, 8)
                hi_loop(FF0 + 5, i, 8)
                ffn_act(1, i)
            i = NF // 2 - 1
            hi_loop(FF0 + 2, i, 8)
            hi_loop(FF0 + 3, i, 8)
            ffn_act(0, i)
            for q in range(2):
                hi_loop(DN0 + q, 0, DPARTS[q])
            ffn_act(1, i)
            for q in (2, 3):
                hi_loop(DN0 + q, 0, DPARTS[q])
            act.wait_ge(pre_rinv, 1)
            with act.Fori(1, KC) as d:
                for q in range(4):
                    hi_loop(DN0 + 4 + q, d - 1, DPARTS[q])
                act.wait_ge(dn_evac, d + 2)
                act.activation(SQ[:, 0, :], OF[:, bass.ds(d - 1, 1), :], ACT.Square).then_inc(dn_sq, 1)
                act.wait_ge(dn_sum, d)
            act.wait_ge(dn_evac, KC + 2)
            act.activation(SQ[:, 0, :], OF[:, KC - 1, :], ACT.Square).then_inc(dn_sq, 1)
            act.wait_ge(fin_ss, 1)
            act.wait_ge(dn_sum, KC)
            act.activation(SQ[:, 0, :], R[4][:, :], ACT.Sqrt, scale=1.0 / D, bias=EPSC[:, 0:1]).then_inc(fin_std, 1)
            for n in range(0, 8, 2):
                act.wait_ge(fin_T, n + 1)
                act.activation(OTOK[:, n // 2, 0:512], R[n % 4][:, :], ACT.Copy).then_inc(fin_act, 1)

        @block.vector
        def _(dve):
            chain = Chain(dve, "dve_chain")
            link, do = chain.link, chain.do
            state = {"evac": 0}

            def evac_rinv(n, dst):
                dve.wait_ge(dense_done, n + 1)
                return dve.tensor_tensor(dst, DB[group_of(n) % 2][:, :], RINV[:, :], ALU.mult)

            def evac(n):
                kind, i, part, _ = JOBS[n]
                if n in SPILLED and n < CMP0 and SPILLED.index(n) >= NSTAGE:
                    e = SPILLED.index(n)
                    dve.wait_ge(spill_out[e % NSTAGE], 16 * (e // NSTAGE))
                if n == GC0:
                    spilled_before(dve, GC0)
                if kind in ("nsa", "swa") and i < 4:
                    dst = NQ[:, i, :] if kind == "nsa" else stage(n)
                    dve.wait_ge(dense_done, n + 1)
                    ins = dve.scalar_tensor_tensor(out=dst, in0=DB[group_of(n) % 2][:, :], scalar=HD ** -0.5,
                                                   in1=RINV[:, :], op0=ALU.mult, op1=ALU.mult)
                elif kind == "nsa":
                    ins = evac_rinv(n, NQ[:, i, :] if i < 10 else GL[:, :])
                elif kind == "swa":
                    ins = evac_rinv(n, stage(n))
                elif kind == "gate":
                    ins = evac_rinv(n, stage(n) if n in SPILLED else GATES[:, i, :])
                elif kind == "cmp":
                    gelu(n, i)
                    return
                ins.then_inc(dense_evac, 1)

            def gelu(n, i):
                dve.wait_ge(dense_done, n + 1)
                ps = DB[group_of(n) % 2][:, 0:2 * NCMP]
                link(dve.tensor_scalar(HG[:, i, :], ps, 1.0, None, ALU.mult))
                link(dve.tensor_tensor(HT[:, i % 2, :], HG[:, i, :], HG[:, i, :], ALU.mult))
                link(dve.tensor_scalar(HT[:, i % 2, :], HT[:, i % 2, :], 0.044715, 1.0, ALU.mult, ALU.add))
                dve.tensor_tensor(HT[:, i % 2, :], HT[:, i % 2, :], HG[:, i, :], ALU.mult).then_inc(hg_u, 1)
                dve.wait_ge(hg_t, i + 1)
                link(dve.scalar_tensor_tensor(out=HG[:, i, :], in0=HT[:, i % 2, :], scalar=1.0, in1=HG[:, i, :],
                                              op0=ALU.add, op1=ALU.mult))
                dve.tensor_scalar(HG[:, i, :], HG[:, i, :], 0.5, None, ALU.mult).then_inc(dense_evac, 1)

            def evacs(point):
                while NS0 + state["evac"] < DONE[point]:
                    n = NS0 + state["evac"]
                    if n == CMP0:
                        chain.settle()
                    if ends_group(n):
                        evac(n)
                    state["evac"] += 1

            dve.memset(EPSC[:, 0:1], EPS)
            dve.memset(EPSC[:, 1:2], LN_EPS).then_inc(eps_ok, 1)
            dve.wait_ge(con_in, 32)
            dve.wait_ge(prow_T, 1)
            dve.tensor_copy(PARC[:, 0:NPAR1], R[4][:, 0:NPAR1]).then_inc(prow_ok, 1)
            dve.tensor_copy(PARC[:, NPAR1:NPAR1 + NPAR2], R[5][:, 0:NPAR2]).then_inc(prow_ok, 1)
            dve.wait_ge(prow_ok, 2)
            dve.wait_ge(rel_mm, 1)
            dve.tensor_copy(VR[:, 0:512], DB[0][0:8, :])
            dve.tensor_copy(VR[:, 512:640], DB[1][0:8, 0:128])
            dve.tensor_copy(VR[:, 640:1024], R[3][0:8, 0:384]).then_inc(rel_ok, 1)
            for k in range(KC):
                dve.wait_ge(xsq_ok, k + 1)
                dve.scalar_tensor_tensor(out=HLO[:, k, :], in0=R[k % 4][:, :], scalar=par("g_pre_mix", k),
                                         in1=HHI[:, k, :].bitcast(F32), op0=ALU.mult, op1=ALU.subtract).then_inc(xlo_ok, 1)
                if k == 0:
                    dve.tensor_copy(SSUM[:, :], SQ[:, 0, :]).then_inc(xsum_ok, 1)
                else:
                    dve.wait_ge(xsum_ok, k)
                    dve.tensor_tensor(SSUM[:, :], SSUM[:, :], SQ[:, k % 2, :], ALU.add).then_inc(xsum_ok, 1)
            dve.wait_ge(std_ok, 1)
            link(dve.reciprocal(RINV[:, :], SQ[:, 0, :]))
            dve.wait_ge(prow_T, 1)
            link(dve.memset(PSH[:, :, 0:1], 0.0))
            for n in range(NS0):
                cur = PSH[:, n % 2, 1:T + 1]
                dve.wait_ge(dense_done, n + 1)
                ins = dve.tensor_tensor(cur, DB[n % 2][:, :], RINV[:, :], ALU.mult)
                ins.then_inc(dense_evac, 1)
                dve.wait_ge(dense_evac, n + 1)
                link(dve.tensor_tensor(DSH[:, :], PSH[:, n % 2, 0:T], cur, ALU.subtract))
                dve.scalar_tensor_tensor(out=RW[:, n, :], in0=DSH[:, :], scalar=par("mu", n), in1=cur,
                                         op0=ALU.mult, op1=ALU.add).then_inc(mixed_ok, 1)
            dve.wait_ge(mixed_ok, NS0)
            for m in range(4):
                dve.tensor_scalar(KK[:, m, :], RW[:, 4 + m, :], par("k_k", m), None, ALU.mult).then_inc(kk_raw, 1)
            evacs(PT_UP)
            dve.wait_ge(sig_ok, 8)
            for m in range(4):
                link(dve.tensor_scalar(CUM[:, m, :], CUM[:, m, :], -float(np.exp(-0.5)), None, ALU.mult))
                dve.tensor_tensor_scan(CUM[:, m, :], mask("reset", T), CUM[:, m, :], 0.0, ALU.mult, ALU.add)\
                   .then_inc(cum_ok, 1)
                do(dve.tensor_scalar(DSH[:, :], AA[:, m, :], 1.0, par("k_a", m), ALU.subtract, ALU.mult))
                if m == 0:
                    dve.wait_ge(kk_raw, 4)
                chain.settle()
                link(dve.scalar_tensor_tensor(out=RW[:, 4 + m, :], in0=DSH[:, :], scalar=1.0, in1=RW[:, 4 + m, :],
                                              op0=ALU.add, op1=ALU.mult))
            evacs(PT_UP + 1)
            for m in range(4):
                dve.wait_ge(kk_std, m + 1)
                link(dve.tensor_scalar(TMP[:, m, :], TMP[:, m, :], 1e-12, None, ALU.max))
                link(dve.reciprocal(TMP[:, m, :], TMP[:, m, :]))
                link(dve.scalar_tensor_tensor(out=KK[:, m, :], in0=TMP[:, m, :], scalar=-1.0, in1=KK[:, m, :],
                                              op0=ALU.mult, op1=ALU.mult))
                link(dve.scalar_tensor_tensor(out=AA[:, m, :], in0=KK[:, m, :], scalar=-1.0, in1=AA[:, m, :],
                                              op0=ALU.mult, op1=ALU.mult))
            evacs(PT_UP + 2)
            link(dve.memset(UBD[:, :, :], 0.0))
            dve.memset(ST[:, :, :, :], 0.0).then_inc(st_ok, 1)

            def two(ap):
                return ap.rearrange("p m (c t) -> p m c t", c=2)

            for cp in range(4):
                pt = PT_CP[cp]
                s = slice(cp * P, (cp + 1) * P)
                dve.wait_ge(exp_ok, 2 * cp + 2)
                if cp:
                    dve.wait_ge(ys_mm, 2 * cp)
                do(dve.tensor_tensor(AR[:, :, :, C:P], two(RW[:, 0:4, s]), two(E1[:, :, :]), ALU.mult))
                do(dve.tensor_tensor(AR[:, :, :, 1:C], two(KK[:, :, s])[:, :, :, 1:C], two(E1[:, :, :])[:, :, :, 0:C - 1],
                                     ALU.mult))
                do(dve.tensor_copy(AR[:, :, :, 0:1], two(KK[:, :, s])[:, :, :, 0:1]))
                do(dve.tensor_copy(PCS.rearrange("p (m c) -> p m c", c=2).unsqueeze(3), two(E1[:, :, :])[:, :, :, C - 1:C]))
                do(dve.tensor_tensor(BK[:, :, :, 0:C], two(AA[:, :, s]), two(E2[:, :, :]), ALU.mult))
                dve.tensor_tensor(BK[:, :, :, C:P], two(RW[:, 4:8, s]), two(E2[:, :, :]), ALU.mult).then_inc(arbk_ok, 1)
                dve.memset(SV[0:64, :, :], 0.0).then_inc(svz_ok, 1)
                evacs(pt)
                dve.wait_ge(ag_mm, cp + 1)
                chain.settle()
                dve.wait_ge(arbk_ok, cp + 1)
                for q in range(2):
                    do(dve.tensor_tensor(
                        ABD[:, 4 * q:4 * q + 4, :].rearrange("p a (c t) -> p a c t", c=2),
                        R[q][:, 0:256].rearrange("p (a t) -> p a t", a=4).unsqueeze(2).broadcast_to([P, 4, 2, C]),
                        mask("maskA").rearrange("p (c t) -> p c t", c=2).unsqueeze(1).broadcast_to([P, 4, 2, C]), ALU.mult))
                for c in range(2):
                    for q in range(2):
                        ins = dve.tensor_tensor(G[:, c, 4 * q:4 * q + 4, :],
                                                R[2 + 2 * c + q][:, :].rearrange("p (a b) -> p a b", a=4),
                                                mask("maskG").unsqueeze(1).broadcast_to([P, 4, P]), ALU.mult)
                        if c == 1 and q == 1:
                            ins.then_inc(ag_ok, 1)
                        else:
                            do(ins)
                dve.tensor_tensor(BK[:, :, :, :].rearrange("p m c n -> p (m c) n"),
                                  BK[:, :, :, :].rearrange("p m c n -> p (m c) n"),
                                  PCS.unsqueeze(2).broadcast_to([P, NH, P]), ALU.mult).then_inc(bkend_ok, 1)
                chain.settle()
                if cp:
                    dve.wait_ge(xtbd_ok, 6 * cp)
                link(dve.tensor_tensor(XTBD[:, :, :], ABD[:, :, :], mask("m1").unsqueeze(1).broadcast_to([P, NH, P]), ALU.mult))
                link(dve.tensor_tensor(XTBD[:, :, :], XTBD[:, :, :], ident.unsqueeze(1).broadcast_to([P, NH, P]), ALU.add))
                dve.tensor_tensor(XTC[:, :, :], XTBD[:, :, 0:C], XTBD[:, :, C:P], ALU.add).then_inc(x2t_ok, 1)
                evacs(pt + 1)

                def am(lv):
                    if lv:
                        dve.wait_ge(u_mm, 5 * cp + lv)
                    dve.tensor_tensor(AM[:, :, :], ABD[:, :, :],
                                      mask(f"m{2 << lv}").unsqueeze(1).broadcast_to([P, NH, P]), ALU.mult).then_inc(am_ok, 1)

                am(0)
                dve.wait_ge(x2_mm, cp + 1)
                dve.tensor_copy(XC[:, :, :], R[0][:, :].rearrange("p (a b) -> p a b", a=NH)).then_inc(x2_ok, 1)
                dve.wait_ge(x2_ok, cp + 1)
                for lv in range(5):
                    g = 5 * cp + lv
                    dve.wait_ge(u_mm, g + 1)
                    if g:
                        dve.wait_ge(xa_mm, g)
                    dve.tensor_copy(UC[:, :, :], R[1][:, :].rearrange("p (a b) -> p a b", a=NH)).then_inc(uc_ok, 1)
                    if lv < 4:
                        am(lv + 1)
                    evacs(pt + 2 + 2 * lv)
                    dve.wait_ge(xa_mm, g + 1)
                    dve.wait_ge(x2t_ok, cp + 1)
                    if lv:
                        dve.wait_ge(xt_ok, g)
                    if lv < 4:
                        do(dve.tensor_tensor(XC[:, :, :], XC[:, :, :], R[2][:, :].rearrange("p (a b) -> p a b", a=NH), ALU.add))
                        chain.settle()
                    dve.tensor_tensor(XTC[:, :, :], XTC[:, :, :], R[3][:, :].rearrange("p (a b) -> p a b", a=NH),
                                      ALU.add).then_inc(xt_ok, 1)
                    if lv < 4:
                        evacs(pt + 3 + 2 * lv)
                for c in range(2):
                    g = 2 * cp + c
                    p = slice(64 * c, 64 * c + 64)
                    dve.wait_ge(t1_mm, g + 1)
                    dve.tensor_copy(T1[p, 0:4, :], R[0][p, 0:256].rearrange("p (a b) -> p a b", a=4)).then_inc(t1_dve, 1)
                    dve.wait_ge(st_ok, g + 1)
                    link(dve.tensor_tensor(ST[:, (g + 1) % 2, :, :], ST[:, g % 2, :, :],
                                           PCS.rearrange("p (m c) -> p m c", c=2)[:, :, c:c + 1].broadcast_to([P, 4, C]),
                                           ALU.mult))
                    dve.wait_ge(sa_mm, g + 1)
                    dve.tensor_copy(SV[0:64, c, 0:256], R[2][0:64, 0:256]).then_inc(sa_dve, 1)
                    if c == 0:
                        evacs(pt + 2 + 2 * 4 + 1)
                        evacs(pt + 2 + 2 * 4 + 2)
                    dve.wait_ge(ys_mm, g + 1)
                    dve.tensor_tensor(ST[:, (g + 1) % 2, :, :], ST[:, (g + 1) % 2, :, :],
                                      R[5][:, 0:256].rearrange("p (a b) -> p a b", a=4), ALU.add).then_inc(st_ok, 1)
                evacs(pt + 13)

            for m in range(4):
                dve.scalar_tensor_tensor(out=CUM[:, m, :], in0=RW[:, m, :], scalar=par("r_k", m), in1=RW[:, 4 + m, :],
                                         op0=ALU.mult, op1=ALU.mult).then_inc(gn_bp, 1)
            evacs(PT_GN)
            dve.wait_ge(y_ok, 16)
            for kv in range(2):
                dve.wait_ge(dense_evac, group_of(NS0 + 10) + 1)
                pe = PARC[:, PAR["pe"] + 32 * kv:PAR["pe"] + 32 * kv + 32]
                for l in range(2):
                    for g in range(2):
                        p = slice(64 * g, 64 * g + 64)
                        src = NQ[p, 4 + kv, :]
                        for half in range(2):
                            v = src[:, 16 * half:16 * half + 16 * NCMP].rearrange("p (c j l) -> p j c l", j=8, l=2)[:, :, :, l]
                            e = pe[p, :].rearrange("p (j l) -> p j l", l=2)[:, 8 * half:8 * half + 8, l:l + 1]
                            do(dve.tensor_tensor(XF[64 * l:64 * l + 64, 8 * half:8 * half + 8, g * NCMP:(g + 1) * NCMP],
                                                 v, e.broadcast_to([64, 8, NCMP]), ALU.add))
                chain.settle()
                link(dve.tensor_copy(XHI[:, kv, :, :], XF[:, :, :]))
                dve.tensor_tensor(XLO[:, kv, :, :], XF[:, :, :], XHI[:, kv, :, :].bitcast(F32), ALU.subtract)\
                   .then_inc(xsplit_ok, 1)
                dve.wait_ge(xsplit_ok, kv + 1)
            for m in range(4):
                dve.wait_ge(gn_mean, m + 1)
                dve.scalar_tensor_tensor(out=TMP[:, m, :], in0=R[m][:, :], scalar=-1.0 / HD, in1=KK[:, m, :],
                                         op0=ALU.mult, op1=ALU.add).then_inc(gn_c, 1)

            def gn_bonus(m):
                dve.wait_ge(gn_bmm, m + 1)
                dve.tensor_tensor(AA[:, m, :], R[4 + m % 2][:, :], RW[:, 8 + m, :], ALU.mult).then_inc(gn_b, 1)

            evacs(PT_GN + 1)
            gn_bonus(0)
            gn_bonus(1)
            evacs(PT_GN + 2)
            for m in range(4):
                dve.wait_ge(gn_std, m + 1)
                dve.wait_ge(gn_c, m + 1)
                link(dve.reciprocal(KK[:, m, :], KK[:, m, :]))
                dve.tensor_tensor(TMP[:, m, :], TMP[:, m, :], KK[:, m, :], ALU.mult).then_inc(gn_n, 1)
            gn_bonus(2)
            gn_bonus(3)
            for m in range(4):
                dve.wait_ge(gn_aff, m + 1)
                dve.wait_ge(gn_b, m + 1)
                link(dve.tensor_tensor(AA[:, m, :], AA[:, m, :], TMP[:, m, :], ALU.add))
                dve.wait_ge(gn_g, m + 1)
                dve.tensor_tensor(O[:, 0, m, :], AA[:, m, :], R[m][:, :], ALU.mult).then_inc(gn_ok, 1)
            evacs(PT_GN + 3)
            evacs(PT_GN + 4)
            evacs(PT_GN + 5)
            dve.wait_ge(gl_T, 1)
            dve.tensor_copy(GLT[:, :, :], R[0][:, 0:96].rearrange("p (a b) -> p a b", a=4)).then_inc(glt_ok, 1)
            dve.wait_ge(kv_mm, 1)
            dve.tensor_copy(KCT[:, :], R[1][:, 0:NCMP])
            dve.tensor_copy(VCT[0:NCMP, :, :], R[1][0:NCMP, 128:256].rearrange("p (a b) -> p a b", a=2)).then_inc(kv_ok, 1)
            dve.wait_ge(glt_ok, 1)
            dve.wait_ge(tb_in, 16)

            def bias_of(tiles, h, at0, n, step=1):
                full = tiles[:, h, :]
                return bass.AP(full.tensor, full.offset + at0, [list(full.ap[0]), [-step, n]])

            def nsa_scores(u):
                i, h = divmod(u, NH)
                w, nc_ = P * (i + 1), 8 * i + 7
                dve.wait_ge(qk_mm, u + 1)
                if u >= 2:
                    dve.wait_ge(p_T, u - 1)
                st = STAT[:, u % 2, :]
                dve.tensor_tensor_reduce(ECB[:, u % 2, 0:nc_], R[2][:, 0:nc_], bias_of(TB, h, P * (i + 1) - 32, nc_, 16),
                                         1.0, -3e38, ALU.add, ALU.max, st[:, 0:1]).then_inc(sc_used, 1)
                for b in range(2):
                    do(dve.tensor_tensor_reduce(EB[:, u % 2, b, 0:w], R[b][:, 0:w], bias_of(TB, h, w - 1, w),
                                                1.0, -3e38, ALU.add, ALU.max, st[:, 1 + b:2 + b]))
                chain.settle()
                dve.tensor_scalar(st[:, 0:3], st[:, 0:3], -1e25, -1.0, ALU.max, ALU.mult).then_inc(s_used, 1)

            def nsa_pts(u):
                w = P * (u // NH + 1)
                dve.wait_ge(p_T, u + 1)
                if u >= 2:
                    dve.wait_ge(pv_mm, u - 1)
                nc_ = 8 * (u // NH) + 7
                dve.tensor_copy(PTC[0:nc_, u % 2, :], R[2][0:nc_, 384:512])
                dve.tensor_copy(PTB[:, u % 2, 0, 0:w], R[3][:, 0:w]).then_inc(pts_ok, 1)

            def nsa_out(u):
                i, h = divmod(u, NH)
                st = STAT[:, u % 2, :]
                wt = STAT2[:, u % 2, :]
                o = OTK[:, i % 2, HD * h:HD * h + HD]
                dve.wait_ge(pv_mm, u + 1)
                if h == 0 and i >= 2:
                    dve.wait_ge(o_T, i - 1)
                link(dve.tensor_tensor(o, R[5][:, 0:64], wt[:, 0:1].broadcast_to([P, HD]), ALU.mult))
                link(dve.scalar_tensor_tensor(out=o, in0=R[5][:, 64:128], scalar=wt[:, 1:2], in1=o, op0=ALU.mult, op1=ALU.add))
                dve.scalar_tensor_tensor(out=o, in0=R[5][:, 128:192], scalar=wt[:, 2:3], in1=o,
                                         op0=ALU.mult, op1=ALU.add).then_inc(o_ok, 1)

            def nsa_weights(u):
                i, h = divmod(u, NH)
                st = STAT[:, u % 2, :]
                wt = STAT2[:, u % 2, :]
                dve.wait_ge(p_exp, u + 1)
                if u >= 2:
                    dve.wait_ge(o_ok, u - 1)
                link(dve.tensor_scalar(wt, st[:, 3:6], 1e-30, None, ALU.max))
                link(dve.reciprocal(wt, wt))
                link(dve.tensor_tensor(wt, wt, GLT[:, i, h:3 * NH:NH], ALU.mult))

            for u in range(34):
                if u < 32:
                    nsa_scores(u)
                if 1 <= u < 33:
                    nsa_weights(u - 1)
                    nsa_pts(u - 1)
                if u >= 2:
                    nsa_out(u - 2)
                evacs(PT_NSA + u)

            def swa_scores(v):
                blk, j = divmod(v, 4)
                w = WIN if blk == 0 else 2 * WIN
                dve.wait_ge(sq_mm, v + 1)
                if v >= 2:
                    dve.wait_ge(sp_T, v - 1)
                st = STATS[:, v % 2, :]
                for g in range(2):
                    do(dve.tensor_tensor_reduce(EB[:, v % 2, g, 0:w], R[g][:, 0:w], bias_of(TBS, j + 4 * g, w - 1, w),
                                                1.0, -3e38, ALU.add, ALU.max, st[:, g:g + 1]))
                chain.settle()
                link(dve.tensor_tensor(st[:, 0:2], st[:, 0:2], SNK[:, j:NH:4], ALU.max))
                do(dve.tensor_tensor(st[:, 4:6], SNK[:, j:NH:4], st[:, 0:2], ALU.subtract))
                chain.settle()
                dve.tensor_scalar(st[:, 0:2], st[:, 0:2], -1.0, None, ALU.mult).then_inc(ssw_used, 1)

            def swa_pt(v):
                w = 256 if v // 4 == 0 else 512
                dve.wait_ge(sp_T, v + 1)
                if v >= 2:
                    dve.wait_ge(spv_mm, v - 1)
                dve.tensor_copy(PTB[:, v % 2, 0, 0:w], R[3][:, 0:w]).then_inc(spt_ok, 1)
                st = STATS[:, v % 2, :]
                dve.wait_ge(sp_exp, v + 1)
                if v >= 2:
                    dve.wait_ge(so_ok, v - 1)
                link(dve.tensor_tensor(st[:, 6:8], st[:, 2:4], st[:, 4:6], ALU.add))
                link(dve.reciprocal(st[:, 6:8], st[:, 6:8]))

            def swa_out(v):
                blk, j = divmod(v, 4)
                st = STATS[:, v % 2, :]
                dve.wait_ge(spv_mm, v + 1)
                if j == 0 and blk >= 2:
                    dve.wait_ge(so_T, blk - 1)
                for g in range(2):
                    ins = dve.tensor_scalar(OTS[:, blk % 2, HD * (j + 4 * g):HD * (j + 4 * g) + HD],
                                            R[5][:, 64 * g:64 * g + 64], st[:, 6 + g:7 + g], None, ALU.mult)
                ins.then_inc(so_ok, 1)

            dve.wait_ge(p_T, 32)
            dve.wait_ge(tbs_in, 16)
            for v in range(18):
                if v < 16:
                    swa_scores(v)
                if 1 <= v < 17:
                    swa_pt(v - 1)
                if v >= 2:
                    swa_out(v - 2)
                evacs(PT_SWA + v)

            def split_o(b, m):
                dve.wait_ge(ohi_ok, 4 * b + m + 1)
                dve.tensor_tensor(OLO[:, b, m, :], O[:, b, m, :], OHI[:, b, m, :].bitcast(F32), ALU.subtract)\
                   .then_inc(olo_ok, 1)

            for b in range(3):
                for m in range(4):
                    split_o(b, m)
            dve.wait_ge(olo_ok, 12)
            n = MERGE0
            for d in range(KC):
                gates = GATES[:, 3 * d % 15:3 * d % 15 + 3, :]
                for b in range(3):
                    dve.wait_ge(gsig_ok, 3 * d + b + 1)
                    dve.wait_ge(dense_done, n + 1)
                    if b == 0:
                        if d >= 2:
                            dve.wait_ge(mhi_ok, d - 1)
                        ins = dve.tensor_tensor(MT[:, d % 2, :], DB[group_of(n) % 2][:, :], gates[:, 0, :], ALU.mult)
                    else:
                        ins = dve.tensor_tensor(DSH2[:, b - 1, :], DB[group_of(n) % 2][:, :], gates[:, b, :], ALU.mult)
                    ins.then_inc(dense_evac, 1)
                    dve.wait_ge(dense_evac, group_of(n) + 1)
                    if b:
                        ins = dve.tensor_tensor(MT[:, d % 2, :], MT[:, d % 2, :], DSH2[:, b - 1, :], ALU.add)
                        if b == 1:
                            link(ins)
                        else:
                            ins.then_inc(mt_ok, 1)
                    n += 1
                dve.wait_ge(mhi_ok, d + 1)
                dve.tensor_tensor(MLO[:, d, :], MT[:, d % 2, :], MHI[:, d, :].bitcast(F32), ALU.subtract).then_inc(mlo_ok, 1)
            dve.wait_ge(mlo_ok, KC)
            for d in range(KC):
                if d == 5:
                    for k in range(KC):
                        dve.wait_ge(x1T, k + 1)
                        dve.tensor_copy(X1[:, k, :], R[k % 4][:, :]).then_inc(x1T_ok, 1)
                dve.wait_ge(dense_done, n + 1)
                dve.tensor_copy(OT[:, d, :], DB[group_of(n) % 2][:, :]).then_inc(dense_evac, 1)
                dve.wait_ge(dense_evac, group_of(n) + 1)
                n += 1
                dve.wait_ge(out_sq, d + 1)
                if d == 0:
                    dve.tensor_copy(SSUM[:, :], SQ[:, 0, :]).then_inc(out_sum, 1)
                else:
                    dve.wait_ge(out_sum, d)
                    dve.tensor_tensor(SSUM[:, :], SSUM[:, :], SQ[:, d % 2, :], ALU.add).then_inc(out_sum, 1)
            assert n == FF0
            dve.wait_ge(post_std, 1)
            dve.reciprocal(RINV[:, :], SQ[:, 0, :]).then_inc(post_rinv, 1)
            dve.wait_ge(post_rinv, 1)
            dve.wait_ge(x1T_ok, KC)
            for k in range(KC):
                link(dve.scalar_tensor_tensor(out=OT[:, k, :], in0=OT[:, k, :], scalar=par("g_post_mix", k), in1=RINV[:, :],
                                              op0=ALU.mult, op1=ALU.mult))
                dve.tensor_tensor(X1[:, k, :], X1[:, k, :], OT[:, k, :], ALU.add).then_inc(x1_ok, 1)
                dve.wait_ge(h2hi_ok, k + 1)
                dve.scalar_tensor_tensor(out=HLO[:, k, :], in0=X1[:, k, :], scalar=par("g_pre_ffn", k),
                                         in1=HHI[:, k, :].bitcast(F32), op0=ALU.mult, op1=ALU.subtract).then_inc(h2lo_ok, 1)
                dve.wait_ge(x1_sq, k + 1)
                if k == 0:
                    dve.tensor_copy(SSUM[:, :], SQ[:, 0, :]).then_inc(x1_sum, 1)
                else:
                    dve.wait_ge(x1_sum, k)
                    dve.tensor_tensor(SSUM[:, :], SSUM[:, :], SQ[:, k % 2, :], ALU.add).then_inc(x1_sum, 1)
            dve.wait_ge(pre_std, 1)
            dve.reciprocal(RINV[:, :], SQ[:, 0, :]).then_inc(pre_rinv, 1)
            dve.wait_ge(pre_rinv, 1)

            with dve.Fori(0, NF // 2) as i:
                for f in range(2):
                    b = 3 * f
                    dve.wait_ge(dense_done, i * 4 + (FF0 + 2 * f + 1))
                    dve.tensor_tensor(FT[:, b, :], DB4[2 * f][:, :], RINV[:, :], ALU.mult).then_inc(ff_gate, 1)
                    dve.wait_ge(ff_sig, i * 2 + (f + 1))
                    dve.wait_ge(ff_gate, i * 2 + (f + 1))
                    dve.tensor_tensor(FT[:, b + 1, :], FT[:, b + 1, :], FT[:, b, :], ALU.mult).then_inc(ff_x, 1)
                    dve.wait_ge(ff_x, i * 4 + (2 * f + 1))
                    dve.tensor_tensor(FT[:, b, :], FT[:, b + 1, :], RINV[:, :], ALU.mult).then_inc(ff_x, 1)
                    dve.wait_ge(ff_x, i * 4 + (2 * f + 2))
                    dve.wait_ge(dense_done, i * 4 + (FF0 + 2 * f + 2))
                    dve.tensor_tensor(FT[:, b + 2, :], FT[:, b, :], DB4[2 * f + 1][:, :], ALU.mult).then_inc(ff_hid, 1)
                    dve.wait_ge(ff_hi, i * 2 + (f + 1))
                    dve.tensor_tensor(DLO[:, bass.ds(i * 2 + f, 1), :], FT[:, b + 2, :],
                                      DHI[:, bass.ds(i * 2 + f, 1), :].bitcast(F32), ALU.subtract).then_inc(ff_lo, 1)
                    dve.wait_ge(ff_lo, i * 2 + (f + 1))
            dve.memset(SSUM[:, :], 0.0).then_inc(dn_evac, 2)
            dve.wait_ge(dn_evac, 2)
            with dve.Fori(0, KC // 2) as i:
                for b in range(2):
                    dve.wait_ge(dense_done, i * 8 + (DN0 + 4 * b + 4))
                    dve.tensor_copy(OF[:, bass.ds(i * 2 + b, 1), :], DB[b][:, :]).then_inc(dn_evac, 1)
                    dve.wait_ge(dn_sq, i * 2 + (b + 1))
                    dve.tensor_tensor(SSUM[:, :], SSUM[:, :], SQ[:, 0, :], ALU.add).then_inc(dn_sum, 1)
                    dve.wait_ge(dn_sum, i * 2 + (b + 1))
            dve.wait_ge(fin_std, 1)
            link(dve.reciprocal(RINV[:, :], SQ[:, 0, :]))
            for k in range(KC):
                link(dve.scalar_tensor_tensor(out=OF[:, k, :], in0=OF[:, k, :], scalar=par("g_post_ffn", k), in1=RINV[:, :],
                                              op0=ALU.mult, op1=ALU.mult))
                dve.tensor_tensor(X1[:, k, :], X1[:, k, :], OF[:, k, :], ALU.add).then_inc(fin_ok, 1)
            for n in range(1, 8, 2):
                dve.wait_ge(fin_T, n + 1)
                dve.tensor_copy(OTOK[:, n // 2, 512:1024], R[n % 4][:, :]).then_inc(fin_dve, 1)

        @block.tensor
        def _(pe):
            dense = {"n": 0, "k": 0}

            def rhs(n, k):
                kind, i, part, _ = JOBS[n]
                if kind == "cmp":
                    kv, c = i // 2, 8 * part + k
                    return XHI[:, kv, c, :], XLO[:, kv, c, :]
                if kind == "branch":
                    return OHI[:, i % 3, k, :], OLO[:, i % 3, k, :]
                if kind == "out":
                    return MHI[:, k, :], MLO[:, k, :]
                return HHI[:, k, :], HLO[:, k, :]

            def product(dst, n, k, hi, lo, start, stop):
                s = n % NSPL
                pe.matmul(dst, WHI[:, s, k, :], hi, start=start, stop=False)
                pe.matmul(dst, WHI[:, s, k, :], lo, start=False, stop=False)
                return pe.matmul(dst, WLO[:, s, k, :], hi, start=False, stop=stop)

            def steps(count):
                for _ in range(count):
                    n, k = dense["n"], dense["k"]
                    kind, i, part, chunks = JOBS[n]
                    g = group_of(n)
                    if k == 0:
                        pe.wait_ge(w_lo, n + 1)
                        if part == 0 and g >= 2:
                            pe.wait_ge(dense_evac, g - 1)
                        if kind == "cmp":
                            pe.wait_ge(xsplit_ok, i // 2 + 1)
                        if kind == "branch":
                            pe.wait_ge(olo_ok, 4 * (i % 3) + 4)
                    if n == 0:
                        pe.wait_ge(xlo_ok, k + 1)
                    if n == OUT0:
                        pe.wait_ge(mlo_ok, k + 1)
                    hi, lo = rhs(n, k)
                    dst = DB[g % 2][:, 0:2 * NCMP] if kind == "cmp" else DB[g % 2][:, :]
                    last = product(dst, n, k, hi, lo, part == 0 and k == 0, ends_group(n) and k == chunks - 1)
                    dense["k"] += 1
                    if k == chunks - 1:
                        last.then_inc(dense_done, 1)
                        dense["n"], dense["k"] = n + 1, 0

            def fill(point):
                steps(FILL[point])

            def tr(dst, src, n=P):
                return pe.transpose(dst, src, ident[0:n, 0:n])

            pe.wait_ge(con_in, 32)
            pe.wait_ge(par_in, 32)
            tr(R[4][:, 0:NPAR1], PRAW[0:NPAR1, 0, :], NPAR1)
            tr(R[5][:, 0:NPAR2], PRAW[0:NPAR2, 1, :], NPAR2).then_inc(prow_T, 1)
            pe.wait_ge(hot_in, 32)
            pe.wait_ge(rel_in, 16)
            pe.matmul(DB[0][0:8, :], TBL[:, 0:8], HOT[:, 0:512], start=True, stop=True)
            pe.matmul(DB[1][0:8, 0:128], TBL[:, 0:8], HOT[:, 512:640], start=True, stop=True)
            pe.matmul(R[3][0:8, 0:384], TBL[:, 8:16], HOT[:, 640:1024], start=True, stop=True).then_inc(rel_mm, 1)
            pe.wait_ge(x_in, 16)
            for k in range(KC):
                if k == 3:
                    pe.wait_ge(rel_ok, 1)
                if k >= 4:
                    pe.wait_ge(xlo_ok, k - 3)
                    pe.wait_ge(xsq_ok, k - 3)
                for t in range(4):
                    last = tr(R[k % 4][:, t * P:(t + 1) * P], XTOK0[:, t, k * P:(k + 1) * P])
                last.then_inc(xT_done, 1)
            steps(8)
            pe.wait_ge(xsum_ok, KC)
            pe.wait_ge(prow_ok, 2)
            pe.matmul(R[4][:, :], ones, SSUM[:, :], start=True, stop=True).then_inc(ss_done, 1)
            steps(8 * (NS0 - 1))
            pe.wait_ge(wsmall_in, 32)
            pe.wait_ge(tanh_ok, 1)
            for m in range(4):
                if m == 3:
                    pe.wait_ge(sig_ok, 2)
                pe.matmul(R[(2 * m) % 6][:, :], WA[0:64, m * P:(m + 1) * P], RW[0:64, 12, :], start=True, stop=True)
                pe.matmul(R[(2 * m + 1) % 6][:, :], WA[64:128, m * P:(m + 1) * P], RW[64:128, 12, :],
                          start=True, stop=True).then_inc(zmm_done, 1)
            fill(PT_UP)
            pe.wait_ge(sig_ok, 8)
            for m in range(4):
                pe.wait_ge(kk_sq, m + 1)
                pe.matmul(R[m][:, :], bones, SQ[:, m % 2, :], start=True, stop=True).then_inc(kk_ss, 1)
            fill(PT_UP + 1)
            fill(PT_UP + 2)

            for cp in range(4):
                pt = PT_CP[cp]
                if cp == 0:
                    pe.wait_ge(kk_std, 4)
                    pe.wait_ge(st_ok, 1)
                else:
                    pe.wait_ge(y_ok, 4 * cp)
                    pe.wait_ge(t1_act, 2 * cp)
                flat = RW[:, :, :].rearrange("p a t -> p (a t)")
                for c in range(2):
                    for m in range(4):
                        at0 = (8 + m) * T + cp * P + c * C - C
                        last = tr(R[c][:, m * P:(m + 1) * P], flat[:, at0:at0 + P])
                last.then_inc(vt_T, 1)
                pe.wait_ge(arbk_ok, cp + 1)
                if cp:
                    pe.wait_ge(st_ok, 2 * cp + 1)
                for c in range(2):
                    for h in range(NH):
                        q, m = h % 2, h // 2
                        p = slice(64 * q, 64 * q + 64)
                        pe.matmul(R[2 + 2 * c + q][:, m * P:(m + 1) * P], BK[p, m, c, :], AR[p, m, c, :],
                                  start=True, stop=True)
                pe.wait_ge(vt_ok, 2 * cp + 2)
                for h in range(NH):
                    q, m = h % 2, h // 2
                    p = slice(64 * q, 64 * q + 64)
                    for c in range(2):
                        last = pe.matmul(R[q][64 * c:64 * c + 64, m * C:(m + 1) * C], BK[p, m, c, 0:C], AR[p, m, c, 0:C],
                                         start=True, stop=True)
                last.then_inc(ag_mm, 1)
                fill(pt)
                pe.wait_ge(bkend_ok, cp + 1)
                pe.wait_ge(ag_ok, cp + 1)
                for c in range(2):
                    for m in range(4):
                        last = tr(R[4 + c][:, m * P:(m + 1) * P], BK[:, m, c, :])
                last.then_inc(bkt_T, 1)
                pe.wait_ge(x2t_ok, cp + 1)
                for h in range(NH):
                    last = pe.matmul(R[0][:, h * C:(h + 1) * C], XTBD[:, h, :], mask("ic", C), start=True, stop=True)
                last.then_inc(x2_mm, 1)
                fill(pt + 1)
                for lv in range(5):
                    g = 5 * cp + lv
                    pe.wait_ge(am_ok, g + 1)
                    if lv == 0:
                        pe.wait_ge(x2_ok, cp + 1)
                    else:
                        pe.wait_ge(xt_ok, g)
                    for h in range(NH):
                        last = pe.matmul(R[1][:, h * C:(h + 1) * C], AM[:, h, :], XC[:, h, :], start=True, stop=True)
                    last.then_inc(u_mm, 1)
                    fill(pt + 2 + 2 * lv)
                    pe.wait_ge(uc_ok, g + 1)
                    if lv:
                        pe.wait_ge(xtbd_ok, 6 * cp + 2 * min(lv, 3))
                    if lv < 4:
                        for h in range(NH):
                            pe.matmul(R[2][:, h * C:(h + 1) * C], XTBD[:, h, :], UC[:, h, :], start=True, stop=True)
                    pe.wait_ge(ubd_ok, 2 * g + 2)
                    for h in range(NH):
                        last = pe.matmul(R[3][:, h * C:(h + 1) * C], UBD[:, h, :], XTC[:, h, :], start=True, stop=True)
                    last.then_inc(xa_mm, 1)
                    if lv < 4:
                        fill(pt + 3 + 2 * lv)
                pe.wait_ge(xt_ok, 5 * cp + 5)
                pe.wait_ge(bkt_ok, 2 * cp + 2)
                pe.wait_ge(svz_ok, cp + 1)
                for c in range(2):
                    g = 2 * cp + c
                    pe.wait_ge(st_ok, g + 1)
                    tp = slice(64 * c, 64 * c + 64)
                    for h in range(NH):
                        q, m = h % 2, h // 2
                        p = slice(64 * q, 64 * q + 64)
                        dst = R[q][tp, m * C:(m + 1) * C]
                        pe.matmul(dst, G[:, c, 4 * q + m, 0:C], SV[:, c, h * HD:(h + 1) * HD], start=True, stop=False)
                        last = pe.matmul(dst, AR[p, m, c, 0:C], ST[p, g % 2, m, :], start=False, stop=True)
                    last.then_inc(t1_mm, 1)
                    pe.wait_ge(t1_dve, g + 1)
                    pe.wait_ge(t1_act, g + 1)
                    if g:
                        pe.wait_ge(y_ok, 2 * g)
                    for h in range(NH):
                        q, m = h % 2, h // 2
                        last = pe.matmul(R[2 if h < 4 else 5][0:64, (h % 4) * HD:(h % 4 + 1) * HD], XTC[tp, 4 * q + m, :], T1[tp, 4 * q + m, :],
                                         start=True, stop=True)
                    last.then_inc(sa_mm, 1)
                    if c == 0:
                        fill(pt + 11)
                        fill(pt + 12)
                    pe.wait_ge(sa_dve, g + 1)
                    pe.wait_ge(sa_act, g + 1)
                    for h in range(NH):
                        q, m = h % 2, h // 2
                        pe.matmul(R[5][64 * q:64 * q + 64, m * C:(m + 1) * C], BKT[:, c, m, 64 * q:64 * q + 64],
                                  SV[:, c, h * HD:(h + 1) * HD], start=True, stop=True)
                    for h in range(NH):
                        q, m = h % 2, h // 2
                        p = slice(64 * q, 64 * q + 64)
                        dst = R[3 + q][p, m * C:(m + 1) * C]
                        pe.matmul(dst, SV[:, c, h * HD:(h + 1) * HD], G[:, c, 4 * q + m, C:P], start=True, stop=False)
                        last = pe.matmul(dst, ST[p, g % 2, m, :], AR[p, m, c, C:P], start=False, stop=True)
                    last.then_inc(ys_mm, 1)
                fill(pt + 13)

            fill(PT_GN)
            pe.wait_ge(y_ok, 16)
            pe.wait_ge(st_ok, 9)
            for m in range(4):
                pe.matmul(R[m][:, :], bones, KK[:, m, :], start=True, stop=True).then_inc(gn_mean, 1)

            def gn_bonus(m):
                pe.wait_ge(gn_bp, m + 1)
                if m >= 2:
                    pe.wait_ge(gn_b, m - 1)
                pe.matmul(R[4 + m % 2][:, :], bones, CUM[:, m, :], start=True, stop=True).then_inc(gn_bmm, 1)

            gn_bonus(0)
            gn_bonus(1)
            fill(PT_GN + 1)
            fill(PT_GN + 2)
            for m in range(4):
                pe.wait_ge(gn_sq, m + 1)
                pe.matmul(R[m][:, :], bones, KK[:, m, :], start=True, stop=True).then_inc(gn_var, 1)
            gn_bonus(2)
            gn_bonus(3)
            fill(PT_GN + 3)
            pe.wait_ge(g2_in, 16)
            for m in range(4):
                pe.wait_ge(gn_std, m + 1)
                pe.matmul(R[m][:, :], WA[:, m * P:(m + 1) * P], RW[:, 13, :], start=True, stop=True).then_inc(gn_g, 1)
            fill(PT_GN + 4)
            fill(PT_GN + 5)
            pe.wait_ge(gn_ok, 4)
            pe.wait_ge(gl_ok, 1)
            for t in range(4):
                last = pe.transpose(R[0][:, 24 * t:24 * t + 24], GL[0:24, t * P:(t + 1) * P], ident[0:24, 0:24])
            last.then_inc(gl_T, 1)
            for b in range(2):
                for t in range(4):
                    last = tr(R[2 + b][:, t * P:(t + 1) * P], NQ[:, 7 + 2 * b, t * P:(t + 1) * P])
            last.then_inc(vtok_T, 1)
            pe.wait_ge(cw2_in, 32)
            pe.wait_ge(dense_evac, group_of(GB0 - 1) + 1)
            for g in range(2):
                for half in range(2):
                    pe.matmul(R[1][64 * g:64 * g + 64, 0:NCMP], CW2[:, 0, half, :], HG[:, half, g * NCMP:(g + 1) * NCMP],
                              start=half == 0, stop=half == 1)
                for half in range(2):
                    last = pe.matmul(R[1][0:NCMP, 128 + 64 * g:192 + 64 * g], HG[:, 2 + half, g * NCMP:(g + 1) * NCMP],
                                     CW2[:, 1, half, :], start=half == 0, stop=half == 1)
            last.then_inc(kv_mm, 1)
            pe.wait_ge(kv_ok, 1)
            pe.wait_ge(vtok_ok, 2)
            pe.wait_ge(glt_ok, 1)

            def nsa_qk(u):
                i, h = divmod(u, NH)
                j, g = h % 4, h // 4
                p, w = slice(64 * g, 64 * g + 64), P * (i + 1)
                q = NQ[p, j, i * P:(i + 1) * P]
                if u:
                    pe.wait_ge(s_used, u)
                if u >= 2:
                    pe.wait_ge(pts_ok, u - 1)
                pe.matmul(R[2][:, 0:8 * i + 7], q, KCT[p, 0:8 * i + 7], start=True, stop=True)
                pe.matmul(R[0][:, 0:w], q, NQ[p, 6, 0:w], start=True, stop=True)
                pe.matmul(R[1][:, 0:w], q, NQ[p, 8, 0:w], start=True, stop=True).then_inc(qk_mm, 1)

            def nsa_pT(u):
                i = u // NH
                nc_ = 8 * i + 7
                pe.wait_ge(p_exp, u + 1)
                if u:
                    pe.wait_ge(pts_ok, u)
                    pe.wait_ge(ptw_ok, u)
                if u >= NH + 2:
                    pe.wait_ge(oT_ok, (u - 2) // NH)
                for b in range(2):
                    for k in range(i + 1):
                        tr(R[3 + b][:, k * P:(k + 1) * P], EB[:, u % 2, b, k * P:(k + 1) * P])
                pe.wait_ge(sc_used, min(u + 2, 32))
                tr(R[2][0:nc_, 384:512], ECB[:, u % 2, 0:nc_]).then_inc(p_T, 1)

            def nsa_pv(u):
                i, h = divmod(u, NH)
                g, nc_ = h // 4, 8 * (u // NH) + 7
                pe.wait_ge(pts_ok, u + 1)
                pe.wait_ge(ptw_ok, u + 1)
                if u:
                    pe.wait_ge(o_ok, u)
                pe.matmul(R[5][:, 0:64], PTC[0:nc_, u % 2, :], VCT[0:nc_, g, :], start=True, stop=True)
                for b in range(2):
                    for k in range(i + 1):
                        last = pe.matmul(R[5][:, 64 + 64 * b:128 + 64 * b], PTB[:, u % 2, b, k * P:(k + 1) * P],
                                         VT[:, b, k, 64 * g:64 * g + 64], start=k == 0, stop=k == i)
                last.then_inc(pv_mm, 1)

            def nsa_oT(i, u):
                pe.wait_ge(o_ok, 8 * (i + 1))
                pe.wait_ge(pts_ok, min(u, 32))
                for m in range(4):
                    last = tr(R[3][:, m * P:(m + 1) * P], OTK[:, i % 2, m * P:(m + 1) * P])
                last.then_inc(o_T, 1)

            for u in range(34):
                if u < 32:
                    nsa_qk(u)
                if 1 <= u < 33:
                    nsa_pT(u - 1)
                if u >= 2:
                    nsa_pv(u - 2)
                if u >= 3 and (u - 3) % NH == NH - 1:
                    nsa_oT((u - 3) // NH, u)
                fill(PT_NSA + u)
            nsa_oT(3, 34)

            pe.wait_ge(s_used, 32)
            pe.wait_ge(swq_in, 16)
            for t in range(4):
                last = tr(R[2][:, t * P:(t + 1) * P], SWQ[:, 5, t * P:(t + 1) * P])
            last.then_inc(vtok_T, 1)
            pe.wait_ge(vtok_ok, 3)
            pe.wait_ge(oT_ok, 4)

            def swa_qk(v):
                blk, j = divmod(v, 4)
                w = WIN if blk == 0 else 2 * WIN
                if v:
                    pe.wait_ge(ssw_used, v)
                for g in range(2):
                    p = slice(64 * g, 64 * g + 64)
                    last = pe.matmul(R[g][:, 0:w], SWQ[p, j, blk * WIN:(blk + 1) * WIN],
                                     SWQ[p, 4, (blk + 1) * WIN - w:(blk + 1) * WIN], start=True, stop=True)
                last.then_inc(sq_mm, 1)

            def swa_pT(v):
                n = 1 if v // 4 == 0 else 2
                pe.wait_ge(sp_exp, v + 1)
                if v:
                    pe.wait_ge(spt_ok, v)
                for g in range(2):
                    for k in range(n):
                        at0 = (g * n + k) * P
                        last = tr(R[3][:, at0:at0 + P], EB[:, v % 2, g, k * P:(k + 1) * P])
                last.then_inc(sp_T, 1)

            def swa_pv(v):
                blk = v // 4
                n = 1 if blk == 0 else 2
                pe.wait_ge(spt_ok, v + 1)
                if v:
                    pe.wait_ge(so_ok, v)
                else:
                    pe.wait_ge(o_ok, 32)
                for g in range(2):
                    for k in range(n):
                        last = pe.matmul(R[5][:, 64 * g:64 * g + 64], PTB[:, v % 2, 0, (g * n + k) * P:(g * n + k + 1) * P],
                                         VT[:, 2, blk + 1 - n + k, 64 * g:64 * g + 64], start=k == 0, stop=k == n - 1)
                last.then_inc(spv_mm, 1)

            def swa_oT(blk):
                pe.wait_ge(so_ok, 4 * (blk + 1))
                if blk:
                    pe.wait_ge(soT_ok, blk)
                for m in range(4):
                    last = tr(R[2][:, m * P:(m + 1) * P], OTS[:, blk % 2, m * P:(m + 1) * P])
                last.then_inc(so_T, 1)

            for v in range(18):
                if v < 16:
                    swa_qk(v)
                if 1 <= v < 17:
                    swa_pT(v - 1)
                if v >= 2:
                    swa_pv(v - 2)
                if v >= 3 and (v - 3) % 4 == 3:
                    swa_oT((v - 3) // 4)
                fill(PT_SWA + v)
            swa_oT(3)

            assert dense["n"] == MERGE0
            steps(sum(j[3] for j in JOBS[MERGE0:OUT0]))
            steps(8 * 5)
            pe.wait_ge(xtok_in, 16)
            for k in range(KC):
                if k >= 4:
                    pe.wait_ge(x1T_ok, k - 3)
                for t in range(4):
                    last = tr(R[k % 4][:, t * P:(t + 1) * P], XTOK[:, t, k * P:(k + 1) * P])
                last.then_inc(x1T, 1)
            steps(8 * (KC - 5))
            pe.wait_ge(out_sum, KC)
            pe.matmul(R[4][:, :], ones, SSUM[:, :], start=True, stop=True).then_inc(post_ss, 1)

            def ffn_tile(i, f, u, norm=False):
                n = FF0 + 2 * f + u
                pe.wait_ge(w_lo, i * 4 + (n + 1))
                for k in range(8):
                    if norm:
                        pe.wait_ge(h2lo_ok, k + 1)
                    last = product(DB4[2 * f + u][:, :], n, k, HHI[:, k, :], HLO[:, k, :], k == 0, k == 7)
                last.then_inc(dense_done, 1)

            pe.wait_ge(x1T_ok, KC)
            pe.wait_ge(dense_evac, group_of(FF0 - 1) + 1)
            ffn_tile(0, 0, 0, True)
            ffn_tile(0, 0, 1)
            pe.wait_ge(x1_sum, KC)
            pe.matmul(R[4][:, :], ones, SSUM[:, :], start=True, stop=True).then_inc(pre_ss, 1)
            ffn_tile(0, 1, 0)
            ffn_tile(0, 1, 1)
            with pe.Fori(1, NF // 2) as i:
                for f in range(2):
                    pe.wait_ge(ff_hid, i * 2 + (f - 1))
                    ffn_tile(i, f, 0)
                    ffn_tile(i, f, 1)
            pe.wait_ge(ff_lo, NF)
            with pe.Fori(0, KC // 2) as i:
                for b in range(2):
                    k0 = 0
                    for q in range(4):
                        n = DN0 + 4 * b + q
                        pe.wait_ge(w_lo, i * 8 + (n + 1))
                        if q == 0:
                            pe.wait_ge(dn_evac, i * 2 + (b + 1))
                        for k in range(DPARTS[q]):
                            last = product(DB[b][:, :], n, k, DHI[:, k0 + k, :], DLO[:, k0 + k, :],
                                           k0 + k == 0, k0 + k == NF - 1)
                        last.then_inc(dense_done, 1)
                        k0 += DPARTS[q]
            pe.wait_ge(dn_sum, KC)
            pe.matmul(R[4][:, :], ones, SSUM[:, :], start=True, stop=True).then_inc(fin_ss, 1)
            for n in range(8):
                if n == 0:
                    pe.wait_ge(fin_ok, KC)
                if n >= 4:
                    pe.wait_ge((fin_act, fin_dve)[n % 2], (n - 4) // 2 + 1)
                for m in range(4):
                    last = tr(R[n % 4][:, m * P:(m + 1) * P],
                              X1[:, 4 * (n % 2) + m, (n // 2) * P:(n // 2 + 1) * P])
                last.then_inc(fin_T, 1)


def kernel(**inputs):
    import concourse.bacc as bacc
    from concourse.bass_utils import run_bass_kernel_spmd

    a = {name: np.asarray(value) for name, value in inputs.items()}
    one = lambda name: a[name][0]
    rows = [one(name).reshape(-1, P) for name in (
        "norm_pre_mix", "norm_post_mix", "norm_pre_ffn", "norm_post_ffn", "rwkv_mu", "rwkv_w0", "rwkv_a0", "rwkv_k_k",
        "rwkv_k_a", "rwkv_r_k", "rwkv_ln_w", "rwkv_ln_b")]
    pe_rows = [np.concatenate([one(name), one(name)], axis=1) for name in ("nsa_pe_k", "nsa_pe_v")]
    con, hot = constants()
    arrays = {
        "x": a["x"][0], "w_in": one("w_in"), "w_branch": one("w_branch"), "w_out": one("w_out"),
        "w_gate": one("ffn_w_gate"), "w_up": one("ffn_w_up"), "w_down": one("ffn_w_down"),
        "w2": one("rwkv_w2"), "a2": one("rwkv_a2"), "g2": one("rwkv_g2"),
        "ck1": one("nsa_ck_w1"), "ck2": one("nsa_ck_w2"), "cv1": one("nsa_cv_w1"), "cv2": one("nsa_cv_w2"),
        "sinks": one("swa_sinks"), "rel_bias": a["rel_bias"],
        "par1": np.concatenate(rows, axis=0), "par2": np.concatenate(pe_rows, axis=0), "con": con, "hot": hot,
    }
    arrays = {f"in_{name}": np.ascontiguousarray(value) for name, value in arrays.items()}
    nc = bacc.Bacc("TRN2", target_bir_lowering=False, num_devices=1)
    args = [nc.dram_tensor(name, value.shape, F32, kind="ExternalInput").ap() for name, value in arrays.items()]
    out = nc.dram_tensor("out_0", (T, D), F32, kind="ExternalOutput").ap()
    build(nc, *args, out)
    r = run_bass_kernel_spmd(nc, [arrays], core_ids=[0])
    return r.results[0]["out_0"].reshape(1, T, D)
```

```python
import numpy as np
import concourse.bass as bass
from concourse import mybir

F32 = mybir.dt.float32
F32R = mybir.dt.float32r
ALU = mybir.AluOpType
ACT = mybir.ActivationFunctionType
AX = mybir.AxisListType

T, D, P = 512, 1024, 128
HD, NH = 64, 8
BW = NH * HD
KC = D // P
RW_COLS, NSA_COLS, SWA_COLS = 3 * BW + 256, BW + 6 * 128 + 3 * NH, BW + 256
NSA0, SWA0 = RW_COLS, RW_COLS + NSA_COLS
GATE0 = SWA0 + SWA_COLS
FFN = 2816
NF = FFN // P
NCMP = T // 16 - 1
WIN = 128
C = 64
CH = 256
NEG = -1e30
EPS, LN_EPS = 1e-6, 64e-5
BUCKET0 = list(range(16)) + [16, 21, 27, 35, 46, 59, 77, 99, 128, 166, 216, 280, 363, 470]

PAR = {}
_row = 0
for _name, _n in (("g_pre_mix", 8), ("g_post_mix", 8), ("g_pre_ffn", 8), ("g_post_ffn", 8), ("mu", 14), ("w0", 4),
                  ("a0", 4), ("k_k", 4), ("k_a", 4), ("r_k", 4), ("ln_w", 4), ("ln_b", 4)):
    PAR[_name] = _row
    _row += _n
NPAR1 = _row
NPAR2 = 64
PAR["pe"] = NPAR1

CON = {}
_col = 0
for _name, _n in (("ident", 128), ("bones", 128), ("ones", 128), ("maskG", 128), ("maskA", 192), ("m1", 128),
                  ("m2", 128), ("m4", 128), ("m8", 128), ("m16", 128), ("m32", 128), ("reset", 512), ("sel", 32)):
    CON[_name] = _col
    _col += _n
NCON, NCONP = _col, 384
CON["selT"] = NCON


def constants():
    con = np.zeros((P, NCON + 4 * P), np.float32)
    s, t = np.arange(P)[:, None], np.arange(P)[None, :]
    put = lambda name, x: con.__setitem__((slice(None), slice(CON[name], CON[name] + x.shape[1])), x)
    put("ident", s == t)
    put("bones", (s // C) == (t // C))
    put("ones", np.ones((P, P)))
    put("maskG", np.where(t < C, (s % C) < (t % C), (s % C) <= (t % C)))
    put("maskA", (np.arange(3 * C)[None, :] // C == 1) & (s % C < np.arange(3 * C)[None, :] % C))
    for m in (1, 2, 4, 8, 16, 32):
        put(f"m{m}", (s // (2 * m) == t // (2 * m)) & (s % (2 * m) < m) & (t % (2 * m) >= m))
    put("reset", np.broadcast_to(np.arange(T) % C != 0, (P, T)))
    head = np.arange(4)[:, None] * 2 + np.arange(P)[None, :] // HD
    put("sel", (head.T[:, :, None] == np.arange(NH)).reshape(P, 4 * NH))
    put("selT", np.pad((head.reshape(1, 4 * P) == np.arange(NH)[:, None]), ((0, P - NH), (0, 0))))
    hot = np.zeros((33, 1024), np.float32)
    for x in range(640):
        d = x - 127
        hot[32 if d < 0 else int(np.searchsorted(BUCKET0, d, side="right")) - 1, x] = 1
    for x in range(384):
        d = x - 127
        hot[32 if d < 0 or d >= WIN else int(np.searchsorted(BUCKET0, d, side="right")) - 1, 640 + x] = 1
    return con, hot


JOBS = []
for _n in range(14):
    JOBS.append(("rwkv", _n, 0, 8))
NS0 = len(JOBS)
for _n in range(11):
    JOBS.append(("nsa", _n, 0, 8))
SW0 = len(JOBS)
for _n in range(6):
    JOBS.append(("swa", _n, 0, 8))
GS = 3
NGA = 8
_gates = [("gate", _i, 0, 8) for _i in list(range(3 * GS, 3 * KC)) + list(range(3 * GS))]
JOBS += _gates[:NGA]
CMP0 = len(JOBS)
for _n in range(8):
    JOBS.append(("cmp", _n // 4, _n % 4, 4))
CMP1 = len(JOBS)
NGG = 3
JOBS += _gates[NGA:3 * (KC - GS)]
GC0 = len(JOBS)
JOBS += _gates[3 * (KC - GS):]
MERGE0 = len(JOBS)
for _d in range(KC):
    for _b in range(3):
        JOBS.append(("branch", 3 * _d + _b, 0, 4))
OUT0 = len(JOBS)
for _n in range(KC):
    JOBS.append(("out", _n, 0, 8))
FF0 = len(JOBS)
for _f in range(NF):
    JOBS.append(("ffg", _f, 0, 8))
    JOBS.append(("ffu", _f, 0, 8))
DN0 = len(JOBS)
DPARTS = [6, 6, 5, 5]
for _d in range(KC):
    for _q in range(4):
        JOBS.append(("down", _d, _q, DPARTS[_q]))
NJ = len(JOBS)
NRAW, NSPL = 4, 2
POOL_HI = [n for n in range(NS0, MERGE0) if not CMP0 <= n < CMP1 + NGG]
SPILLED = [n for n in range(SW0, GC0) if JOBS[n][0] != "cmp"]
NSTAGE = 2
LOADS = [2 if (j[0] in ("nsa", "swa") and j[1] < 4) else 1 for j in JOBS]


def is_cmp(n):
    return JOBS[n][0] == "cmp"


def group_of(n):
    return sum(not is_cmp(m) for m in range(n))


def width_of(n):
    return 8 if is_cmp(n) else JOBS[n][3]


def loaded_value(n):
    return 16 * sum(LOADS[m] for m in range(n % NRAW, n + 1, NRAW))


FILL = []
PT_UP = len(FILL); FILL += [3, 3, 3, 3, 8]
PT_CP = []
for _cp in range(4):
    PT_CP.append(len(FILL)); FILL += [5 if _cp == 0 else 1, 5, 3] + [2, 2] * 5 + [1, 2, 1, 2, 4]
_left = 8 * (CMP0 - NS0) - sum(FILL)
assert _left >= 0, _left
PT_GN = len(FILL); FILL += [3, _left - 3, 16, 16, 8, 8 * (NGG - 1)]
PT_NSA = len(FILL); FILL += [2] * 34
_ends = np.cumsum([j[3] for j in JOBS[NS0:MERGE0]])
_rest = _ends[-1] - sum(FILL)
_rest -= 8
PT_SWA = len(FILL); FILL += [_rest // 18] * 18
FILL[-1] += _rest - 18 * (_rest // 18)
PT_SPLIT = len(FILL); FILL += [8]
DONE = []
_k = 0
for _f in FILL:
    _k += _f
    DONE.append(NS0 + int(np.sum(_ends <= _k)))
assert DONE[-1] == MERGE0


def build(nc, x, w_in, w_branch, w_out, w_gate, w_up, w_down, w2, a2, g2, ck1, ck2, cv1, cv2, sinks, rel_bias,
          par1, par2, con, hot, out):
    base = 16512

    class Region:
        def __init__(self, at):
            self.at = at

        def take(self, name, shape, dt=F32):
            n = (4 * int(np.prod(shape[1:])) + 31) // 32 * 32
            t = nc.alloc_sbuf_tensor_at(name, list(shape), dt, offset=self.at)
            self.at += n
            return t

    per = Region(base)
    CONP = per.take("CONP", [P, NCONP])
    PARC = per.take("PARC", [P, NPAR1 + NPAR2])
    MISC = per.take("MISC", [P, 96])
    RINV = per.take("RINV", [P, T])
    SQ = per.take("SQ", [P, 2, T])
    SSUM = per.take("SSUM", [P, T])
    WRAW = per.take("WRAW", [P, NRAW, 8, P])
    WHI = per.take("WHI", [P, NSPL, 8, P], F32R)
    WLO = per.take("WLO", [P, NSPL, 8, P], F32R)
    HHI = per.take("HHI", [P, KC, T], F32R)
    HLO = per.take("HLO", [P, KC, T], F32R)
    Z = per.at
    KB = 1024

    def at(name, kb, shape, dt=F32):
        return Region(Z + int(kb * KB)).take(name, shape, dt)

    RW = at("RW", 0, [P, 14, T])
    CUM = at("CUM", 28, [P, 4, T])
    AA = at("AA", 36, [P, 4, T])
    KK = at("KK", 44, [P, 4, T])
    AR = at("AR", 52, [P, 4, 2, P])
    BK = at("BK", 56, [P, 4, 2, P])
    BKT = at("BKT", 60, [P, 2, 4, P])
    SV = at("SV", 64, [P, 2, BW])
    G = at("G", 68, [P, 2, NH, P])
    ABD = at("ABD", 76, [P, NH, P])
    E1 = at("E1", 76, [P, 4, P])
    E2 = at("E2", 78, [P, 4, P])
    AM = at("AM", 80, [P, NH, P])
    XC = at("XC", 84, [P, NH, C])
    XTC = at("XTC", 86, [P, NH, C])
    UC = at("UC", 88, [P, NH, C])
    UBD = at("UBD", 90, [P, NH, P])
    XTBD = at("XTBD", 94, [P, NH, P])
    T1 = at("T1", 98, [P, NH, C])
    ST = at("ST", 100, [P, 2, 4, C])
    MASK = at("MASK", 102, [P, NCON - NCONP])
    WA = at("WA", 108.5, [P, BW])
    PSH = at("PSH", 52, [P, 2, T + 1])
    DSH = at("DSH", 57, [P, T])
    TMP = at("TMP", 60, [P, 4, T])
    XTOK0 = at("XTOK0", 76, [P, 4, D])
    PRAW = at("PRAW", 52, [P, 2, P])
    NQ = at("NQ", 110.5, [P, 10, T])
    GL = at("GL", 130.5, [P, T])
    SELT = [at("SELT0", 130.5, [NH, 4, P]), at("SELT1", 58, [NH, 4, P])]
    O = at("O", 0, [P, 3, 4, T])
    VT = at("VT", 24, [P, 3, 4, P])
    SWQ = at("SWQ", 30, [P, 6, T])
    TBS = at("TBS", 42, [P, NH, 256])
    EB = at("EB", 50, [P, 2, 2, T])
    PTB = at("PTB", 58, [P, 2, 2, T])
    OTK = at("OTK", 66, [P, 2, BW])
    OTS = at("OTS", 70, [P, 2, BW])
    TB = at("TB", 74, [P, NH, T])
    GATES = at("GATES", 90, [P, 15, T])
    XHI = at("XHI", 90, [P, 2, 16, 2 * NCMP], F32R)
    XLO = at("XLO", 98, [P, 2, 16, 2 * NCMP], F32R)
    XF = at("XF", 52, [P, 16, 2 * NCMP])
    small = Region(Z + int(118.5 * KB))
    HGT = small.take("HGT", [P, 4, 2 * NCMP])
    KCT = small.take("KCT", [P, NCMP])
    VCT = small.take("VCT", [32, 2, C])
    GLT = small.take("GLT", [P, 4, 3 * NH])
    CW2 = small.take("CW2", [P, 2, 2, C])
    ECB = small.take("ECB", [P, 2, 32])
    HG = at("HG", 68, [2 * NCMP, 2, CH])
    HT = at("HT", 70, [2 * NCMP, 2, CH])
    PTC = at("PTC", 108.5, [32, 2, P])
    assert small.at <= Z + int(122.5 * KB)
    OHI = at("OHI", 24, [P, 3, 4, T], F32R)
    OLO = at("OLO", 48, [P, 3, 4, T], F32R)
    MHI = at("MHI", 0, [P, KC, T], F32R)
    MLO = at("MLO", 72, [P, KC, T], F32R)
    MT = at("MT", 122, [P, 2, T])
    DSH2 = at("DSH2", 126, [P, 2, T])
    XTOK = at("XTOK", 24, [P, 4, D])
    OT = at("OT", 40, [P, KC, T])
    X1 = at("X1", 116, [P, KC, T])
    DHI = at("DHI", 0, [P, NF, T], F32R)
    DLO = at("DLO", 44, [P, NF, T], F32R)
    FT = at("FT", 88, [P, 6, T])
    OF = at("OF", 100, [P, 2, T])
    OTOK = Region(Z - 32 * KB).take("OTOK", [P, 4, D])
    X1TOK = Region(Z - 16 * KB).take("X1TOK", [P, 4, D])
    HOT = at("HOT", 24, [33, 1024])
    TBL = at("TBL", 28, [33, 16])
    VR = at("VR", 29, [8, 1024])
    SNK = MISC[:, 0:8]
    EPSC = MISC[:, 8:10]
    PCS = MISC[:, 10:18]
    STAT = MISC[:, 18:42].rearrange("p (a b) -> p a b", b=12)
    STAT2 = STAT[:, :, 6:9]
    RTOK = MISC[:, 66:70]
    STATS = MISC[:, 42:66].rearrange("p (a b) -> p a b", b=12)

    assert Z + 132.9 * KB <= 229344, (Z + 132.9 * KB)

    ident, bones, ones = CONP[:, 0:128], CONP[:, 128:256], CONP[:, 256:384]

    def mask(name, n=128):
        c = CON[name] - NCONP
        return MASK[:, c:c + n]

    def par(name, i):
        return PARC[:, PAR[name] + i:PAR[name] + i + 1]

    bias_rows = nc.dram_tensor("bias_rows", (8, 1024), F32, kind="Internal").ap()

    spilled = nc.dram_tensor("spilled", (len(SPILLED), P, T), F32, kind="Internal").ap()

    def stage(n):
        e = SPILLED.index(n)
        return SQ[:, e % NSTAGE, :]

    psum = [nc.alloc_psum_tensor(f"ps{n}", [P, T], F32) for n in range(8)]
    DB, R = psum[0:2], psum[2:8]
    DB4 = [DB[0], DB[1], R[0], R[1]]

    sem = lambda name: nc.alloc_semaphore(name)
    con_in, x_in, par_in, wsmall_in, hot_in = sem("con_in"), sem("x_in"), sem("par_in"), sem("wsmall_in"), sem("hot_in")
    tb_in, tbs_in, g2_in, cw2_in, rows_out = sem("tb_in"), sem("tbs_in"), sem("g2_in"), sem("cw2_in"), sem("rows_out")
    w_loaded = [sem(f"w_loaded{s}") for s in range(NRAW)]
    spill_out = [sem(f"spill_out{e}") for e in range(NSTAGE)]
    swq_in, gates_in = sem("swq_in"), [sem(f"gates_in{s}") for s in range(2)]
    w_hi, w_lo, dense_done, dense_evac = sem("w_hi"), sem("w_lo"), sem("dense_done"), sem("dense_evac")
    prow_T, prow_ok, rel_mm, rel_ok, rel_tbl = sem("prow_T"), sem("prow_ok"), sem("rel_mm"), sem("rel_ok"), sem("rel_tbl")
    rel_in, sc_used = sem("rel_in"), sem("sc_used")
    xT_done, xsq_ok, xlo_ok, xsum_ok = sem("xT_done"), sem("xsq_ok"), sem("xlo_ok"), sem("xsum_ok")
    norm_ss, norm_std, norm_rinv = sem("norm_ss"), sem("norm_std"), sem("norm_rinv")
    mixed_ok, tanh_ok, eps_ok = sem("mixed_ok"), sem("tanh_ok"), sem("eps_ok")
    zmm_done, sig_ok = sem("zmm_done"), sem("sig_ok")
    kk_raw, kk_sq, kk_ss, kk_std, kk_rinv, kk_bc, kk_ok = (sem(s) for s in (
        "kk_raw", "kk_sq", "kk_ss", "kk_std", "kk_rinv", "kk_bc", "kk_ok"))
    selt_in, xtr_T, xtc_ok = sem("selt_in"), sem("xtr_T"), sem("xtc_ok")
    cum_ok = sem("cum_ok")
    exp_ok, arbk_ok, ag_mm, bkend_ok, vt_T, vt_ok, bkt_T, bkt_ok = (sem(s) for s in (
        "exp_ok", "arbk_ok", "ag_mm", "bkend_ok", "vt_T", "vt_ok", "bkt_T", "bkt_ok"))
    ag_ok, x2t_ok, x2_mm, x2_ok, am_ok = (sem(s) for s in ("ag_ok", "x2t_ok", "x2_mm", "x2_ok", "am_ok"))
    u_mm, uc_ok, ubd_ok, xa_mm, xt_ok, xtbd_ok = (sem(s) for s in ("u_mm", "uc_ok", "ubd_ok", "xa_mm", "xt_ok", "xtbd_ok"))
    svz_ok, t1_mm, t1_dve, t1_act, sa_mm, sa_dve, sa_act = (sem(s) for s in (
        "svz_ok", "t1_mm", "t1_dve", "t1_act", "sa_mm", "sa_dve", "sa_act"))
    ys_mm, y_ok, st_ok = sem("ys_mm"), sem("y_ok"), sem("st_ok")
    gn_mean, gn_c, gn_sq, gn_var, gn_std, gn_bp, gn_bmm, gn_b, gn_rinv, gn_bc, gn_n, gn_aff, gn_ok = (sem(s) for s in (
        "gn_mean", "gn_c", "gn_sq", "gn_var", "gn_std", "gn_bp", "gn_bmm", "gn_b", "gn_rinv", "gn_bc", "gn_n", "gn_aff", "gn_ok"))
    vtok_T, vtok_ok, gl_ok, gl_T, glt_ok = (sem(s) for s in ("vtok_T", "vtok_ok", "gl_ok", "gl_T", "glt_ok"))
    xsplit_ok, cmp_read, hg_u, hg_t, hg_ok, kv_mm, kv_ok = (sem(s) for s in (
        "xsplit_ok", "cmp_read", "hg_u", "hg_t", "hg_ok", "kv_mm", "kv_ok"))
    qk_mm, s_used, p_exp, p_T, pts_ok, ptw_ok, pv_mm, o_ok, o_T, oT_ok = (sem(s) for s in (
        "qk_mm", "s_used", "p_exp", "p_T", "pts_ok", "ptw_ok", "pv_mm", "o_ok", "o_T", "oT_ok"))
    sq_mm, ssw_used, sp_exp, sp_T, spt_ok, spv_mm, so_ok, so_T, soT_ok = (sem(s) for s in (
        "sq_mm", "ssw_used", "sp_exp", "sp_T", "spt_ok", "spv_mm", "so_ok", "so_T", "soT_ok"))
    ohi_ok, olo_ok, gsig_ok, mt_ok, mhi_ok, mlo_ok = (sem(s) for s in (
        "ohi_ok", "olo_ok", "gsig_ok", "mt_ok", "mhi_ok", "mlo_ok"))
    xtok_in, x1T, x1T_ok, out_sq, out_sum = (sem(s) for s in (
        "xtok_in", "x1T", "x1T_ok", "out_sq", "out_sum"))
    o_scaled, x1_ok, h2hi_ok, h2lo_ok, x1_sq, x1_ss = (sem(s) for s in (
        "o_scaled", "x1_ok", "h2hi_ok", "h2lo_ok", "x1_sq", "x1_ss"))
    ff_gate, ff_sig, ff_x, ff_hid, ff_hi, ff_lo = (sem(s) for s in (
        "ff_gate", "ff_sig", "ff_x", "ff_hid", "ff_hi", "ff_lo"))
    dn_sq, dn_sum, dn_gain, dn_T, tok_act, fin_ok, out_stored = (sem(s) for s in (
        "dn_sq", "dn_sum", "dn_gain", "dn_T", "tok_act", "fin_ok", "out_stored"))

    def chunked(w, c0, n=P):
        return w.rearrange("(k p) n -> p k n", p=P)[:, :, c0:c0 + n]

    def job_sources(n):
        kind, i, part, _ = JOBS[n]
        full = slice(0, CH if kind == "cmp" else P)
        if kind in ("nsa", "swa") and i < 4:
            c = (NSA0 if kind == "nsa" else SWA0) + HD * i
            return [(slice(0, HD), chunked(w_in, c, HD)), (slice(HD, P), chunked(w_in, c + 4 * HD, HD))]
        if kind == "rwkv":
            return [(full, chunked(w_in, P * i))]
        if kind == "nsa":
            return [(full, chunked(w_in, NSA0 + P * i))]
        if kind == "swa":
            return [(full, chunked(w_in, SWA0 + P * i))]
        if kind == "gate":
            return [(full, chunked(w_in, GATE0 + (i % 3) * D + P * (i // 3)))]
        if kind == "cmp":
            return [(full, chunked((ck1, cv1)[i][part * 4 * P:(part + 1) * 4 * P, :], 0, CH))]
        if kind == "branch":
            return [(full, chunked(w_branch[i % 3], P * (i // 3)))]
        if kind == "out":
            return [(full, chunked(w_out, P * i))]
        raise ValueError(kind)

    def spill_sem(n):
        return spill_out[SPILLED.index(n) % NSTAGE]

    def spilled_before(eng, n):
        jobs = [m for m in SPILLED if m < n]
        for s in spill_out:
            mine = [m for m in jobs if spill_sem(m) is s]
            if mine:
                eng.wait_ge(s, 16 * len(mine))

    def raw_of(n):
        slot = WRAW[:, n % NRAW, 0:width_of(n), :]
        return slot.rearrange("p k n -> p (k n)").rearrange("p (k n) -> p k n", n=CH) if is_cmp(n) else slot

    class Chain:
        def __init__(self, eng, name):
            self.eng, self.sem, self.n = eng, nc.alloc_semaphore(name), 0

        def do(self, ins):
            self.n += 1
            ins.then_inc(self.sem, 1)

        def link(self, ins):
            self.do(ins)
            self.eng.wait_ge(self.sem, self.n)

        def settle(self):
            self.eng.wait_ge(self.sem, self.n)

    block = nc.Block()
    with block:
        @block.sync
        def _(sp):
            for c in range(2):
                sp.dma_start(XTOK0[:, :, 512 * c:512 * c + 512], x.rearrange("(t p) d -> p t d", p=P)[:, :, 512 * c:512 * c + 512])\
                    .then_inc((x_in, xtok_in)[c], 16)
            for n in range(FF0):
                if n < 2:
                    sp.wait_ge((x_in, xtok_in)[n], 16)
                if n - 4 in SPILLED:
                    sp.wait_ge(dense_evac, group_of(n - 4) + 1)
                    sp.dma_start(spilled[SPILLED.index(n - 4)], stage(n - 4)).then_inc(spill_sem(n - 4), 16)
                if n == GC0 + 4:
                    sp.wait_ge(gn_ok, 4)
                    spilled_before(sp, GC0)
                    sp.dma_start(SWQ[:, :, :], spilled[0:6].rearrange("b p t -> p b t")).then_inc(swq_in, 16)
                for d in range(GS, KC):
                    if n == MERGE0 + max(1, 3 * (d - 2)):
                        sp.wait_ge(pv_mm, 32)
                        sp.wait_ge(s_used, 32)
                        if d >= 5:
                            sp.wait_ge(mt_ok, d - 4)
                        spilled_before(sp, GC0)
                        at0, e0 = 3 * d % 15, 6 + 3 * (d - GS)
                        sp.dma_start(GATES[:, at0:at0 + 3, :], spilled[e0:e0 + 3].rearrange("b p t -> p b t"))\
                            .then_inc(gates_in[(d - GS) % 2], 16)
                if n >= NRAW:
                    sp.wait_ge(w_lo, n - NRAW + 1)
                for cols, src in job_sources(n):
                    sp.dma_start(raw_of(n)[:, :, cols], src).then_inc(w_loaded[n % NRAW], 16)
                if n == OUT0 + 3:
                    sp.wait_ge(dense_done, OUT0)
                    sp.dma_start(XTOK[:, :, :], x.rearrange("(t p) d -> p t d", p=P)).then_inc(xtok_in, 16)
            wg, wu = (w.rearrange("(k p) n -> p k n", p=P) for w in (w_gate, w_up))
            with sp.Fori(0, NF // 2) as i:
                for u in range(4):
                    n = FF0 + u
                    sp.wait_ge(w_lo, i * 4 + (n - NRAW + 1))
                    sp.dma_start(WRAW[:, n % NRAW, :, :],
                                 (wg, wu)[u % 2][:, :, bass.ds(i * (2 * P) + P * (u // 2), P)])\
                        .then_inc(w_loaded[n % NRAW], 16)
            wd = w_down.rearrange("(k p) n -> p k n", p=P)
            with sp.Fori(0, KC) as i:
                k0 = 0
                for q in range(4):
                    n = DN0 + q
                    sp.wait_ge(w_lo, i * 4 + (n - NRAW + 1))
                    sp.dma_start(WRAW[:, n % NRAW, 0:DPARTS[q], :],
                                 wd[:, k0:k0 + DPARTS[q], bass.ds(i * P, P)]).then_inc(w_loaded[n % NRAW], 16)
                    k0 += DPARTS[q]
            for n in range(8):
                sp.wait_ge(fin_ok, n + 1)
                cols = slice(512 * (n // 4), 512 * (n // 4) + 512)
                sp.dma_start(out.rearrange("(t p) d -> p t d", p=P)[:, n % 4, cols], OTOK[:, n % 4, cols])\
                    .then_inc(out_stored, 16)
            sp.wait_ge(out_stored, 128)

        @block.gpsimd
        def _(pool):
            pool.memset(TBL[:, :], NEG).then_inc(rel_tbl, 1)
            pool.wait_ge(rel_tbl, 1)
            pool.dma_start(TBL[0:32, :], rel_bias).then_inc(rel_in, 16)

            def lo_part(n, chunks):
                return pool.tensor_tensor(WLO[:, n % NSPL, 0:chunks, :], WRAW[:, n % NRAW, 0:chunks, :],
                                          WHI[:, n % NSPL, 0:chunks, :].bitcast(F32), ALU.subtract)

            for n in range(FF0):
                if n in POOL_HI:
                    pool.wait_ge(w_loaded[n % NRAW], loaded_value(n))
                    pool.wait_ge(dense_done, n - NSPL + 1)
                    pool.tensor_copy(WHI[:, n % NSPL, 0:width_of(n), :],
                                     WRAW[:, n % NRAW, 0:width_of(n), :]).then_inc(w_hi, 1)
                pool.wait_ge(w_hi, n + 1)
                lo_part(n, width_of(n)).then_inc(w_lo, 1)
            for u in range(4):
                if u == 2:
                    for k in range(KC):
                        pool.wait_ge(o_scaled, k + 1)
                        pool.tensor_tensor(X1[:, k, :], X1[:, k, :], OT[:, k, :], ALU.add).then_inc(x1_ok, 1)
                pool.wait_ge(w_hi, FF0 + u + 1)
                lo_part(FF0 + u, 8).then_inc(w_lo, 1)
            with pool.Fori(1, NF // 2) as i:
                for u in range(4):
                    pool.wait_ge(w_hi, i * 4 + (FF0 + u + 1))
                    lo_part(FF0 + u, 8).then_inc(w_lo, 1)
            with pool.Fori(0, KC) as i:
                for q in range(4):
                    pool.wait_ge(w_hi, i * 4 + (DN0 + q + 1))
                    lo_part(DN0 + q, DPARTS[q]).then_inc(w_lo, 1)

        @block.scalar
        def _(act):
            act.dma_start(CONP[:, :], con[:, 0:NCONP]).then_inc(con_in, 16)
            act.dma_start(PRAW[0:NPAR1, 0, :], par1).then_inc(par_in, 16)
            act.dma_start(PRAW[0:NPAR2, 1, :], par2).then_inc(par_in, 16)
            act.wait_ge(eps_ok, 1)
            act.activation(MISC[:, 70:72], EPSC, ACT.Square)

            def hi_part(n):
                act.wait_ge(w_loaded[n % NRAW], loaded_value(n))
                if n >= NSPL:
                    act.wait_ge(dense_done, n - NSPL + 1)
                if n in (CMP0, MERGE0):
                    act.wait_ge(w_hi, n)
                act.activation(WHI[:, n % NSPL, 0:width_of(n), :], WRAW[:, n % NRAW, 0:width_of(n), :],
                               ACT.Copy).then_inc(w_hi, 1)

            act.wait_ge(prow_ok, 2)
            for k in range(KC):
                act.wait_ge(xT_done, k + 1)
                act.activation(HHI[:, k, :], R[k % 4][:, :], ACT.Identity, scale=par("g_pre_mix", k))
                if k >= 2:
                    act.wait_ge(xsum_ok, k - 1)
                act.activation(SQ[:, k % 2, :], R[k % 4][:, :], ACT.Square).then_inc(xsq_ok, 1)
                if k == 3:
                    hi_part(0)
                    act.dma_start(MASK[:, :], con[:, NCONP:NCON]).then_inc(hot_in, 16)
                    act.dma_start(WA[0:64, :], w2).then_inc(wsmall_in, 16)
                    act.dma_start(WA[64:128, :], a2).then_inc(wsmall_in, 16)
                    selt = con[0:NH, CON["selT"]:CON["selT"] + 4 * P].rearrange("h (m p) -> h m p", m=4)
                    act.dma_start(SELT[0][:, :, :], selt).then_inc(selt_in, 16)
                    act.dma_start(HOT[:, :], hot).then_inc(hot_in, 16)
                    act.dma_start(SNK, bass.AP(sinks.tensor, 0, [[0, P], [1, NH]])).then_inc(hot_in, 16)
            hi_part(1)
            act.wait_ge(norm_ss, 1)
            act.wait_ge(eps_ok, 1)
            act.activation(SQ[:, 0, :], R[4][:, :], ACT.Sqrt, scale=1.0 / D, bias=EPSC[:, 0:1]).then_inc(norm_std, 1)
            for n in range(2, NS0):
                hi_part(n)
                if n == 5:
                    act.wait_ge(rel_ok, 1)
                    act.dma_start(bias_rows, VR[:, :]).then_inc(rows_out, 16)
                if n == 10:
                    for m in range(4):
                        act.wait_ge(kk_raw, m + 1)
                        act.activation(TMP[:, m, :], KK[:, m, :], ACT.Square).then_inc(kk_sq, 1)
                if n == 12:
                    act.wait_ge(kk_ss, 1)
                    act.activation(SSUM[0:NH, :], R[5][0:NH, :], ACT.Sqrt).then_inc(kk_std, 1)
            act.wait_ge(mixed_ok, 13)
            act.activation(RW[0:64, 12, :], RW[0:64, 12, :], ACT.Tanh).then_inc(tanh_ok, 1)
            act.wait_ge(mixed_ok, 14)
            act.activation(RW[:, 13, :], RW[:, 13, :], ACT.Sigmoid).then_inc(tanh_ok, 1)
            act.wait_ge(rows_out, 16)
            for m in range(4):
                act.wait_ge(zmm_done, m + 1)
                act.activation(CUM[:, m, :], R[(2 * m) % 6][:, :], ACT.Sigmoid, bias=par("w0", m)).then_inc(sig_ok, 1)
                act.activation(AA[:, m, :], R[(2 * m + 1) % 6][:, :], ACT.Sigmoid, bias=par("a0", m)).then_inc(sig_ok, 1)
            act.wait_ge(zmm_done, 4)
            act.dma_start(WA[:, :], g2).then_inc(g2_in, 16)
            def chunk_exps(cp):
                at0 = slice(cp * P, (cp + 1) * P)
                act.activation(E1[:, :, :], CUM[:, :, at0], ACT.Exp).then_inc(exp_ok, 1)
                act.activation(E2[:, :, :], CUM[:, :, at0], ACT.Exp, scale=-1.0).then_inc(exp_ok, 1)

            act.wait_ge(cum_ok, 4)
            act.wait_ge(st_ok, 1)
            chunk_exps(0)
            for cp in range(4):
                act.wait_ge(vt_T, cp + 1)
                if cp:
                    act.wait_ge(ys_mm, 2 * cp)
                for c in range(2):
                    act.activation(SV[64:128, c, :], R[c][64:128, :], ACT.Copy).then_inc(vt_ok, 1)
                for lv in range(5):
                    g = 5 * cp + lv
                    if lv == 0:
                        act.wait_ge(bkt_T, cp + 1)
                        for c in range(2):
                            act.activation(BKT[:, c, :, :], R[4 + c][:, :].rearrange("p (m n) -> p m n", m=4),
                                           ACT.Copy).then_inc(bkt_ok, 1)
                    if lv < 3:
                        act.wait_ge(xtr_T, 4 * cp + lv + 1)
                        for h in range(2):
                            act.activation(XTBD[64 * h:64 * h + 64, :, 64 * h:64 * h + 64],
                                           R[3 + h][0:64, :].rearrange("p (a b) -> p a b", a=NH),
                                           ACT.Copy).then_inc(xtbd_ok, 1)
                    if lv == 4:
                        act.wait_ge(uc_ok, g + 1)
                        for h in range(2):
                            act.activation(UBD[64 * h:64 * h + 64, :, 64 * h:64 * h + 64], UC[64 * h:64 * h + 64, :, :],
                                           ACT.Copy).then_inc(ubd_ok, 1)
                if cp < 3:
                    act.wait_ge(x2t_ok, cp + 1)
                    act.wait_ge(am_ok, 5 * cp + 5)
                    chunk_exps(cp + 1)
                for c in range(2):
                    g = 2 * cp + c
                    p = slice(64 * c, 64 * c + 64)
                    act.wait_ge(t1_mm, g + 1)
                    act.activation(T1[p, 4:8, :], R[1][p, 0:256].rearrange("p (a b) -> p a b", a=4),
                                   ACT.Copy).then_inc(t1_act, 1)
                    act.wait_ge(sa_mm, g + 1)
                    act.activation(SV[0:64, c, 256:512], R[5][0:64, 0:256], ACT.Copy).then_inc(sa_act, 1)
                    act.wait_ge(ys_mm, g + 1)
                    t0 = cp * P + c * C
                    for q in range(2):
                        act.activation(KK[64 * q:64 * q + 64, :, t0:t0 + C],
                                       R[3 + q][64 * q:64 * q + 64, 0:256].rearrange("p (a b) -> p a b", a=4),
                                       ACT.Copy).then_inc(y_ok, 1)
            act.wait_ge(ys_mm, 8)
            act.wait_ge(st_ok, 9)
            rows = bias_rows.tensor
            act.dma_start(TB[:, :, :], bass.AP(rows, 0, [[1, P], [1024, NH], [1, T]])).then_inc(tb_in, 16)
            hi_part(CMP0)
            hi_part(CMP0 + 1)
            for m in range(4):
                act.wait_ge(gn_c, m + 1)
                act.activation(KK[:, m, :], TMP[:, m, :], ACT.Square).then_inc(gn_sq, 1)
            act.dma_start(SELT[1][:, :, :], selt).then_inc(selt_in, 16)
            act.wait_ge(xsplit_ok, 2)
            for kv, w in enumerate((ck2, cv2)):
                act.dma_start(CW2[:, kv, :, :], w.rearrange("(h p) d -> p h d", p=P)).then_inc(cw2_in, 16)
            for n in range(CMP0 + 2, CMP0 + 6):
                hi_part(n)

            def hidden_tanh(kv):
                act.wait_ge(hg_u, kv + 1)
                act.activation(HT[:, kv, :], HT[:, kv, :], ACT.Tanh, scale=0.7978845608028654).then_inc(hg_t, 1)

            act.wait_ge(gn_var, 1)
            act.activation(SSUM[0:NH, :], R[0][0:NH, :], ACT.Sqrt, scale=1.0 / HD, bias=EPSC[0:NH, 1:2]).then_inc(gn_std, 1)
            hidden_tanh(0)
            for n in range(CMP0 + 6, CMP1 + 2):
                hi_part(n)
            for m in range(4):
                act.wait_ge(gn_n, m + 1)
                act.activation(TMP[:, m, :], TMP[:, m, :], ACT.Identity, scale=par("ln_w", m),
                               bias=par("ln_b", m)).then_inc(gn_aff, 1)

            hidden_tanh(1)
            for n in range(CMP1 + 2, CMP1 + NGG):
                hi_part(n)
            act.wait_ge(gn_ok, 4)
            act.dma_start(TBS[:, :, :], bass.AP(rows, 640, [[1, P], [1024, NH], [1, 256]])).then_inc(tbs_in, 16)
            act.wait_ge(dense_evac, group_of(NS0 + 10) + 1)
            act.activation(GL[:, :], GL[:, :], ACT.Sigmoid).then_inc(gl_ok, 1)
            act.wait_ge(vtok_T, 1)
            for b in range(2):
                act.activation(VT[:, b, :, :], R[2 + b][:, :].rearrange("p (a b) -> p a b", a=4),
                               ACT.Copy).then_inc(vtok_ok, 1)

            def nsa_exp(u):
                i, h = divmod(u, NH)
                w = P * (i + 1)
                act.wait_ge(s_used, u + 1)
                act.activation(ECB[:, u % 2, 0:8 * i + 7], ECB[:, u % 2, 0:8 * i + 7], ACT.Exp,
                               bias=STAT[:, u % 2, 0:1], accum_out=STAT[:, u % 2, 3:4])
                for b in range(2):
                    last = act.activation(EB[:, u % 2, b, 0:w], EB[:, u % 2, b, 0:w], ACT.Exp,
                                          bias=STAT[:, u % 2, 1 + b:2 + b], accum_out=STAT[:, u % 2, 4 + b:5 + b])
                last.then_inc(p_exp, 1)

            def nsa_ptw(u):
                w = P * (u // NH + 1)
                act.wait_ge(p_T, u + 1)
                if u >= 2:
                    act.wait_ge(pv_mm, u - 1)
                act.activation(PTB[:, u % 2, 1, 0:w], R[4][:, 0:w], ACT.Copy).then_inc(ptw_ok, 1)

            def nsa_oT(i):
                act.wait_ge(o_T, i + 1)
                act.activation(O[:, 1, :, i * P:(i + 1) * P], R[3][:, :].rearrange("p (a b) -> p a b", a=4),
                               ACT.Copy).then_inc(oT_ok, 1)

            for u in range(34):
                if u < 32:
                    nsa_exp(u)
                if 1 <= u < 33:
                    nsa_ptw(u - 1)
                if u >= 3 and (u - 3) % NH == NH - 1:
                    nsa_oT((u - 3) // NH)
            nsa_oT(3)
            act.wait_ge(vtok_T, 2)
            act.activation(VT[:, 2, :, :], R[2][:, :].rearrange("p (a b) -> p a b", a=4), ACT.Copy).then_inc(vtok_ok, 1)

            def swa_exp(v):
                blk = v // 4
                w = WIN if blk == 0 else 2 * WIN
                act.wait_ge(ssw_used, v + 1)
                act.activation(STATS[:, v % 2, 4:6], STATS[:, v % 2, 4:6], ACT.Exp)
                for g in range(2):
                    last = act.activation(EB[:, v % 2, g, 0:w], EB[:, v % 2, g, 0:w], ACT.Exp,
                                          bias=STATS[:, v % 2, g:g + 1], accum_out=STATS[:, v % 2, 2 + g:3 + g])
                last.then_inc(sp_exp, 1)

            def swa_oT(blk):
                act.wait_ge(so_T, blk + 1)
                act.activation(O[:, 2, :, blk * P:(blk + 1) * P], R[2][:, :].rearrange("p (a b) -> p a b", a=4),
                               ACT.Copy).then_inc(soT_ok, 1)

            for v in range(18):
                if v < 16:
                    swa_exp(v)
                if v >= 3 and (v - 3) % 4 == 3:
                    swa_oT((v - 3) // 4)
            swa_oT(3)

            hi_part(MERGE0)
            for b in range(3):
                for m in range(4):
                    if b == 0 and m == 0:
                        act.wait_ge(gn_ok, 4)
                        act.wait_ge(oT_ok, 4)
                        act.wait_ge(so_T, 4)
                        act.wait_ge(soT_ok, 4)
                        act.wait_ge(vtok_ok, 3)
                    act.activation(OHI[:, b, m, :], O[:, b, m, :], ACT.Copy).then_inc(ohi_ok, 1)
            hi_part(MERGE0 + 1)
            act.wait_ge(dense_evac, group_of(MERGE0 - 1) + 1)
            n = MERGE0 + 2
            for d in range(KC):
                if d >= GS:
                    act.wait_ge(gates_in[(d - GS) % 2], 16 * ((d - GS) // 2 + 1))
                for b in range(3):
                    i = 3 * d % 15 + b
                    act.activation(GATES[:, i, :], GATES[:, i, :], ACT.Sigmoid).then_inc(gsig_ok, 1)
                    hi_part(n)
                    n += 1
                act.wait_ge(mt_ok, d + 1)
                act.activation(MHI[:, d, :], MT[:, d % 2, :], ACT.Copy).then_inc(mhi_ok, 1)
            for d in range(KC):
                if n < FF0:
                    hi_part(n)
                    n += 1
                act.wait_ge(dense_evac, group_of(OUT0 + d) + 1)
                if d >= 2:
                    act.wait_ge(out_sum, d - 1)
                act.activation(SQ[:, d % 2, :], OT[:, d, :], ACT.Square).then_inc(out_sq, 1)
            assert n == FF0

            def first_hi(m):
                act.wait_ge(w_loaded[(FF0 + m) % NRAW], loaded_value(FF0 + m))
                act.wait_ge(dense_done, FF0 + m - NSPL + 1)
                act.activation(WHI[:, (FF0 + m) % NSPL, :, :], WRAW[:, (FF0 + m) % NRAW, :, :], ACT.Copy).then_inc(w_hi, 1)

            first_hi(0)
            act.wait_ge(norm_ss, 2)
            act.activation(SQ[:, 0, :], R[4][:, :], ACT.Sqrt, scale=1.0 / D, bias=EPSC[:, 0:1]).then_inc(norm_std, 1)
            first_hi(1)
            act.wait_ge(norm_rinv, 1)
            for k in range(KC):
                act.wait_ge(x1_ok, k + 1)
                act.activation(HHI[:, k, :], X1[:, k, :], ACT.Identity, scale=par("g_pre_ffn", k)).then_inc(h2hi_ok, 1)
                if k >= 2:
                    act.wait_ge(x1_ss, k - 1)
                act.activation(SQ[:, k % 2, :], X1[:, k, :], ACT.Square).then_inc(x1_sq, 1)
            act.wait_ge(norm_ss, 3)
            act.activation(SQ[:, 0, :], R[4][:, :], ACT.Sqrt, scale=1.0 / D, bias=EPSC[:, 0:1]).then_inc(norm_std, 1)

            def hi_loop(n, i, chunks):
                act.wait_ge(w_loaded[n % NRAW], i * 16 + loaded_value(n))
                act.wait_ge(dense_done, i * 4 + (n - NSPL + 1))
                act.activation(WHI[:, n % NSPL, 0:chunks, :], WRAW[:, n % NRAW, 0:chunks, :],
                               ACT.Copy).then_inc(w_hi, 1)

            def ffn_act(f, i):
                act.wait_ge(ff_gate, i * 2 + (f + 1))
                act.activation(FT[:, 3 * (f % 2) + 1, :], FT[:, 3 * (f % 2), :], ACT.Sigmoid).then_inc(ff_sig, 1)
                act.wait_ge(ff_hid, i * 2 + (f + 1))
                act.activation(DHI[:, bass.ds(i * 2 + f, 1), :],
                               FT[:, 3 * (f % 2) + 2, :], ACT.Copy).then_inc(ff_hi, 1)

            with act.Fori(0, NF // 2 - 1) as i:
                hi_loop(FF0 + 2, i, 8)
                hi_loop(FF0 + 3, i, 8)
                ffn_act(0, i)
                hi_loop(FF0 + 4, i, 8)
                hi_loop(FF0 + 5, i, 8)
                ffn_act(1, i)
            i = NF // 2 - 1
            hi_loop(FF0 + 2, i, 8)
            hi_loop(FF0 + 3, i, 8)
            ffn_act(0, i)
            hi_loop(DN0, 0, DPARTS[0])
            ffn_act(1, i)
            hi_loop(DN0 + 1, 0, DPARTS[1])
            act.wait_ge(dense_done, DN0)
            for n in range(0, 8, 2):
                act.wait_ge(x1T, KC + n + 1)
                act.activation(X1TOK[:, n // 2, 0:512], R[2 + n % 4][:, :], ACT.Copy).then_inc(tok_act, 1)
            for q in (2, 3):
                hi_loop(DN0 + q, 0, DPARTS[q])
            act.wait_ge(norm_rinv, 2)

            def square(b, ended, added):
                act.wait_ge(dense_done, ended)
                if added is not None:
                    act.wait_ge(dn_sum, added)
                act.activation(SQ[:, 0, :], DB[b][:, :], ACT.Square).then_inc(dn_sq, 1)

            def token_copy(at0, b, count):
                act.wait_ge(dn_T, count)
                act.activation(OTOK[:, :, at0], R[2 + b][:, :].rearrange("p (t n) -> p t n", t=4), ACT.Copy)                   .then_inc(tok_act, 1)

            def down_act(i, b):
                for q in range(2):
                    hi_loop(DN0 + 4 * b + q, i * 2, DPARTS[q])
                square(1 - b, i * 8 + (4 * b + DN0), None if isinstance(i, int) else i * 2 + (b - 1))
                for q in (2, 3):
                    hi_loop(DN0 + 4 * b + q, i * 2, DPARTS[q])
                token_copy(bass.ds(i * (2 * P) + (b - 1) * P, P), 1 - b, i * 2 + (b + 2))

            down_act(0, 1)
            with act.Fori(1, KC // 2) as i:
                for b in range(2):
                    down_act(i, b)
            square(1, NJ, KC - 1)
            act.wait_ge(norm_ss, 4)
            act.activation(RTOK, R[0][:, 0:4], ACT.Sqrt, scale=1.0 / D, bias=EPSC[:, 0:1]).then_inc(norm_std, 1)
            token_copy(slice((KC - 1) * P, KC * P), 1, KC + 2)

        @block.vector
        def _(dve):
            chain = Chain(dve, "dve_chain")
            link, do = chain.link, chain.do
            state = {"evac": 0}

            def evac_rinv(n, dst):
                dve.wait_ge(dense_done, n + 1)
                return dve.tensor_tensor(dst, DB[group_of(n) % 2][:, :], RINV[:, :], ALU.mult)

            def evac(n):
                kind, i, part, _ = JOBS[n]
                if n in SPILLED and SPILLED.index(n) >= NSTAGE:
                    e = SPILLED.index(n)
                    dve.wait_ge(spill_out[e % NSTAGE], 16 * (e // NSTAGE))
                if kind in ("nsa", "swa") and i < 4:
                    dst = NQ[:, i, :] if kind == "nsa" else stage(n)
                    dve.wait_ge(dense_done, n + 1)
                    ins = dve.scalar_tensor_tensor(out=dst, in0=DB[group_of(n) % 2][:, :], scalar=HD ** -0.5,
                                                   in1=RINV[:, :], op0=ALU.mult, op1=ALU.mult)
                elif kind == "nsa":
                    ins = evac_rinv(n, NQ[:, i, :] if i < 10 else GL[:, :])
                elif kind == "swa":
                    ins = evac_rinv(n, stage(n))
                elif kind == "gate":
                    ins = evac_rinv(n, stage(n) if n in SPILLED else GATES[:, i, :])
                elif kind == "cmp":
                    if part == 3:
                        gelu(n, i)
                    return
                ins.then_inc(dense_evac, 1)

            def gelu(n, kv):
                dve.wait_ge(dense_done, n + 1)
                dve.tensor_copy(HG[:, kv, :], R[5][0:2 * NCMP, 0:CH]).then_inc(cmp_read, 1)
                dve.wait_ge(cmp_read, kv + 1)
                link(dve.tensor_tensor(HT[:, kv, :], HG[:, kv, :], HG[:, kv, :], ALU.mult))
                link(dve.tensor_scalar(HT[:, kv, :], HT[:, kv, :], 0.044715, 1.0, ALU.mult, ALU.add))
                dve.tensor_tensor(HT[:, kv, :], HT[:, kv, :], HG[:, kv, :], ALU.mult).then_inc(hg_u, 1)
                dve.wait_ge(hg_t, kv + 1)
                link(dve.scalar_tensor_tensor(out=HG[:, kv, :], in0=HT[:, kv, :], scalar=1.0, in1=HG[:, kv, :],
                                              op0=ALU.add, op1=ALU.mult))
                dve.tensor_scalar(HG[:, kv, :], HG[:, kv, :], 0.5, None, ALU.mult).then_inc(hg_ok, 1)

            def evacs(point):
                while NS0 + state["evac"] < DONE[point]:
                    n = NS0 + state["evac"]
                    if n == CMP0:
                        chain.settle()
                    evac(n)
                    state["evac"] += 1

            dve.memset(EPSC[:, 0:1], EPS)
            dve.memset(EPSC[:, 1:2], LN_EPS).then_inc(eps_ok, 1)
            dve.wait_ge(con_in, 16)
            dve.wait_ge(prow_T, 1)
            dve.tensor_copy(PARC[:, 0:NPAR1], R[4][:, 0:NPAR1]).then_inc(prow_ok, 1)
            dve.tensor_copy(PARC[:, NPAR1:NPAR1 + NPAR2], R[5][:, 0:NPAR2]).then_inc(prow_ok, 1)
            dve.wait_ge(prow_ok, 2)
            for k in range(KC):
                dve.wait_ge(xsq_ok, k + 1)
                dve.scalar_tensor_tensor(out=HLO[:, k, :], in0=R[k % 4][:, :], scalar=par("g_pre_mix", k),
                                         in1=HHI[:, k, :].bitcast(F32), op0=ALU.mult, op1=ALU.subtract).then_inc(xlo_ok, 1)
                if k == 0:
                    dve.tensor_copy(SSUM[:, :], SQ[:, 0, :]).then_inc(xsum_ok, 1)
                else:
                    dve.wait_ge(xsum_ok, k)
                    dve.tensor_tensor(SSUM[:, :], SSUM[:, :], SQ[:, k % 2, :], ALU.add).then_inc(xsum_ok, 1)
            dve.wait_ge(norm_std, 1)
            link(dve.reciprocal(RINV[:, :], SQ[:, 0, :]))
            dve.wait_ge(prow_T, 1)
            link(dve.memset(PSH[:, :, 0:1], 0.0))
            for n in range(NS0):
                cur = PSH[:, n % 2, 1:T + 1]
                dve.wait_ge(dense_done, n + 1)
                ins = dve.tensor_tensor(cur, DB[n % 2][:, :], RINV[:, :], ALU.mult)
                ins.then_inc(dense_evac, 1)
                dve.wait_ge(dense_evac, n + 1)
                link(dve.tensor_tensor(DSH[:, :], PSH[:, n % 2, 0:T], cur, ALU.subtract))
                dve.scalar_tensor_tensor(out=RW[:, n, :], in0=DSH[:, :], scalar=par("mu", n), in1=cur,
                                         op0=ALU.mult, op1=ALU.add).then_inc(mixed_ok, 1)
                if n == 1:
                    dve.wait_ge(rel_mm, 1)
                    dve.tensor_copy(VR[:, 0:512], R[0][0:8, :])
                    dve.tensor_copy(VR[:, 512:640], R[1][0:8, 0:128])
                    dve.tensor_copy(VR[:, 640:1024], R[2][0:8, 0:384]).then_inc(rel_ok, 1)
                if n == 7:
                    dve.wait_ge(mixed_ok, 8)
                    for m in range(4):
                        dve.tensor_scalar(KK[:, m, :], RW[:, 4 + m, :], par("k_k", m), None, ALU.mult).then_inc(kk_raw, 1)
                if n == 11:
                    dve.wait_ge(kk_std, 1)
                    link(dve.tensor_scalar(SSUM[0:NH, :], SSUM[0:NH, :], 1e-12, None, ALU.max))
                    dve.reciprocal(SSUM[0:NH, :], SSUM[0:NH, :]).then_inc(kk_rinv, 1)
            dve.wait_ge(kk_bc, 1)
            dve.wait_ge(kk_raw, 4)
            for m in range(4):
                dve.scalar_tensor_tensor(out=KK[:, m, :], in0=R[m][:, :], scalar=-1.0, in1=KK[:, m, :],
                                         op0=ALU.mult, op1=ALU.mult).then_inc(kk_ok, 1)
            dve.wait_ge(hot_in, 48)
            for m in range(4):
                if m >= 2:
                    evacs(PT_UP + m)
                dve.wait_ge(sig_ok, 2 * m + 2)
                link(dve.tensor_scalar(CUM[:, m, :], CUM[:, m, :], -float(np.exp(-0.5)), None, ALU.mult))
                dve.tensor_tensor_scan(CUM[:, m, :], mask("reset", T), CUM[:, m, :], 0.0, ALU.mult, ALU.add)\
                   .then_inc(cum_ok, 1)
                do(dve.tensor_scalar(DSH[:, :], AA[:, m, :], 1.0, par("k_a", m), ALU.subtract, ALU.mult))
                if m == 0:
                    dve.wait_ge(kk_ok, 4)
                chain.settle()
                do(dve.scalar_tensor_tensor(out=RW[:, 4 + m, :], in0=DSH[:, :], scalar=1.0, in1=RW[:, 4 + m, :],
                                              op0=ALU.add, op1=ALU.mult))
                link(dve.scalar_tensor_tensor(out=AA[:, m, :], in0=KK[:, m, :], scalar=-1.0, in1=AA[:, m, :],
                                              op0=ALU.mult, op1=ALU.mult))
            evacs(PT_UP + 4)
            link(dve.memset(UBD[:, :, :], 0.0))
            dve.memset(ST[:, :, :, :], 0.0).then_inc(st_ok, 1)

            def two(ap):
                return ap.rearrange("p m (c t) -> p m c t", c=2)

            def scaled_bk(cp):
                at0 = slice(cp * P, (cp + 1) * P)
                dve.wait_ge(exp_ok, 2 * cp + 2)
                if cp:
                    dve.wait_ge(bkt_T, cp)
                do(dve.tensor_tensor(BK[:, :, :, 0:C], two(AA[:, :, at0]), two(E2[:, :, :]), ALU.mult))
                do(dve.tensor_tensor(BK[:, :, :, C:P], two(RW[:, 4:8, at0]), two(E2[:, :, :]), ALU.mult))

            scaled_bk(0)
            for cp in range(4):
                pt = PT_CP[cp]
                s = slice(cp * P, (cp + 1) * P)
                if cp:
                    dve.wait_ge(ys_mm, 2 * cp)
                do(dve.tensor_tensor(AR[:, :, :, C:P], two(RW[:, 0:4, s]), two(E1[:, :, :]), ALU.mult))
                do(dve.tensor_tensor(AR[:, :, :, 1:C], two(KK[:, :, s])[:, :, :, 1:C], two(E1[:, :, :])[:, :, :, 0:C - 1],
                                     ALU.mult))
                dve.tensor_copy(AR[:, :, :, 0:1], two(KK[:, :, s])[:, :, :, 0:1]).then_inc(arbk_ok, 1)
                chain.settle()
                do(dve.tensor_copy(PCS.rearrange("p (m c) -> p m c", c=2).unsqueeze(3), two(E1[:, :, :])[:, :, :, C - 1:C]))
                dve.memset(SV[0:64, :, :], 0.0).then_inc(svz_ok, 1)
                evacs(pt)
                dve.wait_ge(ag_mm, cp + 1)
                chain.settle()
                for c in range(2):
                    half = slice(64 * c, 64 * c + 64)
                    for q in range(2):
                        do(dve.tensor_tensor(
                            ABD[half, 4 * q:4 * q + 4, :].rearrange("p a (c t) -> p a c t", c=2),
                            R[2 + 2 * c + q][0:64, :].rearrange("p (a b) -> p a b", a=4)[:, :, 0:C].unsqueeze(2)
                            .broadcast_to([64, 4, 2, C]),
                            mask("maskA", 3 * C)[0:64, C - C * c:3 * C - C * c].rearrange("p (c t) -> p c t", c=2)
                            .unsqueeze(1).broadcast_to([64, 4, 2, C]), ALU.mult))
                chain.settle()
                if cp:
                    dve.wait_ge(xtbd_ok, 6 * cp)
                link(dve.tensor_tensor(XTBD[:, :, :], ABD[:, :, :], mask("m1").unsqueeze(1).broadcast_to([P, NH, P]), ALU.mult))
                dve.tensor_tensor(XTBD[:, :, :], XTBD[:, :, :], ident.unsqueeze(1).broadcast_to([P, NH, P]), ALU.add)\
                   .then_inc(x2t_ok, 1)
                evacs(pt + 1)

                def am(lv):
                    if lv:
                        dve.wait_ge(u_mm, 5 * cp + lv)
                    dve.tensor_tensor(AM[:, :, :], ABD[:, :, :],
                                      mask(f"m{2 << lv}").unsqueeze(1).broadcast_to([P, NH, P]), ALU.mult).then_inc(am_ok, 1)

                am(0)
                for c in range(2):
                    for q in range(2):
                        ins = dve.tensor_tensor(G[:, c, 4 * q:4 * q + 4, :],
                                                R[2 + 2 * c + q][:, :].rearrange("p (a b) -> p a b", a=4),
                                                mask("maskG").unsqueeze(1).broadcast_to([P, 4, P]), ALU.mult)
                        if c == 1 and q == 1:
                            ins.then_inc(ag_ok, 1)
                        else:
                            do(ins)
                    if c == 0:
                        dve.wait_ge(x2_mm, cp + 1)
                        do(dve.tensor_copy(XC[0:64, :, :], R[0][0:64, :].rearrange("p (a b) -> p a b", a=NH)))
                        dve.tensor_copy(XC[64:128, :, :], R[1][0:64, :].rearrange("p (a b) -> p a b", a=NH)).then_inc(x2_ok, 1)
                chain.settle()
                dve.tensor_tensor(BK[:, :, :, :].rearrange("p m c n -> p (m c) n"),
                                  BK[:, :, :, :].rearrange("p m c n -> p (m c) n"),
                                  PCS.unsqueeze(2).broadcast_to([P, NH, P]), ALU.mult).then_inc(bkend_ok, 1)
                dve.wait_ge(x2_ok, cp + 1)
                evacs(pt + 2)
                for lv in range(5):
                    g = 5 * cp + lv
                    dve.wait_ge(u_mm, g + 1)
                    if g:
                        dve.wait_ge(xa_mm, g)
                    dve.tensor_copy(UC[:, :, :], R[1][:, :].rearrange("p (a b) -> p a b", a=NH)).then_inc(uc_ok, 1)
                    if lv < 4:
                        am(lv + 1)
                    evacs(pt + 3 + 2 * lv)
                    dve.wait_ge(xa_mm, g + 1)
                    if lv:
                        dve.wait_ge(xt_ok, g)
                    if lv < 4:
                        dve.tensor_tensor(XC[:, :, :], XC[:, :, :], R[2][:, :].rearrange("p (a b) -> p a b", a=NH),
                                          ALU.add).then_inc(xt_ok, 1)
                    else:
                        dve.wait_ge(xtc_ok, cp + 1)
                        dve.tensor_tensor(XTC[:, :, :], XTC[:, :, :], R[3][:, :].rearrange("p (a b) -> p a b", a=NH),
                                          ALU.add).then_inc(xt_ok, 1)
                    if lv == 3:
                        dve.wait_ge(xtr_T, 4 * cp + 4)
                        do(dve.tensor_copy(XTC[0:64, :, :], R[3][0:64, :].rearrange("p (a b) -> p a b", a=NH)))
                        dve.tensor_copy(XTC[64:128, :, :], R[4][0:64, :].rearrange("p (a b) -> p a b", a=NH)).then_inc(xtc_ok, 1)
                    evacs(pt + 4 + 2 * lv)
                for c in range(2):
                    g = 2 * cp + c
                    p = slice(64 * c, 64 * c + 64)
                    dve.wait_ge(t1_mm, g + 1)
                    dve.tensor_copy(T1[p, 0:4, :], R[0][p, 0:256].rearrange("p (a b) -> p a b", a=4)).then_inc(t1_dve, 1)
                    dve.wait_ge(st_ok, g + 1)
                    link(dve.tensor_tensor(ST[:, (g + 1) % 2, :, :], ST[:, g % 2, :, :],
                                           PCS.rearrange("p (m c) -> p m c", c=2)[:, :, c:c + 1].broadcast_to([P, 4, C]),
                                           ALU.mult))
                    dve.wait_ge(sa_mm, g + 1)
                    dve.tensor_copy(SV[0:64, c, 0:256], R[2][0:64, 0:256]).then_inc(sa_dve, 1)
                    if c == 0 and cp < 3:
                        scaled_bk(cp + 1)
                    evacs(pt + 13 + 2 * c)
                    evacs(pt + 14 + 2 * c)
                    dve.wait_ge(ys_mm, g + 1)
                    dve.tensor_tensor(ST[:, (g + 1) % 2, :, :], ST[:, (g + 1) % 2, :, :],
                                      R[5][:, 0:256].rearrange("p (a b) -> p a b", a=4), ALU.add).then_inc(st_ok, 1)
                evacs(pt + 17)

            for m in range(4):
                dve.scalar_tensor_tensor(out=CUM[:, m, :], in0=RW[:, m, :], scalar=par("r_k", m), in1=RW[:, 4 + m, :],
                                         op0=ALU.mult, op1=ALU.mult).then_inc(gn_bp, 1)
            evacs(PT_GN)
            dve.wait_ge(y_ok, 16)
            for kv in range(2):
                dve.wait_ge(dense_evac, group_of(NS0 + 10) + 1)
                pe = PARC[:, PAR["pe"] + 32 * kv:PAR["pe"] + 32 * kv + 32]
                for l in range(2):
                    for g in range(2):
                        p = slice(64 * g, 64 * g + 64)
                        src = NQ[p, 4 + kv, :]
                        for half in range(2):
                            v = src[:, 16 * half:16 * half + 16 * NCMP].rearrange("p (c j l) -> p j c l", j=8, l=2)[:, :, :, l]
                            e = pe[p, :].rearrange("p (j l) -> p j l", l=2)[:, 8 * half:8 * half + 8, l:l + 1]
                            do(dve.tensor_tensor(XF[64 * l:64 * l + 64, 8 * half:8 * half + 8, g * NCMP:(g + 1) * NCMP],
                                                 v, e.broadcast_to([64, 8, NCMP]), ALU.add))
                chain.settle()
                link(dve.tensor_copy(XHI[:, kv, :, :], XF[:, :, :]))
                dve.tensor_tensor(XLO[:, kv, :, :], XF[:, :, :], XHI[:, kv, :, :].bitcast(F32), ALU.subtract)\
                   .then_inc(xsplit_ok, 1)
                dve.wait_ge(xsplit_ok, kv + 1)
            for m in range(4):
                dve.wait_ge(gn_mean, m + 1)
                dve.scalar_tensor_tensor(out=TMP[:, m, :], in0=R[m][:, :], scalar=-1.0 / HD, in1=KK[:, m, :],
                                         op0=ALU.mult, op1=ALU.add).then_inc(gn_c, 1)

            def gn_bonus(m):
                dve.wait_ge(gn_bmm, m + 1)
                dve.tensor_tensor(AA[:, m, :], R[4][:, :], RW[:, 8 + m, :], ALU.mult).then_inc(gn_b, 1)

            gn_bonus(0)
            evacs(PT_GN + 1)
            gn_bonus(1)
            evacs(PT_GN + 2)
            dve.wait_ge(gn_std, 1)
            dve.reciprocal(SSUM[0:NH, :], SSUM[0:NH, :]).then_inc(gn_rinv, 1)
            gn_bonus(2)
            dve.wait_ge(gn_c, 4)
            gn_bonus(3)
            for m in range(4):
                dve.wait_ge(gn_bc, m + 1)
                dve.tensor_tensor(TMP[:, m, :], TMP[:, m, :], R[m][:, :], ALU.mult).then_inc(gn_n, 1)
            evacs(PT_GN + 3)
            for m in range(4):
                dve.wait_ge(gn_aff, m + 1)
                dve.wait_ge(gn_b, m + 1)
                link(dve.tensor_tensor(AA[:, m, :], AA[:, m, :], TMP[:, m, :], ALU.add))
                dve.wait_ge(gn_bc, 4 + m + 1)
                dve.tensor_tensor(O[:, 0, m, :], AA[:, m, :], R[m][:, :], ALU.mult).then_inc(gn_ok, 1)
            evacs(PT_GN + 4)
            evacs(PT_GN + 5)
            dve.wait_ge(gl_T, 1)
            dve.tensor_copy(GLT[:, :, :], R[0][:, 0:96].rearrange("p (a b) -> p a b", a=4)).then_inc(glt_ok, 1)
            dve.wait_ge(kv_mm, 1)
            dve.tensor_copy(HGT[:, :, :], R[1][:, 0:256].rearrange("p (a b) -> p a b", a=4)[:, :, 0:2 * NCMP]).then_inc(hg_ok, 1)
            dve.wait_ge(kv_mm, 2)
            dve.tensor_copy(KCT[:, :], R[1][:, 0:NCMP])
            dve.tensor_copy(VCT[0:NCMP, :, :], R[1][0:NCMP, 128:256].rearrange("p (a b) -> p a b", a=2)).then_inc(kv_ok, 1)
            dve.wait_ge(glt_ok, 1)
            dve.wait_ge(tb_in, 16)

            def bias_of(tiles, h, at0, n, step=1):
                full = tiles[:, h, :]
                return bass.AP(full.tensor, full.offset + at0, [list(full.ap[0]), [-step, n]])

            def nsa_scores(u):
                i, h = divmod(u, NH)
                w, nc_ = P * (i + 1), 8 * i + 7
                dve.wait_ge(qk_mm, u + 1)
                if u >= 2:
                    dve.wait_ge(p_T, u - 1)
                st = STAT[:, u % 2, :]
                dve.tensor_tensor_reduce(ECB[:, u % 2, 0:nc_], R[2][:, 0:nc_], bias_of(TB, h, P * (i + 1) - 32, nc_, 16),
                                         1.0, -3e38, ALU.add, ALU.max, st[:, 0:1]).then_inc(sc_used, 1)
                for b in range(2):
                    do(dve.tensor_tensor_reduce(EB[:, u % 2, b, 0:w], R[b][:, 0:w], bias_of(TB, h, w - 1, w),
                                                1.0, -3e38, ALU.add, ALU.max, st[:, 1 + b:2 + b]))
                chain.settle()
                dve.tensor_scalar(st[:, 0:3], st[:, 0:3], -1e25, -1.0, ALU.max, ALU.mult).then_inc(s_used, 1)

            def nsa_pts(u):
                w = P * (u // NH + 1)
                dve.wait_ge(p_T, u + 1)
                if u >= 2:
                    dve.wait_ge(pv_mm, u - 1)
                nc_ = 8 * (u // NH) + 7
                dve.tensor_copy(PTC[0:nc_, u % 2, :], R[2][0:nc_, 384:512])
                dve.tensor_copy(PTB[:, u % 2, 0, 0:w], R[3][:, 0:w]).then_inc(pts_ok, 1)

            def nsa_out(u):
                i, h = divmod(u, NH)
                st = STAT[:, u % 2, :]
                wt = STAT2[:, u % 2, :]
                o = OTK[:, i % 2, HD * h:HD * h + HD]
                dve.wait_ge(pv_mm, u + 1)
                if h == 0 and i >= 2:
                    dve.wait_ge(o_T, i - 1)
                link(dve.tensor_tensor(o, R[5][:, 0:64], wt[:, 0:1].broadcast_to([P, HD]), ALU.mult))
                link(dve.scalar_tensor_tensor(out=o, in0=R[5][:, 64:128], scalar=wt[:, 1:2], in1=o, op0=ALU.mult, op1=ALU.add))
                dve.scalar_tensor_tensor(out=o, in0=R[5][:, 128:192], scalar=wt[:, 2:3], in1=o,
                                         op0=ALU.mult, op1=ALU.add).then_inc(o_ok, 1)

            def nsa_weights(u):
                i, h = divmod(u, NH)
                st = STAT[:, u % 2, :]
                wt = STAT2[:, u % 2, :]
                dve.wait_ge(p_exp, u + 1)
                if u >= 2:
                    dve.wait_ge(o_ok, u - 1)
                link(dve.tensor_scalar(wt, st[:, 3:6], 1e-30, None, ALU.max))
                link(dve.reciprocal(wt, wt))
                link(dve.tensor_tensor(wt, wt, GLT[:, i, h:3 * NH:NH], ALU.mult))

            for u in range(34):
                if u < 32:
                    nsa_scores(u)
                if 1 <= u < 33:
                    nsa_weights(u - 1)
                    nsa_pts(u - 1)
                if u >= 2:
                    nsa_out(u - 2)
                evacs(PT_NSA + u)

            def swa_scores(v):
                blk, j = divmod(v, 4)
                w = WIN if blk == 0 else 2 * WIN
                dve.wait_ge(sq_mm, v + 1)
                if v >= 2:
                    dve.wait_ge(sp_T, v - 1)
                st = STATS[:, v % 2, :]
                for g in range(2):
                    do(dve.tensor_tensor_reduce(EB[:, v % 2, g, 0:w], R[g][:, 0:w], bias_of(TBS, j + 4 * g, w - 1, w),
                                                1.0, -3e38, ALU.add, ALU.max, st[:, g:g + 1]))
                chain.settle()
                link(dve.tensor_tensor(st[:, 0:2], st[:, 0:2], SNK[:, j:NH:4], ALU.max))
                do(dve.tensor_tensor(st[:, 4:6], SNK[:, j:NH:4], st[:, 0:2], ALU.subtract))
                chain.settle()
                dve.tensor_scalar(st[:, 0:2], st[:, 0:2], -1.0, None, ALU.mult).then_inc(ssw_used, 1)

            def swa_pt(v):
                w = 256 if v // 4 == 0 else 512
                dve.wait_ge(sp_T, v + 1)
                if v >= 2:
                    dve.wait_ge(spv_mm, v - 1)
                dve.tensor_copy(PTB[:, v % 2, 0, 0:w], R[3][:, 0:w]).then_inc(spt_ok, 1)
                st = STATS[:, v % 2, :]
                dve.wait_ge(sp_exp, v + 1)
                if v >= 2:
                    dve.wait_ge(so_ok, v - 1)
                link(dve.tensor_tensor(st[:, 6:8], st[:, 2:4], st[:, 4:6], ALU.add))
                link(dve.reciprocal(st[:, 6:8], st[:, 6:8]))

            def swa_out(v):
                blk, j = divmod(v, 4)
                st = STATS[:, v % 2, :]
                dve.wait_ge(spv_mm, v + 1)
                if j == 0 and blk >= 2:
                    dve.wait_ge(so_T, blk - 1)
                for g in range(2):
                    ins = dve.tensor_scalar(OTS[:, blk % 2, HD * (j + 4 * g):HD * (j + 4 * g) + HD],
                                            R[5][:, 64 * g:64 * g + 64], st[:, 6 + g:7 + g], None, ALU.mult)
                ins.then_inc(so_ok, 1)

            dve.wait_ge(p_T, 32)
            dve.wait_ge(tbs_in, 16)
            for v in range(18):
                if v < 16:
                    swa_scores(v)
                if 1 <= v < 17:
                    swa_pt(v - 1)
                if v >= 2:
                    swa_out(v - 2)
                evacs(PT_SWA + v)

            def split_o(b, m):
                dve.wait_ge(ohi_ok, 4 * b + m + 1)
                dve.tensor_tensor(OLO[:, b, m, :], O[:, b, m, :], OHI[:, b, m, :].bitcast(F32), ALU.subtract)\
                   .then_inc(olo_ok, 1)

            for b in range(3):
                for m in range(4):
                    split_o(b, m)
                if b == 1:
                    evacs(PT_SPLIT)
            dve.wait_ge(olo_ok, 12)
            n = MERGE0
            for d in range(KC):
                gates = GATES[:, 3 * d % 15:3 * d % 15 + 3, :]
                for b in range(3):
                    dve.wait_ge(gsig_ok, 3 * d + b + 1)
                    dve.wait_ge(dense_done, n + 1)
                    if b == 0:
                        if d >= 2:
                            dve.wait_ge(mhi_ok, d - 1)
                        ins = dve.tensor_tensor(MT[:, d % 2, :], DB[group_of(n) % 2][:, :], gates[:, 0, :], ALU.mult)
                    else:
                        ins = dve.tensor_tensor(DSH2[:, b - 1, :], DB[group_of(n) % 2][:, :], gates[:, b, :], ALU.mult)
                    ins.then_inc(dense_evac, 1)
                    dve.wait_ge(dense_evac, group_of(n) + 1)
                    if b:
                        ins = dve.tensor_tensor(MT[:, d % 2, :], MT[:, d % 2, :], DSH2[:, b - 1, :], ALU.add)
                        if b == 1:
                            link(ins)
                        else:
                            ins.then_inc(mt_ok, 1)
                    n += 1
                dve.wait_ge(mhi_ok, d + 1)
                dve.tensor_tensor(MLO[:, d, :], MT[:, d % 2, :], MHI[:, d, :].bitcast(F32), ALU.subtract).then_inc(mlo_ok, 1)
            dve.wait_ge(mlo_ok, KC)
            for d in range(KC):
                if d == 5:
                    for k in range(KC):
                        dve.wait_ge(x1T, k + 1)
                        dve.tensor_copy(X1[:, k, :], R[k % 4][:, :]).then_inc(x1T_ok, 1)
                dve.wait_ge(dense_done, n + 1)
                dve.tensor_copy(OT[:, d, :], DB[group_of(n) % 2][:, :]).then_inc(dense_evac, 1)
                dve.wait_ge(dense_evac, group_of(n) + 1)
                n += 1
                if d == KC - 1:
                    continue
                dve.wait_ge(out_sq, d + 1)
                if d == 0:
                    dve.tensor_copy(SSUM[:, :], SQ[:, 0, :]).then_inc(out_sum, 1)
                else:
                    dve.wait_ge(out_sum, d)
                    dve.tensor_tensor(SSUM[:, :], SSUM[:, :], SQ[:, d % 2, :], ALU.add).then_inc(out_sum, 1)
            assert n == FF0
            dve.wait_ge(norm_std, 2)
            dve.reciprocal(RINV[:, :], SQ[:, 0, :]).then_inc(norm_rinv, 1)
            dve.wait_ge(norm_rinv, 1)
            dve.wait_ge(x1T_ok, KC)

            def scale_o(k):
                dve.scalar_tensor_tensor(out=OT[:, k, :], in0=OT[:, k, :], scalar=par("g_post_mix", k), in1=RINV[:, :],
                                         op0=ALU.mult, op1=ALU.mult).then_inc(o_scaled, 1)

            scale_o(0)
            scale_o(1)
            for k in range(KC):
                if k + 2 < KC:
                    scale_o(k + 2)
                dve.wait_ge(h2hi_ok, k + 1)
                dve.scalar_tensor_tensor(out=HLO[:, k, :], in0=X1[:, k, :], scalar=par("g_pre_ffn", k),
                                         in1=HHI[:, k, :].bitcast(F32), op0=ALU.mult, op1=ALU.subtract).then_inc(h2lo_ok, 1)
            dve.wait_ge(norm_std, 3)
            dve.reciprocal(RINV[:, :], SQ[:, 0, :]).then_inc(norm_rinv, 1)
            dve.wait_ge(norm_rinv, 2)

            with dve.Fori(0, NF // 2) as i:
                for f in range(2):
                    b = 3 * f
                    dve.wait_ge(dense_done, i * 4 + (FF0 + 2 * f + 1))
                    dve.tensor_tensor(FT[:, b, :], DB4[2 * f][:, :], RINV[:, :], ALU.mult).then_inc(ff_gate, 1)
                    dve.wait_ge(ff_sig, i * 2 + (f + 1))
                    dve.wait_ge(ff_gate, i * 2 + (f + 1))
                    dve.tensor_tensor(FT[:, b + 1, :], FT[:, b + 1, :], FT[:, b, :], ALU.mult).then_inc(ff_x, 1)
                    dve.wait_ge(ff_x, i * 4 + (2 * f + 1))
                    dve.tensor_tensor(FT[:, b, :], FT[:, b + 1, :], RINV[:, :], ALU.mult).then_inc(ff_x, 1)
                    dve.wait_ge(ff_x, i * 4 + (2 * f + 2))
                    dve.wait_ge(dense_done, i * 4 + (FF0 + 2 * f + 2))
                    dve.tensor_tensor(FT[:, b + 2, :], FT[:, b, :], DB4[2 * f + 1][:, :], ALU.mult).then_inc(ff_hid, 1)
                    dve.wait_ge(ff_hi, i * 2 + (f + 1))
                    dve.tensor_tensor(DLO[:, bass.ds(i * 2 + f, 1), :], FT[:, b + 2, :],
                                      DHI[:, bass.ds(i * 2 + f, 1), :].bitcast(F32), ALU.subtract).then_inc(ff_lo, 1)
                    dve.wait_ge(ff_lo, i * 2 + (f + 1))
            dve.wait_ge(dense_done, DN0)
            for n in range(1, 8, 2):
                dve.wait_ge(x1T, KC + n + 1)
                dve.tensor_copy(X1TOK[:, n // 2, 512:1024], R[2 + n % 4][:, :]).then_inc(x1T_ok, 1)
            dve.memset(SSUM[:, :], 0.0).then_inc(dn_T, 2)
            dve.wait_ge(dn_T, 2)
            with dve.Fori(0, KC // 2) as i:
                for b in range(2):
                    dve.wait_ge(dn_sq, i * 2 + (b + 1))
                    dve.tensor_tensor(SSUM[:, :], SSUM[:, :], SQ[:, 0, :], ALU.add).then_inc(dn_sum, 1)
                    dve.wait_ge(dn_T, i * 2 + (b + 1))
                    gain = PARC[:, bass.ds(i * 2 + (PAR["g_post_ffn"] + b), 1)]
                    dve.tensor_tensor(OF[:, b, :], DB[b][:, :], gain.broadcast_to([P, T]), ALU.mult).then_inc(dn_gain, 1)
                    dve.wait_ge(dn_sum, i * 2 + (b + 1))
            dve.wait_ge(norm_std, 4)
            link(dve.reciprocal(RTOK, RTOK))
            for n in range(8):
                t, cols = n % 4, slice(512 * (n // 4), 512 * (n // 4) + 512)
                if n % 4 == 0:
                    dve.wait_ge(tok_act, 4 + KC // 2 * (n // 4 + 1))
                    dve.wait_ge(x1T_ok, KC + 4)
                dve.scalar_tensor_tensor(out=OTOK[:, t, cols], in0=OTOK[:, t, cols], scalar=RTOK[:, t:t + 1],
                                         in1=X1TOK[:, t, cols], op0=ALU.mult, op1=ALU.add).then_inc(fin_ok, 1)

        @block.tensor
        def _(pe):
            dense = {"n": 0, "k": 0}

            def rhs(n, k):
                kind, i, part, _ = JOBS[n]
                if kind == "cmp":
                    kv, c = i, 4 * part + k
                    return XHI[:, kv, c, :], XLO[:, kv, c, :]
                if kind == "branch":
                    return OHI[:, i % 3, k, :], OLO[:, i % 3, k, :]
                if kind == "out":
                    return MHI[:, k, :], MLO[:, k, :]
                return HHI[:, k, :], HLO[:, k, :]

            def product(dst, n, k, hi, lo, start, stop):
                s = n % NSPL
                pe.matmul(dst, WHI[:, s, k, :], hi, start=start, stop=False)
                pe.matmul(dst, WHI[:, s, k, :], lo, start=False, stop=False)
                return pe.matmul(dst, WLO[:, s, k, :], hi, start=False, stop=stop)

            def cmp_product(n, k, hi, lo, start, stop):
                dst, cols = R[5][0:2 * NCMP, 0:CH], slice(2 * k, 2 * k + 2)
                whi, wlo = (w[:, n % NSPL, cols, :].rearrange("p k n -> p (k n)") for w in (WHI, WLO))
                pe.matmul(dst, hi, whi, start=start, stop=False)
                pe.matmul(dst, lo, whi, start=False, stop=False)
                return pe.matmul(dst, hi, wlo, start=False, stop=stop)

            def steps(count):
                for _ in range(count):
                    n, k = dense["n"], dense["k"]
                    kind, i, part, chunks = JOBS[n]
                    g = group_of(n)
                    if k == 0:
                        pe.wait_ge(w_lo, n + 1)
                        if g >= 2 and kind != "cmp":
                            pe.wait_ge(dense_evac, g - 1)
                        if kind == "cmp":
                            pe.wait_ge(xsplit_ok, i + 1)
                            if i == 1 and part == 0:
                                pe.wait_ge(cmp_read, 1)
                        if kind == "branch":
                            pe.wait_ge(olo_ok, 4 * (i % 3) + 4)
                    if n == 0:
                        pe.wait_ge(xlo_ok, k + 1)
                    if n == OUT0:
                        pe.wait_ge(mlo_ok, k + 1)
                    hi, lo = rhs(n, k)
                    if kind == "cmp":
                        last = cmp_product(n, k, hi, lo, part == 0 and k == 0, part == 3 and k == 3)
                    else:
                        last = product(DB[g % 2][:, :], n, k, hi, lo, k == 0, k == chunks - 1)
                    dense["k"] += 1
                    if k == chunks - 1:
                        last.then_inc(dense_done, 1)
                        dense["n"], dense["k"] = n + 1, 0

            def fill(point):
                steps(FILL[point])

            def tr(dst, src, n=P):
                return pe.transpose(dst, src, ident[0:n, 0:n])

            pe.wait_ge(con_in, 16)
            pe.wait_ge(par_in, 32)
            tr(R[4][:, 0:NPAR1], PRAW[0:NPAR1, 0, :], NPAR1)
            tr(R[5][:, 0:NPAR2], PRAW[0:NPAR2, 1, :], NPAR2).then_inc(prow_T, 1)
            pe.wait_ge(x_in, 16)
            for k in range(KC):
                if k == 4:
                    pe.wait_ge(xtok_in, 16)
                if k >= 4:
                    pe.wait_ge(xlo_ok, k - 3)
                    pe.wait_ge(xsq_ok, k - 3)
                for t in range(4):
                    last = tr(R[k % 4][:, t * P:(t + 1) * P], XTOK0[:, t, k * P:(k + 1) * P])
                last.then_inc(xT_done, 1)
            steps(8)
            pe.wait_ge(xsum_ok, KC)
            pe.wait_ge(prow_ok, 2)
            pe.matmul(R[4][:, :], ones, SSUM[:, :], start=True, stop=True).then_inc(norm_ss, 1)
            steps(8)
            pe.wait_ge(hot_in, 48)
            pe.wait_ge(rel_in, 16)
            pe.matmul(R[0][0:8, :], TBL[:, 0:8], HOT[:, 0:512], start=True, stop=True)
            pe.matmul(R[1][0:8, 0:128], TBL[:, 0:8], HOT[:, 512:640], start=True, stop=True)
            pe.matmul(R[2][0:8, 0:384], TBL[:, 8:16], HOT[:, 640:1024], start=True, stop=True).then_inc(rel_mm, 1)
            steps(8 * 9)
            for m in range(4):
                pe.wait_ge(kk_sq, m + 1)
                last = pe.matmul(R[5][0:NH, :], mask("sel", 32)[:, NH * m:NH * m + NH], TMP[:, m, :], start=m == 0, stop=m == 3)
            last.then_inc(kk_ss, 1)
            steps(8 * (NS0 - 11))
            pe.wait_ge(kk_rinv, 1)
            pe.wait_ge(selt_in, 16)
            for m in range(4):
                last = pe.matmul(R[m][:, :], SELT[0][:, m, :], SSUM[0:NH, :], start=True, stop=True)
            last.then_inc(kk_bc, 1)
            pe.wait_ge(wsmall_in, 32)
            pe.wait_ge(tanh_ok, 1)
            pe.wait_ge(kk_ok, 4)
            for m in range(4):
                if m == 3:
                    pe.wait_ge(sig_ok, 2)
                pe.matmul(R[(2 * m) % 6][:, :], WA[0:64, m * P:(m + 1) * P], RW[0:64, 12, :], start=True, stop=True)
                pe.matmul(R[(2 * m + 1) % 6][:, :], WA[64:128, m * P:(m + 1) * P], RW[64:128, 12, :],
                          start=True, stop=True).then_inc(zmm_done, 1)
                fill(PT_UP + m)
            pe.wait_ge(sig_ok, 8)
            fill(PT_UP + 4)

            def values_T(cp):
                flat = RW[:, :, :].rearrange("p a t -> p (a t)")
                for c in range(2):
                    for m in range(4):
                        at0 = (8 + m) * T + cp * P + c * C - C
                        last = tr(R[c][:, m * P:(m + 1) * P], flat[:, at0:at0 + P])
                last.then_inc(vt_T, 1)

            pe.wait_ge(st_ok, 1)
            values_T(0)
            for cp in range(4):
                pt = PT_CP[cp]
                fill(pt)
                pe.wait_ge(arbk_ok, cp + 1)
                if cp:
                    pe.wait_ge(y_ok, 4 * cp)
                    pe.wait_ge(st_ok, 2 * cp + 1)
                for c in range(2):
                    for h in range(NH):
                        q, m = h % 2, h // 2
                        p = slice(64 * q, 64 * q + 64)
                        last = pe.matmul(R[2 + 2 * c + q][:, m * P:(m + 1) * P], BK[p, m, c, :], AR[p, m, c, :],
                                         start=True, stop=True)
                last.then_inc(ag_mm, 1)
                fill(pt + 1)
                pe.wait_ge(x2t_ok, cp + 1)
                pe.wait_ge(vt_ok, 2 * cp + 2)
                for h in range(NH):
                    for c in range(2):
                        p = slice(64 * c, 64 * c + 64)
                        last = pe.transpose(R[c][0:64, h * C:(h + 1) * C], XTBD[p, h, p], ident[p, p])
                last.then_inc(x2_mm, 1)
                fill(pt + 2)
                for lv in range(5):
                    g = 5 * cp + lv
                    pe.wait_ge(am_ok, g + 1)
                    if lv == 0:
                        pe.wait_ge(x2_ok, cp + 1)
                    else:
                        pe.wait_ge(xt_ok, g)
                    for h in range(NH):
                        last = pe.matmul(R[1][:, h * C:(h + 1) * C], AM[:, h, :], XC[:, h, :], start=True, stop=True)
                    last.then_inc(u_mm, 1)
                    fill(pt + 3 + 2 * lv)
                    if lv == 0:
                        pe.wait_ge(bkend_ok, cp + 1)
                        pe.wait_ge(ag_ok, cp + 1)
                        for c in range(2):
                            for m in range(4):
                                last = tr(R[4 + c][:, m * P:(m + 1) * P], BK[:, m, c, :])
                        last.then_inc(bkt_T, 1)
                    pe.wait_ge(uc_ok, g + 1)
                    if lv < 4:
                        if lv:
                            pe.wait_ge(xtbd_ok, 6 * cp + 2 * lv)
                        for h in range(NH):
                            last = pe.matmul(R[2][:, h * C:(h + 1) * C], XTBD[:, h, :], UC[:, h, :], start=True, stop=True)
                    else:
                        pe.wait_ge(ubd_ok, 2 * cp + 2)
                        pe.wait_ge(xtc_ok, cp + 1)
                        for h in range(NH):
                            last = pe.matmul(R[3][:, h * C:(h + 1) * C], UBD[:, h, :], XTC[:, h, :], start=True, stop=True)
                    last.then_inc(xa_mm, 1)
                    fill(pt + 4 + 2 * lv)
                    if lv < 4:
                        pe.wait_ge(xt_ok, g + 1)
                        pe.wait_ge(bkt_ok, 2 * cp + 2)
                        for h in range(NH):
                            for c in range(2):
                                p = slice(64 * c, 64 * c + 64)
                                last = pe.transpose(R[3 + c][0:64, h * C:(h + 1) * C], XC[p, h, :], ident[p, p])
                        last.then_inc(xtr_T, 1)
                pe.wait_ge(xt_ok, 5 * cp + 5)
                pe.wait_ge(bkt_ok, 2 * cp + 2)
                pe.wait_ge(svz_ok, cp + 1)
                for c in range(2):
                    g = 2 * cp + c
                    pe.wait_ge(st_ok, g + 1)
                    tp = slice(64 * c, 64 * c + 64)
                    for h in range(NH):
                        q, m = h % 2, h // 2
                        p = slice(64 * q, 64 * q + 64)
                        dst = R[q][tp, m * C:(m + 1) * C]
                        pe.matmul(dst, G[:, c, 4 * q + m, 0:C], SV[:, c, h * HD:(h + 1) * HD], start=True, stop=False)
                        last = pe.matmul(dst, AR[p, m, c, 0:C], ST[p, g % 2, m, :], start=False, stop=True)
                    last.then_inc(t1_mm, 1)
                    fill(pt + 13 + 2 * c)
                    pe.wait_ge(t1_dve, g + 1)
                    pe.wait_ge(t1_act, g + 1)
                    if g:
                        pe.wait_ge(y_ok, 2 * g)
                    for h in range(NH):
                        q, m = h % 2, h // 2
                        last = pe.matmul(R[2 if h < 4 else 5][0:64, (h % 4) * HD:(h % 4 + 1) * HD], XTC[tp, 4 * q + m, :], T1[tp, 4 * q + m, :],
                                         start=True, stop=True)
                    last.then_inc(sa_mm, 1)
                    if c == 1 and cp < 3:
                        values_T(cp + 1)
                    fill(pt + 14 + 2 * c)
                    pe.wait_ge(sa_dve, g + 1)
                    pe.wait_ge(sa_act, g + 1)
                    for h in range(NH):
                        q, m = h % 2, h // 2
                        pe.matmul(R[5][64 * q:64 * q + 64, m * C:(m + 1) * C], BKT[:, c, m, 64 * q:64 * q + 64],
                                  SV[:, c, h * HD:(h + 1) * HD], start=True, stop=True)
                    for h in range(NH):
                        q, m = h % 2, h // 2
                        p = slice(64 * q, 64 * q + 64)
                        dst = R[3 + q][p, m * C:(m + 1) * C]
                        pe.matmul(dst, SV[:, c, h * HD:(h + 1) * HD], G[:, c, 4 * q + m, C:P], start=True, stop=False)
                        last = pe.matmul(dst, ST[p, g % 2, m, :], AR[p, m, c, C:P], start=False, stop=True)
                    last.then_inc(ys_mm, 1)
                fill(pt + 17)

            fill(PT_GN)
            pe.wait_ge(y_ok, 16)
            pe.wait_ge(st_ok, 9)
            for m in range(4):
                pe.matmul(R[m][:, :], bones, KK[:, m, :], start=True, stop=True).then_inc(gn_mean, 1)

            def gn_bonus(m):
                pe.wait_ge(gn_bp, m + 1)
                if m:
                    pe.wait_ge(gn_b, m)
                pe.matmul(R[4][:, :], bones, CUM[:, m, :], start=True, stop=True).then_inc(gn_bmm, 1)

            gn_bonus(0)
            fill(PT_GN + 1)
            gn_bonus(1)
            fill(PT_GN + 2)
            for m in range(4):
                pe.wait_ge(gn_sq, m + 1)
                last = pe.matmul(R[0][0:NH, :], mask("sel", 32)[:, NH * m:NH * m + NH], KK[:, m, :], start=m == 0, stop=m == 3)
            last.then_inc(gn_var, 1)
            gn_bonus(2)
            fill(PT_GN + 3)
            gn_bonus(3)
            pe.wait_ge(gn_rinv, 1)
            pe.wait_ge(selt_in, 32)
            for m in range(4):
                pe.matmul(R[m][:, :], SELT[1][:, m, :], SSUM[0:NH, :], start=True, stop=True).then_inc(gn_bc, 1)
            pe.wait_ge(g2_in, 16)
            for m in range(4):
                pe.wait_ge(gn_n, m + 1)
                pe.matmul(R[m][:, :], WA[:, m * P:(m + 1) * P], RW[:, 13, :], start=True, stop=True).then_inc(gn_bc, 1)
            fill(PT_GN + 4)
            fill(PT_GN + 5)
            pe.wait_ge(gn_ok, 4)
            pe.wait_ge(gl_ok, 1)
            for t in range(4):
                last = pe.transpose(R[0][:, 24 * t:24 * t + 24], GL[0:24, t * P:(t + 1) * P], ident[0:24, 0:24])
            last.then_inc(gl_T, 1)
            for b in range(2):
                for t in range(4):
                    last = tr(R[2 + b][:, t * P:(t + 1) * P], NQ[:, 7 + 2 * b, t * P:(t + 1) * P])
            last.then_inc(vtok_T, 1)
            pe.wait_ge(cw2_in, 32)
            pe.wait_ge(hg_ok, 2)
            for i in range(4):
                last = tr(R[1][:, 64 * i:64 * i + 2 * NCMP], HG[:, i // 2, P * (i % 2):P * (i % 2) + P], 2 * NCMP)
            last.then_inc(kv_mm, 1)
            pe.wait_ge(hg_ok, 3)
            for g in range(2):
                for half in range(2):
                    pe.matmul(R[1][64 * g:64 * g + 64, 0:NCMP], CW2[:, 0, half, :], HGT[:, half, g * NCMP:(g + 1) * NCMP],
                              start=half == 0, stop=half == 1)
                for half in range(2):
                    last = pe.matmul(R[1][0:NCMP, 128 + 64 * g:192 + 64 * g], HGT[:, 2 + half, g * NCMP:(g + 1) * NCMP],
                                     CW2[:, 1, half, :], start=half == 0, stop=half == 1)
            last.then_inc(kv_mm, 1)
            pe.wait_ge(kv_ok, 1)
            pe.wait_ge(vtok_ok, 2)
            pe.wait_ge(glt_ok, 1)

            def nsa_qk(u):
                i, h = divmod(u, NH)
                j, g = h % 4, h // 4
                p, w = slice(64 * g, 64 * g + 64), P * (i + 1)
                q = NQ[p, j, i * P:(i + 1) * P]
                if u:
                    pe.wait_ge(s_used, u)
                if u >= 2:
                    pe.wait_ge(pts_ok, u - 1)
                pe.matmul(R[2][:, 0:8 * i + 7], q, KCT[p, 0:8 * i + 7], start=True, stop=True)
                pe.matmul(R[0][:, 0:w], q, NQ[p, 6, 0:w], start=True, stop=True)
                pe.matmul(R[1][:, 0:w], q, NQ[p, 8, 0:w], start=True, stop=True).then_inc(qk_mm, 1)

            def nsa_pT(u):
                i = u // NH
                nc_ = 8 * i + 7
                pe.wait_ge(p_exp, u + 1)
                if u:
                    pe.wait_ge(pts_ok, u)
                    pe.wait_ge(ptw_ok, u)
                if u >= NH + 2:
                    pe.wait_ge(oT_ok, (u - 2) // NH)
                for b in range(2):
                    for k in range(i + 1):
                        tr(R[3 + b][:, k * P:(k + 1) * P], EB[:, u % 2, b, k * P:(k + 1) * P])
                pe.wait_ge(sc_used, min(u + 2, 32))
                tr(R[2][0:nc_, 384:512], ECB[:, u % 2, 0:nc_]).then_inc(p_T, 1)

            def nsa_pv(u):
                i, h = divmod(u, NH)
                g, nc_ = h // 4, 8 * (u // NH) + 7
                pe.wait_ge(pts_ok, u + 1)
                pe.wait_ge(ptw_ok, u + 1)
                if u:
                    pe.wait_ge(o_ok, u)
                pe.matmul(R[5][:, 0:64], PTC[0:nc_, u % 2, :], VCT[0:nc_, g, :], start=True, stop=True)
                for b in range(2):
                    for k in range(i + 1):
                        last = pe.matmul(R[5][:, 64 + 64 * b:128 + 64 * b], PTB[:, u % 2, b, k * P:(k + 1) * P],
                                         VT[:, b, k, 64 * g:64 * g + 64], start=k == 0, stop=k == i)
                last.then_inc(pv_mm, 1)

            def nsa_oT(i, u):
                pe.wait_ge(o_ok, 8 * (i + 1))
                pe.wait_ge(pts_ok, min(u, 32))
                for m in range(4):
                    last = tr(R[3][:, m * P:(m + 1) * P], OTK[:, i % 2, m * P:(m + 1) * P])
                last.then_inc(o_T, 1)

            for u in range(34):
                if u < 32:
                    nsa_qk(u)
                if 1 <= u < 33:
                    nsa_pT(u - 1)
                if u >= 2:
                    nsa_pv(u - 2)
                if u >= 3 and (u - 3) % NH == NH - 1:
                    nsa_oT((u - 3) // NH, u)
                fill(PT_NSA + u)
            nsa_oT(3, 34)

            pe.wait_ge(s_used, 32)
            pe.wait_ge(swq_in, 16)
            for t in range(4):
                last = tr(R[2][:, t * P:(t + 1) * P], SWQ[:, 5, t * P:(t + 1) * P])
            last.then_inc(vtok_T, 1)
            pe.wait_ge(vtok_ok, 3)
            pe.wait_ge(oT_ok, 4)

            def swa_qk(v):
                blk, j = divmod(v, 4)
                w = WIN if blk == 0 else 2 * WIN
                if v:
                    pe.wait_ge(ssw_used, v)
                for g in range(2):
                    p = slice(64 * g, 64 * g + 64)
                    last = pe.matmul(R[g][:, 0:w], SWQ[p, j, blk * WIN:(blk + 1) * WIN],
                                     SWQ[p, 4, (blk + 1) * WIN - w:(blk + 1) * WIN], start=True, stop=True)
                last.then_inc(sq_mm, 1)

            def swa_pT(v):
                n = 1 if v // 4 == 0 else 2
                pe.wait_ge(sp_exp, v + 1)
                if v:
                    pe.wait_ge(spt_ok, v)
                for g in range(2):
                    for k in range(n):
                        at0 = (g * n + k) * P
                        last = tr(R[3][:, at0:at0 + P], EB[:, v % 2, g, k * P:(k + 1) * P])
                last.then_inc(sp_T, 1)

            def swa_pv(v):
                blk = v // 4
                n = 1 if blk == 0 else 2
                pe.wait_ge(spt_ok, v + 1)
                if v:
                    pe.wait_ge(so_ok, v)
                else:
                    pe.wait_ge(o_ok, 32)
                for g in range(2):
                    for k in range(n):
                        last = pe.matmul(R[5][:, 64 * g:64 * g + 64], PTB[:, v % 2, 0, (g * n + k) * P:(g * n + k + 1) * P],
                                         VT[:, 2, blk + 1 - n + k, 64 * g:64 * g + 64], start=k == 0, stop=k == n - 1)
                last.then_inc(spv_mm, 1)

            def swa_oT(blk):
                pe.wait_ge(so_ok, 4 * (blk + 1))
                if blk:
                    pe.wait_ge(soT_ok, blk)
                for m in range(4):
                    last = tr(R[2][:, m * P:(m + 1) * P], OTS[:, blk % 2, m * P:(m + 1) * P])
                last.then_inc(so_T, 1)

            for v in range(18):
                if v < 16:
                    swa_qk(v)
                if 1 <= v < 17:
                    swa_pT(v - 1)
                if v >= 2:
                    swa_pv(v - 2)
                if v >= 3 and (v - 3) % 4 == 3:
                    swa_oT((v - 3) // 4)
                fill(PT_SWA + v)
            swa_oT(3)
            fill(PT_SPLIT)

            assert dense["n"] == MERGE0
            steps(sum(j[3] for j in JOBS[MERGE0:OUT0]))
            steps(8 * 5)
            pe.wait_ge(xtok_in, 32)
            for k in range(KC):
                if k >= 4:
                    pe.wait_ge(x1T_ok, k - 3)
                for t in range(4):
                    last = tr(R[k % 4][:, t * P:(t + 1) * P], XTOK[:, t, k * P:(k + 1) * P])
                last.then_inc(x1T, 1)
            steps(8 * (KC - 5))
            pe.wait_ge(out_sum, KC - 1)
            pe.matmul(R[4][:, :], ones, SSUM[:, :], start=True, stop=False)
            pe.wait_ge(out_sq, KC)
            pe.matmul(R[4][:, :], ones, SQ[:, (KC - 1) % 2, :], start=False, stop=True).then_inc(norm_ss, 1)

            def ffn_tile(i, f, u):
                n = FF0 + 2 * f + u
                pe.wait_ge(w_lo, i * 4 + (n + 1))
                for k in range(8):
                    last = product(DB4[2 * f + u][:, :], n, k, HHI[:, k, :], HLO[:, k, :], k == 0, k == 7)
                last.then_inc(dense_done, 1)

            pe.wait_ge(x1T_ok, KC)
            pe.wait_ge(dense_evac, group_of(FF0 - 1) + 1)
            pe.wait_ge(w_lo, FF0 + 1)
            for k in range(KC):
                pe.wait_ge(h2lo_ok, k + 1)
                last = product(DB4[0][:, :], FF0, k, HHI[:, k, :], HLO[:, k, :], k == 0, k == 7)
                if k == 7:
                    last.then_inc(dense_done, 1)
                pe.wait_ge(x1_sq, k + 1)
                last = pe.matmul(R[4][:, :], ones, SQ[:, k % 2, :], start=k == 0, stop=k == 7)
                last.then_inc(x1_ss if k < 7 else norm_ss, 1)
            ffn_tile(0, 0, 1)
            ffn_tile(0, 1, 0)
            ffn_tile(0, 1, 1)
            with pe.Fori(1, NF // 2) as i:
                for f in range(2):
                    pe.wait_ge(ff_hid, i * 2 + (f - 1))
                    ffn_tile(i, f, 0)
                    ffn_tile(i, f, 1)
            for n in range(8):
                if n >= 4:
                    if n % 2 == 0:
                        pe.wait_ge(tok_act, (n - 4) // 2 + 1)
                    else:
                        pe.wait_ge(x1T_ok, KC + (n - 4) // 2 + 1)
                for m in range(4):
                    last = tr(R[2 + n % 4][:, m * P:(m + 1) * P],
                              X1[:, 4 * (n % 2) + m, (n // 2) * P:(n // 2 + 1) * P])
                last.then_inc(x1T, 1)
            pe.wait_ge(ff_lo, NF - 1)

            def output_T(b, gained, copied):
                pe.wait_ge(dn_gain, gained)
                pe.wait_ge(tok_act, copied)
                for t in range(4):
                    last = tr(R[2 + b][:, t * P:(t + 1) * P], OF[:, b, t * P:(t + 1) * P])
                last.then_inc(dn_T, 1)

            def down_tile(i, b):
                first = isinstance(i, int)
                k0 = 0
                for q in range(4):
                    n = DN0 + 4 * b + q
                    pe.wait_ge(w_lo, i * 8 + (n + 1))
                    if q == 3 and first and b == 0:
                        pe.wait_ge(ff_lo, NF)
                    if q == 0 and not first:
                        pe.wait_ge(dn_gain, i * 2 + (b - 1))
                    for k in range(DPARTS[q]):
                        last = product(DB[b][:, :], n, k, DHI[:, k0 + k, :], DLO[:, k0 + k, :],
                                       k0 + k == 0, k0 + k == NF - 1)
                    last.then_inc(dense_done, 1)
                    k0 += DPARTS[q]
                    if q == 2 and not (first and b == 0):
                        output_T(1 - b, i * 2 + b, 4 if first else i * 2 + (b + 2))

            down_tile(0, 0)
            pe.wait_ge(x1T_ok, KC + 4)
            down_tile(0, 1)
            with pe.Fori(1, KC // 2) as i:
                for b in range(2):
                    down_tile(i, b)
            pe.wait_ge(dn_sum, KC)
            for t in range(4):
                last = pe.matmul(R[0][:, t:t + 1], SSUM[:, t * P:(t + 1) * P], ones[:, 0:1], start=True, stop=True)
            last.then_inc(norm_ss, 1)
            output_T(1, KC, 4 + KC - 2)


def kernel(**inputs):
    import concourse.bacc as bacc
    from concourse.bass_utils import run_bass_kernel_spmd

    a = {name: np.asarray(value) for name, value in inputs.items()}
    one = lambda name: a[name][0]
    rows = [one(name).reshape(-1, P) for name in (
        "norm_pre_mix", "norm_post_mix", "norm_pre_ffn", "norm_post_ffn", "rwkv_mu", "rwkv_w0", "rwkv_a0", "rwkv_k_k",
        "rwkv_k_a", "rwkv_r_k", "rwkv_ln_w", "rwkv_ln_b")]
    pe_rows = [np.concatenate([one(name), one(name)], axis=1) for name in ("nsa_pe_k", "nsa_pe_v")]
    con, hot = constants()
    arrays = {
        "x": a["x"][0], "w_in": one("w_in"), "w_branch": one("w_branch"), "w_out": one("w_out"),
        "w_gate": one("ffn_w_gate"), "w_up": one("ffn_w_up"), "w_down": one("ffn_w_down"),
        "w2": one("rwkv_w2"), "a2": one("rwkv_a2"), "g2": one("rwkv_g2"),
        "ck1": one("nsa_ck_w1"), "ck2": one("nsa_ck_w2"), "cv1": one("nsa_cv_w1"), "cv2": one("nsa_cv_w2"),
        "sinks": one("swa_sinks"), "rel_bias": a["rel_bias"],
        "par1": np.concatenate(rows, axis=0), "par2": np.concatenate(pe_rows, axis=0), "con": con, "hot": hot,
    }
    arrays = {f"in_{name}": np.ascontiguousarray(value) for name, value in arrays.items()}
    nc = bacc.Bacc("TRN2", target_bir_lowering=False, num_devices=1)
    args = [nc.dram_tensor(name, value.shape, F32, kind="ExternalInput").ap() for name, value in arrays.items()]
    out = nc.dram_tensor("out_0", (T, D), F32, kind="ExternalOutput").ap()
    build(nc, *args, out)
    r = run_bass_kernel_spmd(nc, [arrays], core_ids=[0])
    return r.results[0]["out_0"].reshape(1, T, D)
```
